# Optimizing a Trainium2 kernel written in Bass

```python
import math
import jax, jax.numpy as jnp
from jax import lax
import numpy as np

D_MODEL = 1024
BATCH = 1
SEQ = 1024
DEPTH = 1
DEC_BATCH = 8
DEC_SEQ = 1
PAST_LEN = 8192
PAGE_SIZE = 128

D_MIX = D_MODEL
D_CONV = D_MIX // 2
D_RET = D_MIX - D_CONV
RET_HEADS = 4
RET_HD = D_RET // RET_HEADS
CONV_WIDTH = 31
CONV_BUF = CONV_WIDTH - 1
RET_CHUNK = 128
ROPE_BASE = 10000.0
N_EXPERTS = 64
TOP_K = 6
N_GROUPS = 8
TOPK_GROUPS = 4
D_EXPERT = D_MODEL // 4
D_SHARED = D_EXPERT
ROUTED_SCALE = 2.5
MOE_BLOCK = 128
EPS = 1e-6
D_IN = 2 * D_CONV + 4 * D_RET

kernel_name = 'hybrid_conv_retention_moe_step'

F32 = jnp.float32

def rmsnorm(x, g):
    xf = x.astype(F32)
    y = xf * lax.rsqrt(jnp.mean(xf * xf, axis=-1, keepdims=True) + EPS)
    return (y * g.astype(F32)).astype(x.dtype)

def layernorm(x, g, b):
    xf = x.astype(F32)
    mu = jnp.mean(xf, axis=-1, keepdims=True)
    var = jnp.mean(jnp.square(xf - mu), axis=-1, keepdims=True)
    return ((xf - mu) * lax.rsqrt(var + EPS) * g.astype(F32) + b.astype(F32)).astype(x.dtype)

def rotary(x, pos):
    half = x.shape[-1] // 2
    inv = ROPE_BASE ** (-jnp.arange(half, dtype=F32) / half)
    ang = pos[:, None] * inv[None, :]
    cos = jnp.cos(ang)[None, :, None, :]
    sin = jnp.sin(ang)[None, :, None, :]
    xf = x.astype(F32)
    x1, x2 = xf[..., :half], xf[..., half:]
    return jnp.concatenate([x1 * cos - x2 * sin, x1 * sin + x2 * cos], axis=-1)

def retention(q, k, v, s0):
    B, L, H, D = q.shape
    C = math.gcd(L, RET_CHUNK)
    n = L // C
    log_g = jnp.log(1.0 - 2.0 ** (-5.0 - jnp.arange(H, dtype=F32)))
    idx = jnp.arange(C, dtype=F32)
    rel = idx[:, None] - idx[None, :]
    mask = jnp.where(rel >= 0, jnp.exp(log_g[:, None, None] * jnp.maximum(rel, 0.0)), 0.0)
    q_decay = jnp.exp(log_g[None, :] * (idx[:, None] + 1.0))
    k_decay = jnp.exp(log_g[None, :] * (C - 1.0 - idx[:, None]))
    chunk_decay = jnp.exp(log_g * C)

    def split(t):
        return t.reshape(B, n, C, H, D).swapaxes(0, 1)

    def step(s, qkv):
        qc, kc, vc = qkv
        scores = jnp.einsum('bchd,bshd->bhcs', qc, kc) * mask[None]
        inner = jnp.einsum('bhcs,bshe->bche', scores, vc)
        cross = jnp.einsum('bchd,bhde->bche', qc * q_decay[None, :, :, None], s)
        s_new = chunk_decay[None, :, None, None] * s + jnp.einsum(
            'bshd,bshe->bhde', kc * k_decay[None, :, :, None], vc)
        return s_new, inner + cross

    s_fin, out = lax.scan(step, s0, (split(q), split(k), split(v)))
    return out.swapaxes(0, 1).reshape(B, L, H, D), s_fin

def mixer(h, conv_buf, ret_s, pos0, w_in, conv_w, conv_b, conv_norm_g, conv_norm_b,
          ret_norm_g, ret_norm_b, w_out):
    B, L, _ = h.shape
    u = h @ w_in
    a, b, q, k, v, g = jnp.split(
        u, [D_CONV, 2 * D_CONV, 2 * D_CONV + D_RET, 2 * D_CONV + 2 * D_RET, 2 * D_CONV + 3 * D_RET], axis=-1)
    glu = a * jax.nn.sigmoid(b)
    xpad = jnp.concatenate([conv_buf.astype(glu.dtype), glu], axis=1)
    conv = lax.conv_general_dilated(
        xpad, conv_w[:, None, :].astype(glu.dtype), window_strides=(1,), padding='VALID',
        dimension_numbers=('NWC', 'WIO', 'NWC'), feature_group_count=D_CONV) + conv_b.astype(glu.dtype)
    new_conv_buf = xpad[:, -CONV_BUF:]
    conv_out = jax.nn.silu(layernorm(conv, conv_norm_g, conv_norm_b))
    pos = jnp.arange(L, dtype=F32) + pos0
    qh = rotary(q.reshape(B, L, RET_HEADS, RET_HD), pos) * (RET_HD ** -0.5)
    kh = rotary(k.reshape(B, L, RET_HEADS, RET_HD), pos)
    vh = v.reshape(B, L, RET_HEADS, RET_HD).astype(F32)
    o, s_new = retention(qh, kh, vh, ret_s.astype(F32))
    mu = jnp.mean(o, axis=-1, keepdims=True)
    var = jnp.mean(jnp.square(o - mu), axis=-1, keepdims=True)
    o = ((o - mu) * lax.rsqrt(var + EPS)).reshape(B, L, D_RET)
    o = o * ret_norm_g.astype(F32) + ret_norm_b.astype(F32)
    ret_out = o.astype(h.dtype) * jax.nn.silu(g)
    y = jnp.concatenate([conv_out, ret_out], axis=-1) @ w_out
    return y, new_conv_buf, s_new.astype(ret_s.dtype)

def moe(h, w_router, router_bias, w1, w3, w2, ws1, ws3, ws2):
    B, L, Dm = h.shape
    T = B * L
    t = h.reshape(T, Dm)
    scores = jax.nn.sigmoid((t @ w_router).astype(F32))
    sel = scores + router_bias.astype(F32)
    per = N_EXPERTS // N_GROUPS
    grp_score = lax.top_k(sel.reshape(T, N_GROUPS, per), 2)[0].sum(-1)
    _, gidx = lax.top_k(grp_score, TOPK_GROUPS)
    keep = jnp.zeros((T, N_GROUPS), bool).at[jnp.arange(T)[:, None], gidx].set(True)
    sel = jnp.where(jnp.repeat(keep, per, axis=1), sel, -jnp.inf)
    _, eidx = lax.top_k(sel, TOP_K)
    wts = jnp.take_along_axis(scores, eidx, axis=1)
    wts = wts / jnp.sum(wts, axis=-1, keepdims=True) * ROUTED_SCALE
    A = T * TOP_K
    flat_e = eidx.reshape(A)
    order = jnp.argsort(flat_e)
    se = flat_e[order]
    stok = (order // TOP_K).astype(jnp.int32)
    sw = wts.reshape(A)[order]
    counts = jnp.bincount(flat_e, length=N_EXPERTS)
    padded = (counts + MOE_BLOCK - 1) // MOE_BLOCK * MOE_BLOCK
    pend = jnp.cumsum(padded)
    pstart = pend - padded
    start = jnp.cumsum(counts) - counts
    dest = pstart[se] + jnp.arange(A) - start[se]
    n_blocks = -(-(A + N_EXPERTS * (MOE_BLOCK - 1)) // MOE_BLOCK)
    cap = n_blocks * MOE_BLOCK
    tok_buf = jnp.zeros((cap,), jnp.int32).at[dest].set(stok)
    w_buf = jnp.zeros((cap,), F32).at[dest].set(sw)
    blk_e = jnp.minimum(jnp.searchsorted(pend, jnp.arange(n_blocks) * MOE_BLOCK, side='right'),
                        N_EXPERTS - 1)
    xb = t[tok_buf].reshape(n_blocks, MOE_BLOCK, Dm)

    def run_block(args):
        xblk, e = args
        hid = jax.nn.silu(xblk @ w1[e]) * (xblk @ w3[e])
        return hid @ w2[e]

    yb = lax.map(run_block, (xb, blk_e))
    routed = jnp.zeros((T, Dm), F32).at[tok_buf].add(yb.reshape(cap, Dm).astype(F32) * w_buf[:, None])
    shared = (jax.nn.silu(t @ ws1) * (t @ ws3)) @ ws2
    return (routed + shared.astype(F32)).astype(h.dtype).reshape(B, L, Dm)

def layer(x, c, conv_buf, ret_s, pos0, w_ada, b_ada, g_mix, g_ffn, w_in, conv_w, conv_b,
          conv_norm_g, conv_norm_b, ret_norm_g, ret_norm_b, w_out, w_router, router_bias,
          w1, w3, w2, ws1, ws3, ws2):
    mod = (jax.nn.silu(c) @ w_ada + b_ada)[:, None, :]
    sh_m, sc_m, gt_m, sh_f, sc_f, gt_f = jnp.split(mod, 6, axis=-1)
    h = rmsnorm(x, g_mix) * (1 + sc_m) + sh_m
    y, new_buf, new_s = mixer(h, conv_buf, ret_s, pos0, w_in, conv_w, conv_b, conv_norm_g,
                              conv_norm_b, ret_norm_g, ret_norm_b, w_out)
    x = x + gt_m * y
    h = rmsnorm(x, g_ffn) * (1 + sc_f) + sh_f
    x = x + gt_f * moe(h, w_router, router_bias, w1, w3, w2, ws1, ws3, ws2)
    return x, new_buf, new_s

def setup_inputs(seed: int = 0) -> dict:
    key = jax.random.key(seed)
    ks = jax.random.split(key, 32)
    nrm = jax.random.normal
    D = D_MODEL
    return {
        'x_prompt': nrm(ks[0], (BATCH, SEQ, D), F32),
        'x_sample': nrm(ks[1], (DEC_BATCH, DEC_SEQ, D), F32),
        'c_prompt': nrm(ks[2], (BATCH, D), F32),
        'c_sample': nrm(ks[3], (DEC_BATCH, D), F32),
        'state_conv': 0.5 * nrm(ks[4], (DEPTH, DEC_BATCH, CONV_BUF, D_CONV), F32),
        'state_ret': 4.0 * nrm(ks[5], (DEPTH, DEC_BATCH, RET_HEADS, RET_HD, RET_HD), F32),
        'w_ada': 0.5 * D ** -0.5 * nrm(ks[6], (DEPTH, D, 6 * D), F32),
        'b_ada': 0.02 * nrm(ks[7], (DEPTH, 6 * D), F32),
        'g_mix': 1.0 + 0.02 * nrm(ks[8], (DEPTH, D), F32),
        'g_ffn': 1.0 + 0.02 * nrm(ks[9], (DEPTH, D), F32),
        'w_in': D ** -0.5 * nrm(ks[10], (DEPTH, D, D_IN), F32),
        'conv_w': CONV_WIDTH ** -0.5 * nrm(ks[11], (DEPTH, CONV_WIDTH, D_CONV), F32),
        'conv_b': 0.02 * nrm(ks[12], (DEPTH, D_CONV), F32),
        'conv_norm_g': 1.0 + 0.02 * nrm(ks[13], (DEPTH, D_CONV), F32),
        'conv_norm_b': 0.02 * nrm(ks[14], (DEPTH, D_CONV), F32),
        'ret_norm_g': 1.0 + 0.02 * nrm(ks[15], (DEPTH, D_RET), F32),
        'ret_norm_b': 0.02 * nrm(ks[16], (DEPTH, D_RET), F32),
        'w_out': D_MIX ** -0.5 * nrm(ks[17], (DEPTH, D_MIX, D), F32),
        'w_router': D ** -0.5 * nrm(ks[18], (DEPTH, D, N_EXPERTS), F32),
        'router_bias': 0.01 * nrm(ks[19], (DEPTH, N_EXPERTS), F32),
        'w1': D ** -0.5 * nrm(ks[20], (DEPTH, N_EXPERTS, D, D_EXPERT), F32),
        'w3': D ** -0.5 * nrm(ks[21], (DEPTH, N_EXPERTS, D, D_EXPERT), F32),
        'w2': D_EXPERT ** -0.5 * nrm(ks[22], (DEPTH, N_EXPERTS, D_EXPERT, D), F32),
        'ws1': D ** -0.5 * nrm(ks[23], (DEPTH, D, D_SHARED), F32),
        'ws3': D ** -0.5 * nrm(ks[24], (DEPTH, D, D_SHARED), F32),
        'ws2': D_SHARED ** -0.5 * nrm(ks[25], (DEPTH, D_SHARED, D), F32),
        'g_final': 1.0 + 0.02 * nrm(ks[26], (D,), F32),
    }

def reference(x_prompt, x_sample, c_prompt, c_sample, state_conv, state_ret, w_ada, b_ada,
              g_mix, g_ffn, w_in, conv_w, conv_b, conv_norm_g, conv_norm_b, ret_norm_g,
              ret_norm_b, w_out, w_router, router_bias, w1, w3, w2, ws1, ws3, ws2, g_final):
    bp = x_prompt.shape[0]
    xp, xs = x_prompt, x_sample
    conv_p, ret_p, conv_s, ret_s = [], [], [], []
    for l in range(DEPTH):
        params = (w_ada[l], b_ada[l], g_mix[l], g_ffn[l], w_in[l], conv_w[l], conv_b[l],
                  conv_norm_g[l], conv_norm_b[l], ret_norm_g[l], ret_norm_b[l], w_out[l],
                  w_router[l], router_bias[l], w1[l], w3[l], w2[l], ws1[l], ws3[l], ws2[l])
        zero_conv = jnp.zeros((bp, CONV_BUF, D_CONV), x_prompt.dtype)
        zero_ret = jnp.zeros((bp, RET_HEADS, RET_HD, RET_HD), x_prompt.dtype)
        xp, cbp, rsp = layer(xp, c_prompt, zero_conv, zero_ret, 0, *params)
        xs, cbs, rss = layer(xs, c_sample, state_conv[l], state_ret[l], PAST_LEN, *params)
        conv_p.append(cbp)
        ret_p.append(rsp)
        conv_s.append(cbs)
        ret_s.append(rss)
    y_prompt = rmsnorm(xp, g_final)
    y_sample = rmsnorm(xs, g_final)
    return (y_prompt, y_sample, jnp.stack(conv_p), jnp.stack(ret_p), jnp.stack(conv_s), jnp.stack(ret_s))


_drawn_inputs = setup_inputs


def setup_inputs(seed=0):
    import zlib

    import numpy as np

    out = dict(_drawn_inputs(seed))
    spreads = {}
    factors = {'g_mix': 2.864,
     'conv_norm_g': 4.073,
     'conv_norm_b': 6.124,
     'ret_norm_b': 5.031,
     'g_final': 7.669,
     'conv_b': 3.279,
     'ret_norm_g': 2.783}
    for name, (base, spread) in spreads.items():
        noise = np.random.default_rng([zlib.crc32(name.encode()), seed]).standard_normal(out[name].shape)
        drawn = base * np.exp(spread * noise) if base else spread * noise
        out[name] = __import__('jax').numpy.asarray(drawn.astype(out[name].dtype))
    for name, factor in factors.items():
        out[name] = (out[name] * factor).astype(out[name].dtype)
    return out
```

```python
import numpy as np
import concourse.bass as bass
import concourse.mybir as mybir
from concourse.alu_op_type import AluOpType as ALU
from contextlib import ExitStack

P = 128
D = 1024
KT = D // P
SEQ, NS = 1024, 8
TP = SEQ // P
NT = TP + 1
ROWS = NT * P
DC, DR, H, HD = 512, 512, 4, 128
CT = DC // P
CW = 31
PAST = 8192
NE, NG, PER, TOPG, TOPK = 64, 8, 8, 4, 6
DE = 256
FT = DE // P
EPS = 1e-6
BIG = 1e30
TOKENS = SEQ + NS
MAXBLK = -(-(TOKENS * TOPK + NE * (P - 1)) // P)
MINBLK = -(-TOKENS * TOPK // P)
NSLOT = P * P
RING = 4
WE = KT * 2 * DE + FT * D
F32, BF16, I32 = mybir.dt.float32, mybir.dt.bfloat16, mybir.dt.int32
ACT = mybir.ActivationFunctionType
AX = mybir.AxisListType
GA, GB, GQ, GK, GV, GG = range(6)




class Steps:

    def __init__(self, eng, sem):
        self.eng, self.sem, self.base, self.k = eng, sem, 0, 0

    def add(self, ins):
        ins.then_inc(self.sem, 1)
        self.k += 1

    def link(self, ins):
        self.add(ins)
        self.eng.wait_ge(self.sem, self.base + self.k)

    def at(self, base):
        self.base, self.k = base, 0


def build(nc, t, out):
    with ExitStack() as ctx:
        def sb(name, shape, dt=F32):
            return ctx.enter_context(nc.sbuf_tensor(name, shape, dt))

        def sem(name):
            return ctx.enter_context(nc.semaphore(name))

        c_in, bada_in, ident_in, csilu, c_posed, cT_ready, ada_done, mod_ready, mod_stored, consts_in, win_in = (
            sem(n) for n in "c_in bada_in ident_in csilu c_posed cT_ready ada_done mod_ready mod_stored consts_in win_in".split())
        wout_in, modv_in, smod1_in, smod2_in, smod3_in, state_zero, x_in, rope_in, xr_in, norm1_ssq, norm1_std = (
            sem(n) for n in "wout_in modv_in smod1_in smod2_in smod3_in state_zero x_in rope_in xr_in norm1_ssq norm1_std".split())
        h_scaled, h_ready, x_posed, hT_ready, ub_done, ua_done, uq_done, uk_done, uv_done, ug_done, sig_ready = (
            sem(n) for n in "h_scaled h_ready x_posed hT_ready ub_done ua_done uq_done uk_done uv_done ug_done sig_ready".split())
        glu_ready, q_rot, k_rot, v_ready, sg_ready, glu_posed, win_ready, q_posed, qT_ready, k_posed, kT_ready = (
            sem(n) for n in "glu_ready q_rot k_rot v_ready sg_ready glu_posed win_ready q_posed qT_ready k_posed kT_ready".split())
        scores_done, sm_ready, kd_ready, ret_done, S_ready, conv_ready, win_shifted, sum1_done, cen_ready = (
            sem(n) for n in "scores_done sm_ready kd_ready ret_done S_ready conv_ready win_shifted sum1_done cen_ready".split())
        sq_ready, sum2_done, std_c, cnorm_ready, catA_part, gn_var, gn_std, gn_ready, ret_ready, ret_posed = (
            sem(n) for n in "sq_ready sum2_done std_c cnorm_ready catA_part gn_var gn_std gn_ready ret_ready ret_posed".split())
        catB_ready, wout_done, y_gated, x2_ready, norm2_ssq, norm2_std, x2_stored, h2_ready, h2_stored, h2_posed = (
            sem(n) for n in "catB_ready wout_done y_gated x2_ready norm2_ssq norm2_std x2_stored h2_ready h2_stored h2_posed".split())
        h2T_ready, router_done, score_ready, topk_done, cvec_in, cvec_posed, cvec_ready, glu_last_out = (
            sem(n) for n in "h2T_ready router_done score_ready topk_done cvec_in cvec_posed cvec_ready glu_last_out".split())
        newconv_out, newret_out, s0_in, sconv_in, cs_posed, cs_half, s_cross_done, crossT_ready, cross_posed = (
            sem(n) for n in "newconv_out newret_out s0_in sconv_in cs_posed cs_half s_cross_done crossT_ready cross_posed".split())
        sret_ready, vmask_ready, state_mm, state_upd, tri_in, pairs_ready, pos_done, pad_ready, table_filled = (
            sem(n) for n in "sret_ready vmask_ready state_mm state_upd tri_in pairs_ready pos_done pad_ready table_filled".split())
        dest_ready, slots_out, slot_in, slot_posed, slot_ready, blk_ready, blkrow_posed, blkrow_ready, shw_in = (
            sem(n) for n in "dest_ready slots_out slot_in slot_posed slot_ready blk_ready blkrow_posed blkrow_ready shw_in".split())
        xg_in, gathered, xg_posed, xgT_ready, h_done, silu_ready, hid_ready, hid_posed, hidT_ready, y_done, y_evac = (
            sem(n) for n in "xg_in gathered xg_posed xgT_ready h_done silu_ready hid_ready hid_posed hidT_ready y_done y_evac".split())
        ysh_stored, scattered, w_ready, finv_in, x3_ready, fin_ssq, fin_std, dve_step, act_step, pool_step = (
            sem(n) for n in "ysh_stored scattered w_ready finv_in x3_ready fin_ssq fin_std dve_step act_step pool_step".split())
        pool_free = sem("pool_free")
        ada_in = [sem(f"ada_in{r}") for r in range(3)]
        ring_in = [sem(f"ring_in{r}") for r in range(RING)]
        rows_in, fin_ready, fin_stored = ([sem(f"{n}{r}") for r in range(2)] for n in ("rows_in", "fin_ready", "fin_stored"))

        def scratch(name, shape, dt=F32):
            return nc.dram_tensor(name, shape, dt, kind="Internal").ap()

        mod_rows = scratch("mod_rows", (1 + NS, 6 * D))
        x2_rows = scratch("x2_rows", (ROWS, D))
        h2_rows = scratch("h2_rows", (ROWS, D))
        y_rows = scratch("y_rows", (ROWS * 8, D))
        slot_tab = scratch("slot_tab", (NSLOT, 1))

        W = sb("W", [P, KT * 3072 + KT * D])
        ada_w = [W[:, 12288 + 4096 * r:16384 + 4096 * r].rearrange("p (k n) -> p k n", k=KT) for r in range(3)]
        mod_sb = W[0:9, 24576:24576 + 6 * D]
        gains = W[0:9, 24576 + 6 * D:24576 + 8 * D]
        w_in = W[:, 0:KT * 3072].rearrange("p (k n) -> p k n", k=KT)
        w_out = W[:, KT * 3072:KT * 4096].rearrange("p (k n) -> p k n", k=KT)
        S0 = W[:, 12288:16384].rearrange("p (b h e) -> p b h e", b=NS, h=H)
        vmask = W[0:NS, 16384:20480].rearrange("p (b n) -> p b n", b=NS)
        cbuf = W[:, 20480:20480 + CT * NS * CW].rearrange("p (c b w) -> p c b w", c=CT, b=NS)
        cprod = W[:, 21504:21504 + NS * CW].rearrange("p (b w) -> p b w", b=NS)
        crossT = W[:, 21760:21760 + H * NS].rearrange("p (h b) -> p h b", h=H)
        qk = W[:, 21800:21800 + H]
        qk_prod = W[:, 22016:22528].rearrange("p (h d) -> p h d", h=H)
        sconv = W[:, 22528:22528 + 2 * DC].rearrange("p (r n) -> p r n", r=2)
        ring = W[:, 0:RING * WE].rearrange("p (r w) -> p r w", r=RING)
        shw = W[:, RING * WE:RING * WE + WE]
        yk = [W[:, 7168 * r:7168 * (r + 1)].rearrange("p (k n) -> p k n", k=7) for r in range(2)]
        x2f = [W[:, 14336 + D * r:15360 + D * r] for r in range(2)]
        fin = [W[:, 16384 + D * r:17408 + D * r] for r in range(2)]

        ident = sb("ident", [P, P])
        mean_w = sb("mean_w", [P, P])
        ones_bf = sb("ones_bf", [P, P], BF16)
        tri_bf = sb("tri_bf", [P, P], BF16)
        maskT = sb("maskT", [P, H, P])
        rows_c = sb("rows_c", [P, 12])
        q_dec, k_dec, s_dec = rows_c[:, 0:4], rows_c[:, 4:8], rows_c[:, 8:12]
        lt = sb("lt", [P, NG, NG])
        kconst = sb("kconst", [P, 8])
        ones64 = sb("ones64", [P, NE])
        w_rt = sb("w_rt", [P, KT, NE])
        bias_r = sb("bias_r", [P, NE])
        mods = sb("mods", [P, 5, D])
        A_m, B_m, gt_m, A_f, B_f = (mods[:, v, :] for v in range(5))
        gret = sb("gret", [P, 2, DR])
        cvec = sb("cvec", [P, 12])
        cw = sb("cw", [P, CT, CW])
        mk_all = sb("mk_all", [P, NT, NE], BF16)
        w6 = sb("w6", [P, NT, TOPK])

        x_t = sb("x_t", [P, D])
        hT = sb("hT", [P, KT, P])
        sig = sb("sig", [P, DC])
        junk = sig[:, :].bitcast(BF16)
        glu = sb("glu", [P, DC])
        rt2 = sb("rt2", [P, DC])
        q_r = sb("q_r", [P, DR])
        k_r = sb("k_r", [P, DR])
        k_d = sb("k_d", [P, DR])
        v_t = sb("v_t", [P, DR])
        sg = sb("sg", [P, DR])
        win = sb("win", [P, CT, CW - 1 + P])
        qT = sb("qT", [P, H, P])
        kT = sb("kT", [P, H, P])
        sm = sb("sm", [P, H, P])
        S = sb("S", [P, H, HD])
        o_t = sb("o_t", [P, H, HD])
        cv = sb("cv", [P, CT, P])
        cat = sb("cat", [P, KT, P])
        h2T = cat
        xr = sb("xr", [P, D])
        rope = sb("rope", [P, 3, HD // 2])
        bn = sb("bn", [P, H, 6])
        mv = sb("mv", [P, H, 2])
        gstd = sb("gstd", [P, H])
        st = sb("st", [P, 6])
        eps_c = sb("eps_c", [P, 1])
        scrap = sb("scrap", [P, 1])
        tok_cur = sb("tok_cur", [P, 1], I32)
        slot_cur = sb("slot_cur", [P, 1], I32)
        ssq1, std1, rstd1, ssq2, std2, rstd2 = (st[:, i:i + 1] for i in range(6))
        sq = rt2[:, :].rearrange("p (c n) -> p c n", c=CT)
        cvrow = sm[:, 0, :]
        tk = cat[:, CT:, :].rearrange("p c n -> p (c n)")
        sc_t, sel, top8s = tk[:, 0:64], tk[:, 64:128], tk[:, 128:192]
        pair_a, pair_b = tk[:, 192:256], tk[:, 256:320]
        gsum, rank, keep, pen, t8 = (tk[:, 320 + 8 * i:328 + 8 * i] for i in range(5))
        ngt, need, wsum, wrec = (tk[:, 360 + i:361 + i] for i in range(4))
        pick, wfull = tk[:, 384:448], tk[:, 448:512]
        eq_k = rt2[:, 0:TOPK * NE].rearrange("p (k e) -> p k e", k=TOPK)
        U = [ctx.enter_context(nc.psum_tensor(f"U{i}", [P, 512], F32)) for i in range(2)]
        X = ctx.enter_context(nc.psum_tensor("X", [P, D], F32))
        T0 = ctx.enter_context(nc.psum_tensor("T0", [P, 512], F32))
        R = ctx.enter_context(nc.psum_tensor("R", [P, D], F32))
        R2 = ctx.enter_context(nc.psum_tensor("R2", [P, 512], F32))
        Xk = X[:, :].rearrange("p (k n) -> p k n", k=KT)
        T4 = T0[:, :].rearrange("p (h n) -> p h n", h=4)
        inner, cross = (R[:, 512 * i:512 * i + 512].rearrange("p (h n) -> p h n", h=H) for i in range(2))
        R24 = R2[:, :].rearrange("p (h n) -> p h n", h=4)
        xg, xgT, y_sb = x_t, hT, xr
        hsil, hid = sig[:, 0:DE], sig[:, DE:2 * DE]
        hidT = glu[:, 0:DE].rearrange("p (f n) -> p f n", f=FT)
        pairs = q_r[:, 0:NT * NE // 2].bitcast(BF16).rearrange("p (t e) -> p t e", t=NT)
        cnt_f, nblk, pend, pbase = (k_r[:, 64 * i:64 * i + 64] for i in range(4))
        cnt_i = k_r[:, 256:320].bitcast(I32)
        dest = k_d[:, 0:NE]
        dst_f = v_t[:, 0:8]
        dst_i = qT[:, 0, 0:NT * 8].bitcast(I32).rearrange("p (t k) -> p t k", t=NT)
        slot_val = qT[:, 3, 0:NT * 8].rearrange("p (t k) -> p t k", t=NT)
        slot_row, pad_row, tri_f = cv[:, 0, :], cv[:, 1, :], cv[:, 2, :]
        slot_i = kT[:, 0, :].bitcast(I32)
        tok_i = kT[:, 1, :].bitcast(I32)
        blk_f = st[:, 0:1]
        blk_cmp = o_t[:, 0, 0:NE]
        blk_no = sb("blk_no", [P, 1])
        blk_e = qT[0:1, 1, :].bitcast(I32)
        pend_i = qT[0:1, 2, 0:NE + 1].bitcast(I32)
        pos_last = R2[:, 0:NE]
        count = R2[:, NE:2 * NE]
        gt_f, g_fin = mods[:, 0, :], mods[:, 1, :]
        y_of = y_rows.rearrange("(t p k) d -> t p k d", p=P, k=8)

        BANK = {GB: 0, GA: 1, GQ: 0, GK: 1, GV: 0, GG: 1}

        def floor(n):
            return max(n, 0) if isinstance(n, int) else n

        def bc(ap, shape):
            return ap.unsqueeze(2).to_broadcast(shape)

        def everywhere(row, n=P):
            return row.to_broadcast([n, row.shape[1]])

        block = ctx.enter_context(nc.Block())

        @block.sync
        def _(sp):
            def ada(ch):
                sp.dma_start(ada_w[ch % 3],
                             t["w_ada"][0][:, 512 * ch:512 * ch + 512].rearrange("(k p) n -> p k n", p=P)).then_inc(ada_in[ch % 3], 16)

            sp.dma_start(xr[0:1, :], t["c_prompt"]).then_inc(c_in, 16)
            sp.dma_start(xr[1:9, :], t["c_sample"]).then_inc(c_in, 16)
            sp.dma_start(ident[:, :], t["ident"]).then_inc(ident_in, 16)
            for ch in range(3):
                ada(ch)
            sp.dma_start(mod_sb, everywhere(t["b_ada"][0:1, :], 9)).then_inc(bada_in, 16)
            sp.dma_start(gains[:, 0:D], everywhere(t["g_mix"][0:1, :], 9)).then_inc(bada_in, 16)
            sp.dma_start(gains[:, D:2 * D], everywhere(t["g_ffn"][0:1, :], 9)).then_inc(bada_in, 16)
            sp.dma_start(x_t[:, :], t["x_prompt"][0, 0:P, :]).then_inc(x_in, 16)
            sp.dma_start(rope[:, :, :], t["rope"][0:P]).then_inc(rope_in, 16)
            for ch in range(3, 12):
                sp.wait_ge(ada_done, ch - 2)
                ada(ch)
            for k in range(KT // 2):
                sp.dma_start(w_in[:, k, :], t["w_in"][0][P * k:P * k + P, :]).then_inc(win_in, 16)
            for n, name in enumerate(("conv_b", "conv_norm_g", "conv_norm_b")):
                sp.dma_start(cvrow[4 * n:4 * n + 4, :], t[name][0].rearrange("(c p) -> c p", p=P)).then_inc(cvec_in, 16)
            sp.dma_start(cv[0:CW, :, :], t["conv_w"][0].rearrange("w (c p) -> w c p", p=P)).then_inc(cvec_in, 16)
            for o, n in ((mean_w, "mean_w"), (maskT, "maskT"), (rows_c, "rows_c"), (lt, "lt"), (kconst, "kconst"),
                         (blk_no, "blk_no")):
                sp.dma_start(o[:], t[n]).then_inc(consts_in, 16)
            sp.dma_start(w_rt[:, :, :], t["w_router"][0].rearrange("(k p) n -> p k n", p=P)).then_inc(consts_in, 16)
            sp.dma_start(bias_r[:, :], everywhere(t["router_bias"][0:1, :])).then_inc(consts_in, 16)
            sp.dma_start(gret[:, 0, :], everywhere(t["ret_norm_g"][0:1, :])).then_inc(consts_in, 16)
            sp.dma_start(gret[:, 1, :], everywhere(t["ret_norm_b"][0:1, :])).then_inc(consts_in, 16)
            sp.wait_ge(mod_ready, 12)
            sp.dma_start(mod_rows, mod_sb).then_inc(mod_stored, 16)
            for k in range(KT // 2, KT):
                sp.dma_start(w_in[:, k, :], t["w_in"][0][P * k:P * k + P, :]).then_inc(win_in, 16)
            sp.wait_ge(mod_stored, 16)
            for v, m in enumerate((1, 0, 2, 4, 3)):
                sp.dma_start(mods[:, v, :], everywhere(mod_rows[0:1, D * m:D * m + D])).then_inc(modv_in, 16)
            sp.dma_start(w_out[:, :, :], t["w_out"][0].rearrange("(k p) n -> p k n", p=P)).then_inc(wout_in, 16)

            def load_next(i):
                sp.wait_ge(x_posed, i + 1)
                if isinstance(i, int) and i + 1 == TP:
                    sp.dma_start(x_t[0:NS, :], t["x_sample"][:, 0, :]).then_inc(x_in, 16)
                else:
                    sp.dma_start(x_t[:, :], t["x_prompt"][0][bass.ds((i + 1) * P, P), :]).then_inc(x_in, 16)

            def load_rope(i):
                sp.wait_ge(k_rot, i + 1)
                sp.dma_start(rope[:, :, :], t["rope"][bass.ds((i + 1) * P, P)]).then_inc(rope_in, 16)

            def store_route(m):
                sp.wait_ge(x2_ready, m + 1)
                sp.dma_start(x2_rows[bass.ds(m * P, P), :], xr[:, :]).then_inc(x2_stored, 16)
                sp.wait_ge(h2_ready, m + 1)
                sp.dma_start(h2_rows[bass.ds(m * P, P), :], xr[:, :]).then_inc(h2_stored, 16)

            def load_residual(j):
                if isinstance(j, int) and j == 0:
                    sp.wait_ge(cT_ready, 1)
                else:
                    sp.wait_ge(h2_stored, 16 * j)
                    sp.wait_ge(h2_posed, j)
                if isinstance(j, int) and j == TP:
                    sp.dma_start(xr[0:NS, :], t["x_sample"][:, 0, :]).then_inc(xr_in, 16)
                else:
                    sp.dma_start(xr[:, :], t["x_prompt"][0][bass.ds(j * P, P), :]).then_inc(xr_in, 16)

            load_next(0)
            load_rope(0)
            load_next(1)
            load_residual(0)
            load_rope(1)
            with sp.Fori(2, TP - 1) as i:
                load_next(i)
                store_route(i - 2)
                load_residual(i - 1)
                load_rope(i)
            sp.wait_ge(h_ready, TP)
            sp.dma_start(mods[0:NS, 0, :], mod_rows[1:9, D:2 * D]).then_inc(smod1_in, 16)
            sp.dma_start(mods[0:NS, 1, :], mod_rows[1:9, 0:D]).then_inc(smod1_in, 16)
            load_next(TP - 1)
            store_route(TP - 3)
            load_residual(TP - 2)
            sp.wait_ge(glu_ready, TP)
            sp.dma_start(out["new_conv_prompt"][0, 0], glu[P - CW + 1:P, :]).then_inc(glu_last_out, 16)
            load_rope(TP - 1)
            sp.dma_start(out["new_conv_sample"][0][:, 0:CW - 2, :],
                         t["state_conv"][0][:, 1:CW - 1, :]).then_inc(newconv_out, 16)
            store_route(TP - 2)
            load_residual(TP - 1)
            sp.wait_ge(ug_done, NT)
            for r in range(2):
                sp.dma_start(sconv[0:120, r, :],
                             t["state_conv"][0][4 * r:4 * r + 4].rearrange("b w n -> (b w) n")).then_inc(sconv_in, 16)
            for b in range(NS):
                sp.dma_start(S0[:, b, :, :], t["state_ret"][0][b].rearrange("h d e -> d h e")).then_inc(s0_in, 16)

            def load_expert(e, r):
                o = ring[:, r, 0:KT * 2 * DE].rearrange("p (k x n) -> p k x n", k=KT, x=2)
                one = bass.ds(e, 1)
                sp.dma_start(o[:, :, 0, :],
                             t["w1"][0][one].rearrange("a (k p) n -> p (a k) n", p=P)).then_inc(ring_in[r], 16)
                sp.dma_start(o[:, :, 1, :],
                             t["w3"][0][one].rearrange("a (k p) n -> p (a k) n", p=P)).then_inc(ring_in[r], 16)
                sp.dma_start(ring[:, r, KT * 2 * DE:].rearrange("p (f n) -> p f n", f=FT),
                             t["w2"][0][one].rearrange("a (f p) n -> p (a f) n", p=P)).then_inc(ring_in[r], 16)

            load_expert(0, 0)
            load_expert(1, 1)
            sp.wait_ge(glu_ready, NT)
            sp.dma_start(out["new_conv_sample"][0][:, CW - 2, :], glu[0:NS, :]).then_inc(newconv_out, 16)
            sp.wait_ge(S_ready, TP)
            sp.dma_start(out["new_ret_prompt"][0, 0].rearrange("h d e -> d h e"), S[:, :, :]).then_inc(newret_out, 16)
            sp.wait_ge(y_gated, TP)
            sp.dma_start(mods[0:NS, 2, :], mod_rows[1:9, 2 * D:3 * D]).then_inc(smod2_in, 16)
            store_route(TP - 1)
            sp.dma_start(mods[0:NS, 3, :],
                         mod_rows[1:9, 4 * D:5 * D]).then_inc(smod3_in, 16)
            sp.dma_start(mods[0:NS, 4, :], mod_rows[1:9, 3 * D:4 * D]).then_inc(smod3_in, 16)
            load_residual(TP)
            sp.wait_ge(state_upd, 2 * H)
            for b in range(NS):
                sp.dma_start(out["new_ret_sample"][0, b].rearrange("h d e -> d h e"),
                             S0[:, b, :, :]).then_inc(newret_out, 16)
            sp.wait_ge(newret_out, 16 * (NS + 1))
            sp.wait_ge(wout_done, NT)
            o = shw[:, 0:KT * 2 * DE].rearrange("p (k x n) -> p k x n", k=KT, x=2)
            sp.dma_start(o[:, :, 0, :], t["ws1"][0].rearrange("(k p) n -> p k n", p=P)).then_inc(shw_in, 16)
            sp.dma_start(o[:, :, 1, :], t["ws3"][0].rearrange("(k p) n -> p k n", p=P)).then_inc(shw_in, 16)
            sp.dma_start(shw[:, KT * 2 * DE:].rearrange("p (f n) -> p f n", f=FT),
                         t["ws2"][0].rearrange("(f p) n -> p f n", p=P)).then_inc(shw_in, 16)
            store_route(TP)
            sp.wait_ge(h2_stored, 16 * NT)
            sp.dma_start(tri_f, t["tri"]).then_inc(tri_in, 16)
            sp.dma_start(slot_val, t["slot_val"]).then_inc(tri_in, 16)
            sp.wait_ge(pad_ready, 1)
            sp.dma_start(slot_tab.rearrange("(b r) a -> b (r a)", r=P), pad_row).then_inc(table_filled, 16)
            sp.dma_start(xg[:, :], h2_rows[0:P, :]).then_inc(xg_in, 16)
            load_expert(2, 2)
            load_expert(3, 3)

            def load_rows(n):
                sp.wait_ge(xg_posed, n)
                sp.dma_start(xg[:, :], h2_rows[bass.ds(n * P, P), :]).then_inc(xg_in, 16)

            def store_shared(n):
                sp.wait_ge(y_evac, n + 1)
                sp.dma_start(y_of[bass.ds(n, 1), :, 6, :].rearrange("a p d -> (a p) d"), y_sb[:, :]).then_inc(ysh_stored, 16)

            load_rows(1)
            with sp.Fori(1, NT - 1) as n:
                load_rows(n + 1)
                store_shared(n - 1)
            store_shared(NT - 2)
            store_shared(NT - 1)
            sp.wait_ge(slots_out, 16 * NT * TOPK)
            sp.dma_start(slot_row, slot_tab.rearrange("(b r) a -> b (r a)", r=P)).then_inc(slot_in, 16)
            for r in range(RING - 1):
                sp.wait_ge(ring_in[r], 48)
                sp.sem_inc(w_ready, 1)
            sp.wait_ge(blkrow_ready, 1)
            with sp.Fori(1, NE // RING) as g:
                for r in range(RING):
                    before = sp.value_load(pend_i[0:1, bass.ds((g - 1) * RING + r, 1)], min_val=0, max_val=MAXBLK)
                    sp.wait_ge(y_done, before + NT)
                    load_expert(g * RING + r, r)
                    sp.wait_ge(ring_in[(r - 1) % RING], 48 * g if r == 0 else 48 * g + 48)
                    sp.sem_inc(w_ready, 1)
            sp.wait_ge(ring_in[RING - 1], 48 * (NE // RING))
            sp.sem_inc(w_ready, 1)
            last = sp.value_load(pend_i[0:1, NE:], min_val=MINBLK - 1, max_val=MAXBLK - 1)
            sp.dma_start(gt_f, everywhere(mod_rows[0:1, 5 * D:6 * D])).then_inc(finv_in, 16)
            sp.dma_start(g_fin, everywhere(t["g_final"].rearrange("(a n) -> a n", a=1))).then_inc(finv_in, 16)
            sp.wait_ge(ysh_stored, 16 * NT)
            sp.wait_ge(x2_stored, 16 * NT)
            sp.wait_ge(scattered, 16 * last + 16)

            def load_tile(i, r, rows=P):
                sp.dma_start(yk[r][0:rows],
                             y_of[bass.ds(i, 1), 0:rows, 0:7, :].rearrange("a p k d -> (a p) k d")).then_inc(rows_in[r], 16)
                sp.dma_start(x2f[r][0:rows], x2_rows[bass.ds(i * P, rows), :]).then_inc(rows_in[r], 16)

            load_tile(0, 0)
            load_tile(1, 1)

            def store_result(g, r):
                sp.wait_ge(fin_ready[r], g + 1)
                sp.dma_start(out["y_prompt"][0][bass.ds((2 * g + r) * P, P), :], fin[r]).then_inc(fin_stored[r], 16)

            with sp.Fori(0, TP // 2 - 1) as g:
                for r in range(2):
                    store_result(g, r)
                    load_tile(2 * g + r + 2, r)
            for r in range(2):
                store_result(TP // 2 - 1, r)
            sp.dma_start(gt_f[0:NS, :], mod_rows[1:9, 5 * D:6 * D]).then_inc(finv_in, 16)
            load_tile(TP, 0, NS)
            sp.wait_ge(fin_ready[0], TP // 2 + 1)
            sp.dma_start(out["y_sample"][:, 0, :], fin[0][0:NS, :]).then_inc(fin_stored[0], 16)
            sp.wait_ge(fin_stored[0], 16 * (TP // 2 + 1))
            sp.wait_ge(fin_stored[1], 16 * (TP // 2))
            sp.wait_ge(glu_last_out, 16)
            sp.wait_ge(newconv_out, 32)

        @block.tensor
        def _(pe):
            mm, tr = nc.tensor.matmul, nc.tensor.transpose

            pe.wait_ge(csilu, 1)
            pe.wait_ge(ident_in, 16)
            for k in range(KT):
                last = tr(X[:, 16 * k:16 * k + 9], xr[0:9, P * k:P * k + P], ident[0:9, 0:9])
            last.then_inc(c_posed, 1)
            pe.wait_ge(cT_ready, 1)
            for ch in range(12):
                pe.wait_ge(ada_in[ch % 3], 16 * (ch // 3 + 1))
                pe.wait_ge(mod_ready, floor(ch - 1))
                for k in range(KT):
                    last = mm(U[ch % 2][0:9, :], hT[:, k, 0:9], ada_w[ch % 3][:, k, :], start=k == 0, stop=k == KT - 1)
                last.then_inc(ada_done, 1)
            pe.wait_ge(cvec_in, 64)
            for c in range(CT):
                tr(T0[:, 32 * c:32 * c + CW], cv[0:CW, c, :], ident[0:CW, 0:CW])
            tr(T0[:, P:P + 12], cvrow[0:12, :], ident[0:12, 0:12]).then_inc(cvec_posed, 1)

            def x_trans(i):
                pe.wait_ge(h_ready, i + 1)
                pe.wait_ge(h2T_ready, floor(i - 2))
                for k in range(KT):
                    last = tr(Xk[:, k, :], x_t[:, P * k:P * k + P], ident[:, :])
                last.then_inc(x_posed, 1)

            def project(i, g, done, free, n):
                pe.wait_ge(free, n)
                for k in range(KT):
                    last = mm(U[BANK[g]][:, :], hT[:, k, :], w_in[:, k, 512 * g:512 * g + 512], start=k == 0, stop=k == KT - 1)
                last.then_inc(done, 1)

            def four(src, done, free, n, ready, m):
                pe.wait_ge(ready, m)
                pe.wait_ge(free, n)
                for c in range(4):
                    last = tr(T4[:, c, :], src[:, P * c:P * c + P], ident[:, :])
                last.then_inc(done, 1)

            def norm_sum(src, done, ready, n):
                pe.wait_ge(ready, n)
                for c in range(CT):
                    last = mm(T0[:, 0:P], mean_w[:, :], src[:, c, :], start=c == 0, stop=c == CT - 1)
                last.then_inc(done, 1)

            def body(i, front=True, tail=True, route=True, nxt=True):
                j, m = i - 1, i - 2
                if front:
                    pe.wait_ge(hT_ready, i + 1)
                    project(i, GB, ub_done, v_ready, i)
                if tail:
                    four(glu, glu_posed, catB_ready, j, glu_ready, j + 1)
                if front:
                    project(i, GA, ua_done, sg_ready, i)
                if tail:
                    four(q_r, q_posed, win_ready, j + 1, q_rot, j + 1)
                if route:
                    pe.wait_ge(h2_ready, m + 1)
                    pe.wait_ge(hT_ready, min(i + 1, NT) if isinstance(i, int) else i + 1)
                    for k in range(KT):
                        last = tr(Xk[:, k, :], xr[:, P * k:P * k + P], ident[:, :])
                    last.then_inc(h2_posed, 1)
                if front:
                    project(i, GQ, uq_done, sig_ready, i + 1)
                if tail:
                    four(k_r, k_posed, qT_ready, j + 1, k_rot, j + 1)
                if route:
                    pe.wait_ge(h2T_ready, m + 1)
                    for k in range(KT):
                        last = mm(R2[:, 0:NE], h2T[:, k, :], w_rt[:, k, :], start=k == 0, stop=k == KT - 1)
                    last.then_inc(router_done, 1)
                prompt = not (isinstance(j, int) and j == TP)
                if tail and prompt:
                    pe.wait_ge(kT_ready, j + 1)
                    for h in range(H):
                        last = mm(T4[:, h, :], kT[:, h, :], qT[:, h, :], start=True, stop=True)
                    last.then_inc(scores_done, 1)
                if front:
                    project(i, GK, uk_done, glu_ready, i + 1)
                if tail and prompt:
                    pe.wait_ge(sm_ready, j + 1)
                    pe.wait_ge(v_ready, j + 1)
                    pe.wait_ge(S_ready, j)
                    pe.wait_ge(y_gated, j)
                    pe.wait_ge(x2_ready, j)
                    pe.wait_ge(h2_ready, j)
                    for h in range(H):
                        mm(inner[:, h, :], sm[:, h, :], v_t[:, P * h:P * h + P], start=True, stop=True)
                        mm(cross[:, h, :], qT[:, h, :], S[:, h, :], start=True, stop=True)
                    pe.wait_ge(kd_ready, j + 1)
                    pe.wait_ge(score_ready, j)
                    for h in range(H):
                        last = mm(R24[:, h, :], k_d[:, P * h:P * h + P], v_t[:, P * h:P * h + P], start=True, stop=True)
                    last.then_inc(ret_done, 1)
                if tail and not prompt:
                    pe.wait_ge(kT_ready, j + 1)
                    pe.wait_ge(s0_in, 16 * NS)
                    pe.wait_ge(h2_ready, j)
                    for h in range(H):
                        for b in range(NS):
                            last = mm(R[:, h * NS + b:h * NS + b + 1], S0[:, b, h, :], qT[:, h, b:b + 1], start=True, stop=True)
                    last.then_inc(s_cross_done, 1)
                    pe.wait_ge(crossT_ready, 1)
                    for h in range(H):
                        last = tr(cross[0:NS, h, :], crossT[:, h, :], ident[:, :])
                    last.then_inc(cross_posed, 1)
                    pe.wait_ge(vmask_ready, 1)
                    for n in range(2 * H):
                        h, half = n // 2, n % 2
                        pe.wait_ge(state_upd, floor(n - 1))
                        if n == 0:
                            pe.wait_ge(v_ready, NT)
                            pe.wait_ge(sg_ready, NT)
                        mm(U[n % 2][:, :], k_r[0:NS, P * h:P * h + P], vmask[:, 4 * half:4 * half + 4, P * h:P * h + P],
                           start=True, stop=True).then_inc(state_mm, 1)
                    pe.wait_ge(kT_ready, NT)
                    pe.wait_ge(sconv_in, 32)
                    for c in range(CT):
                        pe.wait_ge(cs_half, 2 * (c))
                        for r in range(2):
                            last = tr(T0[:, 128 * r:128 * r + 120], sconv[0:120, r, P * c:P * c + P], ident[0:120, 0:120])
                        last.then_inc(cs_posed, 1)
                    pe.wait_ge(cs_half, 2 * (CT))
                if front:
                    project(i, GV, uv_done, q_rot, i + 1)
                if tail:
                    norm_sum(cv, sum1_done, conv_ready, j + 1)
                if front:
                    project(i, GG, ug_done, k_rot, i + 1)
                if tail:
                    pe.wait_ge(cen_ready, j + 1)
                    norm_sum(sq, sum2_done, sq_ready, j + 1)
                if nxt:
                    x_trans(i + 1)
                if tail:
                    four(o_t[:, :, :].rearrange("p h e -> p (h e)"), ret_posed, cnorm_ready, j + 1, ret_ready, j + 1)
                    pe.wait_ge(catA_part, 4 * (j + 1))
                    pe.wait_ge(catB_ready, j + 1)
                    for n in range(2):
                        for k in range(KT):
                            last = mm(R[:, 512 * n:512 * n + 512], cat[:, k, :], w_out[:, k, 512 * n:512 * n + 512],
                                      start=k == 0, stop=k == KT - 1)
                    last.then_inc(wout_done, 1)

            x_trans(0)
            pe.wait_ge(win_in, 16 * KT)
            body(0, tail=False, route=False)
            pe.wait_ge(consts_in, 16 * 10)
            pe.wait_ge(wout_in, 16)
            pe.wait_ge(state_zero, 1)
            pe.wait_ge(cvec_ready, 1)
            body(1, route=False)
            with pe.Fori(2, TP) as i:
                body(i)
            body(TP, nxt=False)
            body(TP + 1, front=False, nxt=False)
            body(TP + 2, front=False, tail=False, nxt=False)

            pe.wait_ge(pairs_ready, 1)
            pe.wait_ge(score_ready, NT)
            for i in range(NT):
                o = U[0][:, NE * i:NE * i + NE] if i < TP else pos_last
                for j in range(i):
                    mm(o, ones_bf[:, :], pairs[:, j, :], start=j == 0, stop=False)
                mm(o, tri_bf[:, :], pairs[:, i, :], start=i == 0, stop=True)
            for j in range(NT):
                last = mm(count, ones_bf[:, :], pairs[:, j, :], start=j == 0, stop=j == NT - 1)
            last.then_inc(pos_done, 1)

            def rows_trans(n, arrived, k):
                pe.wait_ge(arrived, k)
                pe.wait_ge(xgT_ready, n)
                for c in range(KT):
                    last = tr(Xk[:, c, :], xg[:, P * c:P * c + P], ident[:, :])
                last.then_inc(xg_posed, 1)

            def up(n, weights):
                pe.wait_ge(xgT_ready, n + 1)
                for k in range(KT):
                    last = mm(U[1][:, :], xgT[:, k, :], weights[:, 512 * k:512 * k + 512], start=k == 0, stop=k == KT - 1)
                last.then_inc(h_done, 1)

            def hidden_trans(n):
                pe.wait_ge(hid_ready, n + 1)
                for f in range(FT):
                    last = tr(T0[:, P * f:P * f + P], hid[:, P * f:P * f + P], ident[:, :])
                last.then_inc(hid_posed, 1)

            def down(n, weights):
                pe.wait_ge(hidT_ready, n + 1)
                pe.wait_ge(y_evac, n)
                for half in range(2):
                    for f in range(FT):
                        at = KT * 2 * DE + D * f + 512 * half
                        last = mm(R[:, 512 * half:512 * half + 512], hidT[:, f, :], weights[:, at:at + 512],
                                  start=f == 0, stop=f == FT - 1)
                last.then_inc(y_done, 1)

            pe.wait_ge(shw_in, 48)
            rows_trans(0, xg_in, 16)
            up(0, shw)
            rows_trans(1, xg_in, 32)
            hidden_trans(0)
            def shared(n):
                up(n, shw)
                rows_trans(n + 1, xg_in, 16 * n + 32)
                down(n - 1, shw)
                hidden_trans(n)

            shared(1)
            with pe.Fori(2, NT - 1) as n:
                shared(n)
            up(NT - 1, shw)
            down(NT - 2, shw)
            hidden_trans(NT - 1)
            down(NT - 1, shw)
            pe.wait_ge(dest_ready, NT)
            pe.wait_ge(slot_in, 16)
            tr(U[0][:, 0:P], slot_row, ident[:, :]).then_inc(slot_posed, 1)
            pe.wait_ge(blk_ready, 1)
            mm(U[0][0:1, P:2 * P], blk_f, ident[:, :], start=True, stop=True).then_inc(blkrow_posed, 1)

            def weights_of(b, first=True):
                e = pe.value_load(blk_e[0:1, bass.ds(b, 1)], min_val=0, max_val=NE - 1)
                if first:
                    pe.wait_ge(w_ready, e + 1)
                return ring[:, bass.ds(e % RING, 1), :].rearrange("p a w -> p (a w)")

            pe.wait_ge(blkrow_ready, 1)
            last = pe.value_load(pend_i[0:1, NE:], min_val=MINBLK - 1, max_val=MAXBLK - 1)
            rows_trans(NT, gathered, 16)
            up(NT, weights_of(0))
            rows_trans(NT + 1, gathered, 32)
            hidden_trans(NT)
            with pe.Fori(1, MAXBLK) as b:
                with pe.If(b <= last):
                    up(b + NT, weights_of(b))
                    rows_trans(b + NT + 1, gathered, 16 * b + 32)
                    down(b + NT - 1, weights_of(b - 1, False))
                    hidden_trans(b + NT)
            down(last + NT, weights_of(last, False))

        @block.scalar
        def _(act):
            act.wait_ge(c_in, 32)
            nc.scalar.activation(xr[0:9, :], xr[0:9, :], ACT.Silu).then_inc(csilu, 1)
            act.wait_ge(csilu, 1)
            act.wait_ge(c_posed, 1)
            nc.scalar.activation(hT[:, :, 0:9], X[:, 0:16 * KT].rearrange("p (k n) -> p k n", k=KT)[:, :, 0:9],
                                 ACT.Copy).then_inc(cT_ready, 1)
            act.wait_ge(cT_ready, 1)

            def norm1(i):
                act.wait_ge(x_in, 16 * (i + 1))
                act.wait_ge(glu_ready, i)
                nc.scalar.activation(junk, x_t[:, :], ACT.Square, accum_out=ssq1).then_inc(norm1_ssq, 1)
                act.wait_ge(norm1_ssq, i + 1)
                act.wait_ge(norm1_ssq, i + 1)
                act.wait_ge(h_scaled, i)
                nc.scalar.activation(std1, ssq1, ACT.Sqrt, scale=1.0 / D, bias=eps_c[:, 0:1]).then_inc(norm1_std, 1)
                act.wait_ge(norm1_std, i + 1)

            def hT_copy(i):
                act.wait_ge(x_posed, i + 1)
                nc.scalar.activation(hT[:, :, :], Xk, ACT.Copy).then_inc(hT_ready, 1)
                act.wait_ge(hT_ready, i + 1)

            def body(i, front=True, tail=True, route=True, nxt=True):
                j, m = i - 1, i - 2
                if route:
                    act.wait_ge(x2_ready, m + 1)
                    act.wait_ge(glu_ready, min(i, NT) if isinstance(i, int) else i)
                    nc.scalar.activation(junk, xr[:, :], ACT.Square, accum_out=ssq2).then_inc(norm2_ssq, 1)
                    act.wait_ge(norm2_ssq, m + 1)
                    act.wait_ge(norm2_ssq, m + 1)
                    nc.scalar.activation(std2, ssq2, ACT.Sqrt, scale=1.0 / D, bias=eps_c[:, 0:1]).then_inc(norm2_std, 1)
                    act.wait_ge(norm2_std, m + 1)
                if front:
                    act.wait_ge(ub_done, i + 1)
                    nc.scalar.activation(sig[:, :], U[0][:, :], ACT.Sigmoid).then_inc(sig_ready, 1)
                    act.wait_ge(sig_ready, i + 1)
                if tail:
                    act.wait_ge(glu_posed, j + 1)
                    act.wait_ge(win_shifted, j)
                    nc.scalar.activation(win[:, :, CW - 1:], T4, ACT.Copy).then_inc(win_ready, 1)
                    act.wait_ge(win_ready, j + 1)
                    act.wait_ge(q_posed, j + 1)
                    nc.scalar.activation(qT[:, :, :], T4, ACT.Copy).then_inc(qT_ready, 1)
                    act.wait_ge(qT_ready, j + 1)
                if route:
                    act.wait_ge(h2_posed, m + 1)
                    nc.scalar.activation(h2T[:, :, :], Xk, ACT.Copy).then_inc(h2T_ready, 1)
                    act.wait_ge(h2T_ready, m + 1)
                if tail:
                    act.wait_ge(k_posed, j + 1)
                    nc.scalar.activation(kT[:, :, :], T4, ACT.Copy).then_inc(kT_ready, 1)
                    act.wait_ge(kT_ready, j + 1)
                if route:
                    act.wait_ge(router_done, m + 1)
                    nc.scalar.activation(sc_t, R2[:, 0:NE], ACT.Sigmoid).then_inc(score_ready, 1)
                    act.wait_ge(score_ready, m + 1)
                prompt = not (isinstance(j, int) and j == TP)
                if tail and not prompt:
                    act.wait_ge(s_cross_done, 1)
                    nc.scalar.activation(crossT, R[:, 0:H * NS].rearrange("p (h b) -> p h b", h=H),
                                         ACT.Copy).then_inc(crossT_ready, 1)
                    act.wait_ge(crossT_ready, 1)
                    for c in range(CT):
                        act.wait_ge(cs_posed, c + 1)
                        for r in range(2):
                            nc.scalar.activation(cbuf[:, c, 4 * r:4 * r + 4, 0:CW - 1],
                              T0[:, 128 * r:128 * r + 120].rearrange("p (b w) -> p b w", b=4), ACT.Copy).then_inc(
                                  cs_half, 1)
                            act.wait_ge(cs_half, 2 * c + r + 1)
                if tail:
                    act.wait_ge(gn_var, j + 1)
                    nc.scalar.activation(gstd[:, :], mv[:, :, 1], ACT.Sqrt, bias=eps_c[:, 0:1]).then_inc(gn_std, 1)
                    act.wait_ge(gn_std, j + 1)
                if front:
                    act.wait_ge(uv_done, i + 1)
                    nc.scalar.activation(v_t[:, :], U[0][:, :], ACT.Copy).then_inc(v_ready, 1)
                    act.wait_ge(v_ready, i + 1)
                if tail:
                    act.wait_ge(cen_ready, j + 1)
                    nc.scalar.activation(sq, cv[:, :, :], ACT.Square).then_inc(sq_ready, 1)
                    act.wait_ge(sq_ready, j + 1)
                if nxt:
                    norm1(i + 1)
                if tail:
                    act.wait_ge(sum2_done, j + 1)
                    nc.scalar.activation(T0[:, P:2 * P], T0[:, 0:P], ACT.Sqrt, bias=eps_c[:, 0:1]).then_inc(std_c, 1)
                    act.wait_ge(std_c, j + 1)
                if front:
                    act.wait_ge(ug_done, i + 1)
                    act.wait_ge(ret_ready, i)
                    nc.scalar.activation(sg[:, :], U[1][:, :], ACT.Silu).then_inc(sg_ready, 1)
                    act.wait_ge(sg_ready, i + 1)
                if tail:
                    act.wait_ge(cnorm_ready, j + 1)
                    act.wait_ge(router_done, m + 1)
                    for c in range(CT):
                        nc.scalar.activation(cat[:, c, :], cv[:, c, :],
                                             ACT.Silu, scale=cvec[:, CT + c:CT + c + 1], bias=cvec[:, 2 * CT + c:2 * CT + c + 1]).then_inc(catA_part, 1)
                        act.wait_ge(catA_part, 4 * j + c + 1)
                if nxt:
                    hT_copy(i + 1)
                if tail:
                    act.wait_ge(ret_posed, j + 1)
                    act.wait_ge(topk_done, m + 1)
                    nc.scalar.activation(cat[:, CT:, :], T4, ACT.Copy).then_inc(catB_ready, 1)
                    act.wait_ge(catB_ready, j + 1)

            act.wait_ge(state_zero, 1)
            norm1(0)
            hT_copy(0)
            body(0, tail=False, route=False)
            body(1, route=False)
            with act.Fori(2, TP) as i:
                body(i)
            body(TP, nxt=False)
            body(TP + 1, front=False, nxt=False)
            body(TP + 2, front=False, tail=False, nxt=False)

            def blk_T(n):
                act.wait_ge(xg_posed, n + 1)
                nc.scalar.activation(xgT[:, :, :], Xk, ACT.Copy).then_inc(xgT_ready, 1)

            def blk_silu(n):
                act.wait_ge(h_done, n + 1)
                act.wait_ge(hid_ready, n)
                nc.scalar.activation(hsil, U[1][:, 0:DE], ACT.Silu).then_inc(silu_ready, 1)

            act.wait_ge(h2_posed, NT)
            blk_T(0)
            blk_silu(0)
            blk_T(1)
            with act.Fori(1, NT - 1) as n:
                blk_silu(n)
                blk_T(n + 1)
            blk_silu(NT - 1)
            blk_T(NT)
            act.wait_ge(blkrow_ready, 1)
            last = act.value_load(pend_i[0:1, NE:], min_val=MINBLK - 1, max_val=MAXBLK - 1)
            with act.Fori(0, MAXBLK) as b:
                with act.If(b <= last):
                    blk_silu(b + NT)
                    blk_T(b + NT + 1)

            def last_norm(i, rows=P):
                act.wait_ge(x3_ready, i + 1)
                nc.scalar.activation(junk[0:rows, :], xg[0:rows, :],
                                     ACT.Square, accum_out=ssq1[0:rows, :]).then_inc(fin_ssq, 1)
                act.wait_ge(fin_ssq, i + 1)
                act.wait_ge(fin_ssq, i + 1)
                nc.scalar.activation(std1[0:rows, :], ssq1[0:rows, :],
                                     ACT.Sqrt, scale=1.0 / D, bias=eps_c[0:rows, 0:1]).then_inc(fin_std, 1)
                act.wait_ge(fin_std, i + 1)

            with act.Fori(0, TP) as i:
                last_norm(i)
            last_norm(TP, NS)

        @block.vector
        def _(dve):
            v = nc.vector
            own = Steps(dve, dve_step)
            link = own.link

            link(v.memset(win[:, :, 0:CW - 1], 0.0))
            link(v.memset(ones_bf[:, :], 1.0))
            link(v.memset(ones64[:, :], 1.0))
            link(v.memset(mk_all[:, TP, :], 0.0))
            link(v.memset(eps_c[:, :], EPS))
            v.memset(S[:, :, :], 0.0).then_inc(state_zero, 1)
            dve.wait_ge(state_zero, 1)

            def norm1(i):
                dve.wait_ge(norm1_std, i + 1)
                link(v.reciprocal(rstd1, std1))
                if isinstance(i, int) and i == TP:
                    dve.wait_ge(smod1_in, 32)
                v.scalar_tensor_tensor(x_t[:, :], x_t[:, :], rstd1, A_m, ALU.mult, ALU.mult).then_inc(h_scaled, 1)
                dve.wait_ge(h_scaled, i + 1)

            dve.wait_ge(bada_in, 48)
            for ch in range(12):
                dve.wait_ge(ada_done, ch + 1)
                o = mod_sb[:, 512 * ch:512 * ch + 512]
                ins = v.tensor_tensor(o, U[ch % 2][0:9, :], o, ALU.add)
                if ch // 2 in (1, 4):
                    link(ins)
                    at = D * (ch // 8) + 512 * (ch % 2)
                    ins = v.scalar_tensor_tensor(o, o, 1.0, gains[:, at:at + 512], ALU.add, ALU.mult)
                ins.then_inc(mod_ready, 1)
                dve.wait_ge(mod_ready, ch + 1)
            dve.wait_ge(modv_in, 80)
            norm1(0)
            dve.wait_ge(cvec_posed, 1)
            link(v.tensor_copy(cw[:, :, :], T0[:, 0:P].rearrange("p (c w) -> p c w", c=CT)[:, :, 0:CW]))
            v.tensor_copy(cvec[:, :], T0[:, P:P + 12]).then_inc(cvec_ready, 1)
            dve.wait_ge(cvec_ready, 1)
            dve.wait_ge(consts_in, 16 * 10)

            def rotate(o, bank, done, i):
                u = U[bank][:, :].rearrange("p (g d) -> p g d", d=HD // 2)
                uh = U[bank][:, :].rearrange("p (h z d) -> p h z d", h=H, z=2)
                th = rt2[:, :].rearrange("p (h z d) -> p h z d", h=H, z=2)
                half = [P, H, HD // 2]
                v.tensor_tensor(o[:, :].rearrange("p (g d) -> p g d", d=HD // 2), u,
                                rope[:, 0, :].unsqueeze(1).to_broadcast([P, 2 * H, HD // 2]), ALU.mult)
                v.tensor_tensor(th[:, :, 0, :], uh[:, :, 1, :], rope[:, 1, :].unsqueeze(1).to_broadcast(half), ALU.mult)
                link(v.tensor_tensor(th[:, :, 1, :], uh[:, :, 0, :], rope[:, 2, :].unsqueeze(1).to_broadcast(half), ALU.mult))
                v.tensor_tensor(o[:, :], o[:, :], rt2[:, :], ALU.add).then_inc(done, 1)
                dve.wait_ge(done, i + 1)

            def conv(c):
                link(v.tensor_scalar(cv[:, c, :], win[:, c, 0:P], cw[:, c, 0:1], cvec[:, c:c + 1], ALU.mult, ALU.add))
                for w in range(1, CW):
                    ins = v.scalar_tensor_tensor(cv[:, c, :], win[:, c, w:w + P], cw[:, c, w:w + 1], cv[:, c, :],
                                                 ALU.mult, ALU.add)
                    if w < CW - 1:
                        link(ins)
                return ins

            def route_norm(m):
                dve.wait_ge(wout_done, m + 1)
                if isinstance(m, int) and m == TP:
                    dve.wait_ge(smod2_in, 16)
                v.tensor_tensor(R[:, :], R[:, :], gt_m, ALU.mult).then_inc(y_gated, 1)
                dve.wait_ge(y_gated, m + 1)
                dve.wait_ge(xr_in, 16 * (m + 1))
                v.tensor_tensor(xr[:, :], R[:, :], xr[:, :], ALU.add).then_inc(x2_ready, 1)
                dve.wait_ge(x2_ready, m + 1)
                dve.wait_ge(norm2_std, m + 1)
                link(v.reciprocal(rstd2, std2))
                if isinstance(m, int) and m == TP:
                    dve.wait_ge(smod3_in, 32)
                link(v.scalar_tensor_tensor(R[:, :], xr[:, :], rstd2, A_f, ALU.mult, ALU.mult))
                dve.wait_ge(x2_stored, 16 * (m + 1))
                v.tensor_tensor(xr[:, :], R[:, :], B_f, ALU.add).then_inc(h2_ready, 1)
                dve.wait_ge(h2_ready, m + 1)

            def top_k(m):
                dve.wait_ge(score_ready, m + 1)
                g3 = [P, NG, PER]
                link(v.tensor_tensor(sel, sc_t, bias_r[:, :], ALU.add))
                v.memset(scrap[:, :], 0.0)
                for g in range(NG):
                    ins = v.max(top8s[:, PER * g:PER * g + PER], sel[:, PER * g:PER * g + PER])
                link(ins)
                tops = top8s.rearrange("p (g e) -> p g e", g=NG)
                link(v.tensor_tensor(gsum, tops[:, :, 0], tops[:, :, 1], ALU.add))
                this, other = bc(gsum, g3), gsum.unsqueeze(1).to_broadcast(g3)
                pa, pb = (x.rearrange("p (g e) -> p g e", g=NG) for x in (pair_a, pair_b))
                v.tensor_tensor(pa, other, this, ALU.is_gt)
                link(v.tensor_tensor(pb, other, this, ALU.is_equal))
                link(v.tensor_tensor(pb, pb, lt[:, :, :], ALU.mult))
                link(v.tensor_tensor(pa, pa, pb, ALU.add))
                link(v.tensor_reduce(rank, pa, AX.X, ALU.add))
                link(v.tensor_scalar(keep, rank, float(TOPG), None, ALU.is_lt))
                link(v.tensor_scalar(pen, keep, BIG, -BIG, ALU.mult, ALU.add))
                s3 = sel.rearrange("p (g e) -> p g e", g=NG)
                link(v.tensor_tensor(s3, s3, bc(keep, g3), ALU.mult))
                link(v.tensor_tensor(s3, s3, bc(pen, g3), ALU.add))
                v.memset(scrap[:, :], 0.0)
                link(v.max(t8, sel))
                th = t8[:, TOPK - 1:TOPK]
                link(v.tensor_scalar(pair_a, sel, th, None, ALU.is_gt))
                link(v.tensor_reduce(ngt, pair_a, AX.X, ALU.add))
                v.tensor_scalar(need, ngt, -1.0, float(TOPK), ALU.mult, ALU.add)
                link(v.tensor_scalar(pair_b, sel, th, None, ALU.is_equal))
                link(v.tensor_tensor_scan(top8s, ones64[:, :], pair_b, 0.0, ALU.mult, ALU.add))
                link(v.scalar_tensor_tensor(pair_b, top8s, need, pair_b, ALU.is_le, ALU.mult))
                link(v.tensor_tensor(pick, pair_a, pair_b, ALU.add))
                v.tensor_tensor(wfull, pick, sc_t, ALU.mult)
                link(v.tensor_tensor_scan(top8s, ones64[:, :], pick, 0.0, ALU.mult, ALU.add))
                link(v.tensor_reduce(wsum, wfull, AX.X, ALU.add))
                link(v.reciprocal(wrec, wsum))
                v.tensor_scalar(wfull, wfull, wrec, 2.5, ALU.mult, ALU.mult)
                link(v.tensor_tensor(top8s, top8s, pick, ALU.mult))
                if isinstance(m, int) and m == TP:
                    v.tensor_copy(mk_all[0:NS, TP, :], top8s[0:NS, :])
                    o6 = w6[:, TP, :]
                else:
                    mt = bass.ds(m, 1)
                    v.tensor_copy(mk_all[:, mt, :].rearrange("p a e -> p (a e)"), top8s)
                    o6 = w6[:, mt, :].rearrange("p a k -> p (a k)")
                six = [P, TOPK, NE]
                link(v.tensor_tensor(eq_k, top8s.unsqueeze(1).to_broadcast(six), bc(kconst[:, 0:TOPK], six), ALU.is_equal))
                link(v.tensor_tensor(eq_k, eq_k, wfull.unsqueeze(1).to_broadcast(six), ALU.mult))
                v.tensor_reduce(o6, eq_k, AX.X, ALU.add).then_inc(topk_done, 1)
                dve.wait_ge(topk_done, m + 1)

            def body(i, front=True, tail=True, route=True, nxt=True):
                j, m = i - 1, i - 2
                prompt = not (isinstance(j, int) and j == TP)
                h3 = [P, H, HD]
                if route:
                    route_norm(m)
                if tail and prompt:
                    dve.wait_ge(win_ready, j + 1)
                    dve.wait_ge(catA_part, 4 * (j))
                    link(conv(0))
                if front:
                    dve.wait_ge(ua_done, i + 1)
                    dve.wait_ge(sig_ready, i + 1)
                    if isinstance(i, int) and i == TP:
                        dve.wait_ge(glu_last_out, 16)
                    v.tensor_tensor(glu[:, :], U[1][:, :], sig[:, :], ALU.mult).then_inc(glu_ready, 1)
                    dve.wait_ge(glu_ready, i + 1)
                if tail and prompt:
                    link(conv(1))
                if front:
                    dve.wait_ge(uq_done, i + 1)
                    dve.wait_ge(rope_in, 16 * (i + 1))
                    rotate(q_r, 0, q_rot, i)
                if tail and prompt:
                    dve.wait_ge(scores_done, j + 1)
                    v.tensor_tensor(sm[:, :, :], T4, maskT[:, :, :], ALU.mult).then_inc(sm_ready, 1)
                    dve.wait_ge(sm_ready, j + 1)
                    link(conv(2))
                if front:
                    dve.wait_ge(uk_done, i + 1)
                    rotate(k_r, 1, k_rot, i)
                if tail and prompt:
                    conv(3).then_inc(conv_ready, 1)
                    dve.wait_ge(conv_ready, j + 1)
                    v.tensor_copy(win[:, :, 0:CW - 1], win[:, :, P:P + CW - 1]).then_inc(win_shifted, 1)
                    dve.wait_ge(win_shifted, j + 1)
                    dve.wait_ge(ret_done, j + 1)
                    v.tensor_tensor(o_t[:, :, :], cross, bc(q_dec, h3), ALU.mult)
                    for h in range(H):
                        ins = v.scalar_tensor_tensor(S[:, h, :], S[:, h, :], float(GAMMA[h] ** P), R24[:, h, :], ALU.mult, ALU.add)
                    link(ins)
                    ins = v.tensor_tensor(o_t[:, :, :], o_t[:, :, :], inner, ALU.add)
                    ins.then_inc(S_ready, 1)
                    dve.wait_ge(S_ready, j + 1)
                if tail and not prompt:
                    link(v.tensor_tensor(qk_prod, q_r[:, :].rearrange("p (h d) -> p h d", h=H),
                                         k_r[:, :].rearrange("p (h d) -> p h d", h=H), ALU.mult))
                    link(v.tensor_reduce(qk, qk_prod, AX.X, ALU.add))
                    link(v.tensor_scalar(qk, qk, HD ** -0.5, None, ALU.mult))
                    dve.wait_ge(v_ready, NT)
                    vh = v_t[0:NS, :].rearrange("p (h d) -> p h d", h=H)
                    for b in range(NS):
                        ins = v.tensor_scalar(vmask[:, b, :], v_t[0:NS, :], ident[0:NS, b:b + 1], None, ALU.mult)
                    ins.then_inc(vmask_ready, 1)
                    dve.wait_ge(vmask_ready, 1)
                    n3 = [NS, H, HD]
                    link(v.tensor_tensor(qk_prod[0:NS], vh, bc(qk[0:NS, :], n3), ALU.mult))
                    dve.wait_ge(cross_posed, 1)
                    link(v.tensor_tensor(o_t[0:NS], cross[0:NS], bc(s_dec[0:NS, :], n3), ALU.mult))
                    v.tensor_tensor(o_t[0:NS], o_t[0:NS], qk_prod[0:NS], ALU.add).then_inc(sret_ready, 1)
                    dve.wait_ge(sret_ready, 1)
                    for n in range(2 * H):
                        h, half = n // 2, n % 2
                        dve.wait_ge(state_mm, n + 1)
                        sl = S0[:, 4 * half:4 * half + 4, h, :]
                        v.scalar_tensor_tensor(sl, sl, float(GAMMA[h]), U[n % 2][:, :].rearrange("p (b e) -> p b e", b=4),
                                               ALU.mult, ALU.add).then_inc(state_upd, 1)
                        dve.wait_ge(state_upd, n + 1)
                    dve.wait_ge(cs_half, 2 * (CT))
                    dve.wait_ge(win_ready, NT)
                    dve.wait_ge(catA_part, 4 * (j))
                    link(v.tensor_copy(cbuf[:, :, :, CW - 1], win[:, :, CW - 1:CW - 1 + NS]))
                    for c in range(CT):
                        link(v.tensor_tensor(cprod, cbuf[:, c], cw[:, c, :].unsqueeze(1).to_broadcast([P, NS, CW]), ALU.mult))
                        link(v.tensor_reduce(cv[:, c, 0:NS], cprod, AX.X, ALU.add))
                        ins = v.tensor_scalar(cv[:, c, 0:NS], cv[:, c, 0:NS], cvec[:, c:c + 1], None, ALU.add)
                        if c < CT - 1:
                            link(ins)
                    ins.then_inc(conv_ready, 1)
                    dve.wait_ge(conv_ready, j + 1)
                    dve.wait_ge(sret_ready, 1)
                if tail:
                    for h in range(H):
                        ins = v.bn_stats(bn[:, h, :], o_t[:, h, :])
                    link(ins)
                    v.memset(scrap[:, :], 0.0)
                    for h in range(H):
                        ins = v.bn_aggr(mv[:, h, :], bn[:, h, :])
                    ins.then_inc(gn_var, 1)
                    dve.wait_ge(gn_var, j + 1)
                    dve.wait_ge(gn_std, j + 1)
                    link(v.reciprocal(gstd[:, :], gstd[:, :]))
                    for h in range(H):
                        ins = v.tensor_scalar(o_t[:, h, :], o_t[:, h, :], mv[:, h, 0:1], gstd[:, h:h + 1], ALU.subtract, ALU.mult)
                    ins.then_inc(gn_ready, 1)
                    dve.wait_ge(gn_ready, j + 1)
                if route:
                    top_k(m)
                if tail:
                    c3 = [P, CT, P]
                    dve.wait_ge(sum1_done, j + 1)
                    v.tensor_tensor(cv[:, :, :], cv[:, :, :], T0[:, 0:P].unsqueeze(1).to_broadcast(c3),
                                    ALU.subtract).then_inc(cen_ready, 1)
                    dve.wait_ge(cen_ready, j + 1)
                if front:
                    v.tensor_tensor(k_d[:, :].rearrange("p (h d) -> p h d", h=H), k_r[:, :].rearrange("p (h d) -> p h d", h=H),
                                    bc(k_dec, h3), ALU.mult).then_inc(kd_ready, 1)
                    dve.wait_ge(kd_ready, i + 1)
                if tail:
                    dve.wait_ge(std_c, j + 1)
                    link(v.reciprocal(T0[:, P:2 * P], T0[:, P:2 * P]))
                    dve.wait_ge(sq_ready, j + 1)
                    v.tensor_tensor(cv[:, :, :], cv[:, :, :], T0[:, P:2 * P].unsqueeze(1).to_broadcast(c3),
                                    ALU.mult).then_inc(cnorm_ready, 1)
                    dve.wait_ge(cnorm_ready, j + 1)
                if nxt:
                    norm1(i + 1)

            body(0, tail=False, route=False)
            body(1, route=False)
            before = own.base + own.k
            with dve.Fori(2, TP - 1) as i:
                own.at((i - 2) * DVE_LOOP + before)
                body(i)
                assert own.k == DVE_LOOP, own.k
            own.at(before + DVE_LOOP * (TP - 3))
            body(TP - 1)
            body(TP, nxt=False)
            body(TP + 1, front=False, nxt=False)
            body(TP + 2, front=False, tail=False, nxt=False)

            dve.wait_ge(topk_done, NT)
            dve.wait_ge(tri_in, 32)
            dve.wait_ge(q_posed, NT)
            link(v.tensor_copy(tri_bf[:, :], tri_f))
            v.tensor_scalar(pairs, mk_all[:, :, :], 0.0, None, ALU.is_gt).then_inc(pairs_ready, 1)
            dve.wait_ge(pairs_ready, 1)
            dve.wait_ge(pos_done, 1)
            link(v.tensor_scalar(cnt_f, count, float(P - 1), None, ALU.add))
            link(v.tensor_copy(cnt_i, cnt_f))
            link(v.tensor_scalar(cnt_i, cnt_i, 7, None, ALU.arith_shift_right))
            link(v.tensor_copy(nblk, cnt_i))
            link(v.tensor_tensor_scan(pend, ones64[:, :], nblk, 0.0, ALU.mult, ALU.add))
            link(v.tensor_tensor(pbase, pend, nblk, ALU.subtract))
            link(v.tensor_scalar(pbase, pbase, float(P), None, ALU.mult))
            link(v.tensor_copy(pend_i[:, 0:NE], pend[0:1, :]))
            link(v.tensor_scalar(pend_i[:, NE:], pend[0:1, NE - 1:NE], -1.0, None, ALU.add))
            link(v.tensor_scalar(blk_cmp, pend, blk_no[:, 0:1], None, ALU.is_le))
            link(v.tensor_reduce(blk_f, blk_cmp, AX.X, ALU.add))
            v.tensor_scalar(blk_f, blk_f, float(NE - 1), None, ALU.min).then_inc(blk_ready, 1)
            dve.wait_ge(blk_ready, 1)

            def slots(i):
                it = bass.ds(i, 1)
                pos = pos_last if isinstance(i, int) and i == TP else U[0][:, bass.ds(i * NE, NE)]
                six = [P, TOPK, NE]
                v.tensor_tensor(eq_k, mk_all[:, it, :].to_broadcast(six), bc(kconst[:, 0:TOPK], six), ALU.is_equal)
                link(v.tensor_tensor(dest, pos, pbase, ALU.add))
                link(v.tensor_tensor(eq_k, eq_k, dest.unsqueeze(1).to_broadcast(six), ALU.mult))
                link(v.tensor_reduce(dst_f[:, 0:TOPK], eq_k, AX.X, ALU.add))
                v.tensor_copy(dst_i[:, it, 0:TOPK].rearrange("p a k -> p (a k)"), dst_f[:, 0:TOPK]).then_inc(dest_ready, 1)
                dve.wait_ge(dest_ready, i + 1)

            def blk_hid(n):
                dve.wait_ge(silu_ready, n + 1)
                v.tensor_tensor(hid, U[1][:, DE:2 * DE], hsil, ALU.mult).then_inc(hid_ready, 1)

            def blk_hidT(n):
                dve.wait_ge(hid_posed, n + 1)
                v.tensor_copy(hidT, T0[:, 0:DE].rearrange("p (f n) -> p f n", f=FT)).then_inc(hidT_ready, 1)

            def blk_y(n, stored, k):
                dve.wait_ge(y_done, n + 1)
                dve.wait_ge(stored, k)
                v.tensor_copy(y_sb[:, :], R[:, :]).then_inc(y_evac, 1)

            dve.wait_ge(h2_stored, 16 * NT)
            slots(0)
            blk_hid(0)
            blk_hidT(0)
            def shared(n):
                slots(n)
                blk_hid(n)
                blk_y(n - 1, ysh_stored, 16 * n - 16)
                blk_hidT(n)

            shared(1)
            before = own.base + own.k
            with dve.Fori(2, NT - 1) as n:
                own.at((n - 2) * 3 + before)
                shared(n)
                assert own.k == 3
            own.at(before + 3 * (NT - 3))
            slots(TP)
            blk_hid(NT - 1)
            blk_y(NT - 2, ysh_stored, 16 * (NT - 2))
            blk_hidT(NT - 1)
            blk_y(NT - 1, ysh_stored, 16 * (NT - 1))
            dve.wait_ge(slot_posed, 1)
            dve.wait_ge(blkrow_posed, 1)
            link(v.tensor_copy(slot_i, U[0][:, 0:P]))
            v.tensor_scalar(tok_i, slot_i, 3, None, ALU.arith_shift_right).then_inc(slot_ready, 1)
            dve.wait_ge(slot_ready, 1)
            v.tensor_copy(blk_e, U[0][0:1, P:2 * P]).then_inc(blkrow_ready, 1)
            dve.wait_ge(blkrow_ready, 1)

            dve.wait_ge(blkrow_ready, 1)
            last = dve.value_load(pend_i[0:1, NE:], min_val=MINBLK - 1, max_val=MAXBLK - 1)
            dve.wait_ge(ysh_stored, 16 * NT)
            def routed(b):
                blk_hid(b + NT)
                blk_y(b + NT - 1, scattered, 16 * b - 16)
                blk_hidT(b + NT)

            blk_hid(NT)
            blk_hidT(NT)
            routed(1)
            with dve.Fori(2, MAXBLK) as b:
                with dve.If(b <= last):
                    routed(b)
            blk_y(last + NT, scattered, 16 * last)

            def combine(i, r, g, rows=P):
                it = bass.ds(i, 1)
                dve.wait_ge(rows_in[r], 32 * (g + 1))
                acc = yk[r][0:rows, 6, :]
                for k in range(TOPK):
                    link(v.scalar_tensor_tensor(acc, yk[r][0:rows, k, :], w6[0:rows, it, k:k + 1].rearrange("p a k -> p (a k)"),
                                                acc, ALU.mult, ALU.add))
                link(v.tensor_tensor(acc, acc, gt_f[0:rows, :], ALU.mult))
                v.tensor_tensor(xg[0:rows, :], acc, x2f[r][0:rows], ALU.add).then_inc(x3_ready, 1)
                dve.wait_ge(x3_ready, i + 1)
                dve.wait_ge(fin_std, i + 1)
                link(v.reciprocal(rstd1[0:rows, :], std1[0:rows, :]))
                dve.wait_ge(fin_stored[r], 16 * g)
                v.scalar_tensor_tensor(fin[r][0:rows], xg[0:rows, :], rstd1[0:rows, :], g_fin[0:rows, :],
                                       ALU.mult, ALU.mult).then_inc(fin_ready[r], 1)
                dve.wait_ge(fin_ready[r], g + 1)

            dve.wait_ge(finv_in, 32)
            for r in range(2):
                combine(r, r, 0)
            before = own.base + own.k
            with dve.Fori(1, TP // 2) as g:
                own.at((g - 1) * 16 + before)
                for r in range(2):
                    combine(2 * g + r, r, g)
                assert own.k == 16
            own.at(before + 16 * (TP // 2 - 1))
            dve.wait_ge(finv_in, 48)
            combine(TP, 0, TP // 2, NS)

        @block.gpsimd
        def _(pool):
            g = nc.gpsimd
            own = Steps(pool, pool_step)

            def shift(i):
                pool.wait_ge(h_scaled, i + 1)
                g.tensor_tensor(x_t[:, :], x_t[:, :], B_m, ALU.add).then_inc(h_ready, 1)

            def ret_out(j):
                o = o_t[:, :, :].rearrange("p h e -> p (h e)")
                pool.wait_ge(gn_ready, j + 1)
                own.link(g.tensor_tensor(o, o, gret[:, 0, :], ALU.mult))
                own.link(g.tensor_tensor(o, o, gret[:, 1, :], ALU.add))
                pool.wait_ge(sg_ready, j + 1)
                g.tensor_tensor(o, o, sg[:, :], ALU.mult).then_inc(ret_ready, 1)

            shift(0)
            shift(1)
            ret_out(0)
            shift(2)
            with pool.Fori(2, TP) as i:
                own.at(2 * i - 2)
                ret_out(i - 1)
                shift(i + 1)
            own.at(2 * TP - 2)
            ret_out(TP - 1)
            ret_out(TP)

            pool.wait_ge(cen_ready, NT)
            pool.wait_ge(catA_part, 4 * (NT))
            g.memset(pad_row, float(8 * (ROWS - 1))).then_inc(pad_ready, 1)
            pool.wait_ge(table_filled, 16)
            for i in range(NT):
                pool.wait_ge(dest_ready, i + 1)
                rows = P if i < TP else NS
                for k in range(TOPK):
                    pool.indirect_dma_start(slot_tab, bass.IndirectOffsetOnAxis(ap=dst_i[0:rows, i, k:k + 1], axis=0),
                                            slot_val[0:rows, i, k:k + 1], None, bounds_check=NSLOT - 1,
                                            oob_is_err=False).then_inc(slots_out, 16)

            def gather(b):
                pool.wait_ge(xg_posed, b + NT)
                pool.sem_inc(pool_free, 1)
                pool.indirect_dma_start(xg[:, :], None, h2_rows, bass.IndirectOffsetOnAxis(ap=tok_cur[:, 0:1], axis=0),
                                        bounds_check=ROWS - 1, oob_is_err=False).then_inc(gathered, 16)

            def scatter(b):
                pool.wait_ge(y_evac, b + NT + 1)
                pool.sem_inc(pool_free, 1)
                pool.indirect_dma_start(y_rows, bass.IndirectOffsetOnAxis(ap=slot_cur[:, 0:1], axis=0), y_sb[:, :], None,
                                        bounds_check=8 * TOKENS - 1, oob_is_err=False).then_inc(scattered, 16)

            def pick_tok(b):
                own.link(g.tensor_copy(tok_cur[:, :], tok_i[:, bass.ds(b, 1)]))

            def pick_slot(b):
                own.link(g.tensor_copy(slot_cur[:, :], slot_i[:, bass.ds(b, 1)]))

            pool.wait_ge(slot_ready, 1)
            pool.wait_ge(blkrow_ready, 1)
            last = pool.value_load(pend_i[0:1, NE:], min_val=MINBLK - 1, max_val=MAXBLK - 1)
            before = own.base + own.k
            pick_tok(0)
            gather(0)
            pool.wait_ge(gathered, 16)
            pick_tok(1)
            gather(1)

            def routed(b):
                own.at(b * 2 + before)
                pool.wait_ge(gathered, 16 * b + 16)
                pick_tok(b + 1)
                gather(b + 1)
                pool.wait_ge(scattered, 16 * b - 16)
                pick_slot(b - 1)
                scatter(b - 1)

            routed(1)
            with pool.Fori(2, MAXBLK) as b:
                with pool.If(b <= last):
                    routed(b)
            own.at(last * 2 + 2 + before)
            pool.wait_ge(scattered, 16 * last)
            pick_slot(last)
            scatter(last)


GAMMA = [1.0 - 2.0 ** (-5.0 - h) for h in range(H)]
DVE_LOOP = 156


def constants():
    f = np.float32
    pos = np.concatenate([np.arange(SEQ), np.full(NS, PAST), np.zeros(ROWS - TOKENS)]).astype(f)
    inv = (10000.0 ** (-np.arange(HD // 2) / (HD // 2))).astype(f)
    ang = pos[:, None] * inv[None, :]
    cos, sin = np.cos(ang.astype(np.float64)), np.sin(ang.astype(np.float64))
    i = np.arange(P, dtype=np.float64)
    gam = np.array(GAMMA)
    rel = i[None, :] - i[:, None]
    mask = np.where(rel[:, None, :] >= 0, gam[None, :, None] ** np.maximum(rel, 0)[:, None, :], 0.0) * HD ** -0.5
    rows = np.concatenate([gam[None, :] ** (i[:, None] + 1) * HD ** -0.5, gam[None, :] ** (P - 1 - i[:, None]),
                           np.tile(gam[None, :] * HD ** -0.5, (P, 1))], 1)
    g = np.arange(NG)
    token = np.arange(ROWS).reshape(NT, P).T
    return {
        "ident": np.eye(P), "mean_w": np.full((P, P), 1.0 / DC), "tri": np.triu(np.ones((P, P)), 1), "maskT": mask,
        "rows_c": rows, "lt": np.tile((g[None, :] < g[:, None])[None], (P, 1, 1)), "kconst": np.tile(1.0 + g[None, :], (P, 1)),
        "rope": np.stack([cos, -sin, sin], 1), "slot_val": 8 * token[:, :, None] + g[None, None, :], "blk_no": i[:, None],
    }


OUTS = {
    "y_prompt": (1, SEQ, D), "y_sample": (NS, 1, D), "new_conv_prompt": (1, 1, CW - 1, DC), "new_ret_prompt": (1, 1, H, HD, HD),
    "new_conv_sample": (1, NS, CW - 1, DC), "new_ret_sample": (1, NS, H, HD, HD),
}


def kernel(**inputs):
    import concourse.bacc as bacc
    from concourse.bass_utils import run_bass_kernel_spmd

    nc = bacc.Bacc("TRN2", target_bir_lowering=False, num_devices=1)
    arrays = {name: np.ascontiguousarray(a) for name, a in inputs.items()}
    arrays |= {name: np.ascontiguousarray(a.astype(np.float32)) for name, a in constants().items()}
    t = {name: nc.dram_tensor("in_" + name, a.shape, F32, kind="ExternalInput").ap() for name, a in arrays.items()}
    out = {name: nc.dram_tensor("out_" + name, shape, F32, kind="ExternalOutput").ap() for name, shape in OUTS.items()}
    build(nc, t, out)
    r = run_bass_kernel_spmd(nc, [{"in_" + name: a for name, a in arrays.items()}], core_ids=[0])
    return tuple(r.results[0]["out_" + name] for name in OUTS)
```

```python
import numpy as np
import concourse.bass as bass
import concourse.mybir as mybir
from concourse.alu_op_type import AluOpType as ALU
from contextlib import ExitStack

P = 128
D = 1024
KT = D // P
SEQ, NS = 1024, 8
TP = SEQ // P
NT = TP + 1
ROWS = NT * P
DC, DR, H, HD = 512, 512, 4, 128
CT = DC // P
CW = 31
PAST = 8192
NE, NG, PER, TOPG, TOPK = 64, 8, 8, 4, 6
DE = 256
FT = DE // P
EPS = 1e-6
BIG = 1e30
TOKENS = SEQ + NS
MAXBLK = -(-(TOKENS * TOPK + NE * (P - 1)) // P)
MINBLK = -(-TOKENS * TOPK // P)
MAXPAIR = -(-MAXBLK // 2)
MINPAIR = -(-MINBLK // 2)
NSLOT = P * P
RING = 4
WE = KT * 2 * DE + FT * D
F32, BF16, I32 = mybir.dt.float32, mybir.dt.bfloat16, mybir.dt.int32
ACT = mybir.ActivationFunctionType
AX = mybir.AxisListType
GA, GB, GQ, GK, GV, GG = range(6)




class Steps:

    def __init__(self, eng, sem):
        self.eng, self.sem, self.base, self.k = eng, sem, 0, 0

    def add(self, ins):
        ins.then_inc(self.sem, 1)
        self.k += 1

    def link(self, ins):
        self.add(ins)
        self.eng.wait_ge(self.sem, self.base + self.k)

    def at(self, base):
        self.base, self.k = base, 0


def build(nc, t, out):
    with ExitStack() as ctx:
        def sb(name, shape, dt=F32):
            return ctx.enter_context(nc.sbuf_tensor(name, shape, dt))

        def sem(name):
            return ctx.enter_context(nc.semaphore(name))

        c_in, bada_in, ident_in, csilu, c_posed, cT_ready, ada_done, mod_ready, mod_stored, consts_in, win_in = (
            sem(n) for n in "c_in bada_in ident_in csilu c_posed cT_ready ada_done mod_ready mod_stored consts_in win_in".split())
        wout_in, modv_in, smod1_in, smod2_in, smod3_in, state_zero, x_in, rope_in, xr_in, norm1_ssq, norm1_std = (
            sem(n) for n in "wout_in modv_in smod1_in smod2_in smod3_in state_zero x_in rope_in xr_in norm1_ssq norm1_std".split())
        h_scaled, h_ready, x_posed, hT_ready, ub_done, ua_done, uq_done, uk_done, uv_done, ug_done, sig_ready = (
            sem(n) for n in "h_scaled h_ready x_posed hT_ready ub_done ua_done uq_done uk_done uv_done ug_done sig_ready".split())
        glu_ready, q_rot, k_rot, v_ready, sg_ready, glu_posed, win_ready, q_posed, qT_ready, k_posed, kT_ready = (
            sem(n) for n in "glu_ready q_rot k_rot v_ready sg_ready glu_posed win_ready q_posed qT_ready k_posed kT_ready".split())
        scores_done, sm_ready, kd_ready, ret_done, S_ready, conv_ready, win_shifted, sum1_done, cen_ready = (
            sem(n) for n in "scores_done sm_ready kd_ready ret_done S_ready conv_ready win_shifted sum1_done cen_ready".split())
        sq_ready, sum2_done, std_c, cnorm_ready, catA_part, gn_var, gn_std, gn_ready, ret_ready, ret_posed = (
            sem(n) for n in "sq_ready sum2_done std_c cnorm_ready catA_part gn_var gn_std gn_ready ret_ready ret_posed".split())
        catB_ready, wout_done, y_gated, x2_ready, norm2_ssq, norm2_std, x2_stored, h2_ready, h2_stored, h2_posed = (
            sem(n) for n in "catB_ready wout_done y_gated x2_ready norm2_ssq norm2_std x2_stored h2_ready h2_stored h2_posed".split())
        h2T_ready, router_done, score_ready, topk_done, cvec_in, cvec_posed, cvec_ready, glu_last_out = (
            sem(n) for n in "h2T_ready router_done score_ready topk_done cvec_in cvec_posed cvec_ready glu_last_out".split())
        newconv_out, newret_out, s0_in, sconv_in, cs_posed, cs_half, s_cross_done, crossT_ready, cross_posed = (
            sem(n) for n in "newconv_out newret_out s0_in sconv_in cs_posed cs_half s_cross_done crossT_ready cross_posed".split())
        sret_ready, vmask_ready, state_mm, state_upd, tri_in, pairs_ready, pos_done, pad_ready, table_filled = (
            sem(n) for n in "sret_ready vmask_ready state_mm state_upd tri_in pairs_ready pos_done pad_ready table_filled".split())
        dest_ready, slots_out, slot_in, slot_posed, slot_ready, blk_ready, blkrow_posed, blkrow_ready, shw_in = (
            sem(n) for n in "dest_ready slots_out slot_in slot_posed slot_ready blk_ready blkrow_posed blkrow_ready shw_in".split())
        xg_in, xg_posed, xgT_ready, h_done, silu_ready, hid_ready, hid_posed, hidT_ready, y_done, y_evac = (
            sem(n) for n in "xg_in xg_posed xgT_ready h_done silu_ready hid_ready hid_posed hidT_ready y_done y_evac".split())
        ysh_stored, w_ready, finv_in, x3_ready, fin_ssq, fin_std, dve_step, conv3_ready, pool_step = (
            sem(n) for n in "ysh_stored w_ready finv_in x3_ready fin_ssq fin_std dve_step conv3_ready pool_step".split())
        tok_ready, slot_picked, pool_free, sp_free = (sem(n) for n in "tok_ready slot_picked pool_free sp_free".split())
        ada_in = [sem(f"ada_in{r}") for r in range(3)]
        ring_in = [sem(f"ring_in{r}") for r in range(RING)]
        rows_in, fin_ready, fin_stored = ([sem(f"{n}{r}") for r in range(2)] for n in ("rows_in", "fin_ready", "fin_stored"))
        gathered, scattered = ([sem(f"{n}{r}") for r in range(2)] for n in ("gathered", "scattered"))

        def scratch(name, shape, dt=F32):
            return nc.dram_tensor(name, shape, dt, kind="Internal").ap()

        mod_rows = scratch("mod_rows", (1 + NS, 6 * D))
        x2_rows = scratch("x2_rows", (ROWS, D))
        h2_rows = scratch("h2_rows", (ROWS, D))
        y_rows = scratch("y_rows", (ROWS * 8, D))
        slot_tab = scratch("slot_tab", (NSLOT, 1))

        W = sb("W", [P, KT * 3072 + KT * D])
        ada_w = [W[:, 12288 + 4096 * r:16384 + 4096 * r].rearrange("p (k n) -> p k n", k=KT) for r in range(3)]
        mod_sb = W[0:9, 24576:24576 + 6 * D]
        gains = W[0:9, 24576 + 6 * D:24576 + 8 * D]
        w_in = W[:, 0:KT * 3072].rearrange("p (k n) -> p k n", k=KT)
        w_out = W[:, KT * 3072:KT * 4096].rearrange("p (k n) -> p k n", k=KT)
        S0 = W[:, 12288:16384].rearrange("p (b h e) -> p b h e", b=NS, h=H)
        vmask = W[0:NS, 16384:20480].rearrange("p (b n) -> p b n", b=NS)
        cbuf = W[:, 20480:20480 + CT * NS * CW].rearrange("p (c b w) -> p c b w", c=CT, b=NS)
        cprod = W[:, 21504:21504 + NS * CW].rearrange("p (b w) -> p b w", b=NS)
        crossT = W[:, 21760:21760 + H * NS].rearrange("p (h b) -> p h b", h=H)
        qk = W[:, 21800:21800 + H]
        qk_prod = W[:, 22016:22528].rearrange("p (h d) -> p h d", h=H)
        sconv = W[:, 22528:22528 + 2 * DC].rearrange("p (r n) -> p r n", r=2)
        ring = W[:, 0:RING * WE].rearrange("p (r w) -> p r w", r=RING)
        shw = W[:, RING * WE:RING * WE + WE]
        xg_b, y_sb_b = (W[:, (RING + 1) * WE + D * i:(RING + 1) * WE + D * i + D] for i in range(2))
        yk = [W[:, 7168 * r:7168 * (r + 1)].rearrange("p (k n) -> p k n", k=7) for r in range(2)]
        x2f = [W[:, 14336 + D * r:15360 + D * r] for r in range(2)]
        fin = [W[:, 16384 + D * r:17408 + D * r] for r in range(2)]

        ident = sb("ident", [P, P])
        mean_w = sb("mean_w", [P, P])
        maskT = sb("maskT", [P, H, P])
        rows_c = sb("rows_c", [P, 12])
        q_dec, k_dec, s_dec = rows_c[:, 0:4], rows_c[:, 4:8], rows_c[:, 8:12]
        lt = sb("lt", [P, NG, NG])
        kconst = sb("kconst", [P, 8])
        ones64 = sb("ones64", [P, NE])
        w_rt = sb("w_rt", [P, KT, NE])
        bias_r = sb("bias_r", [P, NE])
        mods = sb("mods", [P, 5, D])
        A_m, B_m, gt_m, A_f, B_f = (mods[:, v, :] for v in range(5))
        gret = sb("gret", [P, 2, DR])
        cvec = sb("cvec", [P, 12])
        cw = sb("cw", [P, CT, CW])
        mk_all = sb("mk_all", [P, NT, NE], BF16)
        w6 = sb("w6", [P, NT, TOPK])

        x_t = sb("x_t", [P, D])
        hT = sb("hT", [P, KT, P])
        sig = sb("sig", [P, DC])
        junk = sig[:, :].bitcast(BF16)
        glu = sb("glu", [P, DC])
        rt2 = sb("rt2", [P, DC])
        q_r = sb("q_r", [P, DR])
        k_r = sb("k_r", [P, DR])
        k_d = sb("k_d", [P, DR])
        v_t = sb("v_t", [P, DR])
        sg = sb("sg", [P, DR])
        win = sb("win", [P, CT, CW - 1 + P])
        qT = sb("qT", [P, H, P])
        kT = sb("kT", [P, H, P])
        sm = sb("sm", [P, H, P])
        S = sb("S", [P, H, HD])
        o_t = sb("o_t", [P, H, HD])
        cv = sb("cv", [P, CT, P])
        cat = sb("cat", [P, KT, P])
        h2T = cat
        xr = sb("xr", [P, D])
        rope = sb("rope", [P, 3, HD // 2])
        bn = sb("bn", [P, H, 6])
        mv = sb("mv", [P, H, 2])
        gstd = sb("gstd", [P, H])
        st = sb("st", [P, 6])
        eps_c = sb("eps_c", [P, 1])
        scrap = sb("scrap", [P, 1])
        prod = sb("prod", [P, P])
        tok_cur = sb("tok_cur", [P, 2], I32)
        slot_cur = sb("slot_cur", [P, 2], I32)
        ssq1, std1, rstd1, ssq2, std2, rstd2 = (st[:, i:i + 1] for i in range(6))
        sq = rt2[:, :].rearrange("p (c n) -> p c n", c=CT)
        cvrow = sm[:, 0, :]
        tk = sm[:, :, :].rearrange("p c n -> p (c n)")
        sc_t, sel, top8s = tk[:, 0:64], tk[:, 64:128], tk[:, 128:192]
        pair_a, pair_b = tk[:, 192:256], tk[:, 256:320]
        gsum, rank, keep, pen, t8 = (tk[:, 320 + 8 * i:328 + 8 * i] for i in range(5))
        ngt, need, wsum, wrec = (tk[:, 360 + i:361 + i] for i in range(4))
        pick, wfull = tk[:, 384:448], tk[:, 448:512]
        eq_k = rt2[:, 0:TOPK * NE].rearrange("p (k e) -> p k e", k=TOPK)
        U = [ctx.enter_context(nc.psum_tensor(f"U{i}", [P, 512], F32)) for i in range(2)]
        X = ctx.enter_context(nc.psum_tensor("X", [P, D], F32))
        T0 = ctx.enter_context(nc.psum_tensor("T0", [P, 512], F32))
        R = ctx.enter_context(nc.psum_tensor("R", [P, D], F32))
        R2 = ctx.enter_context(nc.psum_tensor("R2", [P, 512], F32))
        Xk = X[:, :].rearrange("p (k n) -> p k n", k=KT)
        T4 = T0[:, :].rearrange("p (h n) -> p h n", h=4)
        inner, cross = (R[:, 512 * i:512 * i + 512].rearrange("p (h n) -> p h n", h=H) for i in range(2))
        R24 = R2[:, :].rearrange("p (h n) -> p h n", h=4)
        xg, xgT, y_sb = x_t, hT, xr
        xgs, y_sbs = (xg[:, :], xg_b), (y_sb[:, :], y_sb_b)
        hsil, hid = sig[:, 0:DE], sig[:, DE:2 * DE]
        hidT = glu[:, 0:DE].rearrange("p (f n) -> p f n", f=FT)
        pairs = q_r[:, 0:NT * NE // 2].bitcast(BF16).rearrange("p (t e) -> p t e", t=NT)
        cnt_f, nblk, pend, pbase = (k_r[:, 64 * i:64 * i + 64] for i in range(4))
        cnt_i = k_r[:, 256:320].bitcast(I32)
        dest = k_d[:, 0:NE]
        dst_f = v_t[:, 0:8]
        dst_i = qT[:, 0, 0:NT * 8].bitcast(I32).rearrange("p (t k) -> p t k", t=NT)
        slot_val = qT[:, 3, 0:NT * 8].rearrange("p (t k) -> p t k", t=NT)
        slot_row, pad_row, tri_f = cv[:, 0, :], cv[:, 1, :], cv[:, 2, :]
        tri_bf, ones_bf = (cv[:, 3, 64 * i:64 * i + 64].bitcast(BF16) for i in range(2))
        slot_i = kT[:, 0, :].bitcast(I32)
        tok_i = kT[:, 1, :].bitcast(I32)
        blk_f = st[:, 0:1]
        blk_cmp = o_t[:, 0, 0:NE]
        blk_no = sb("blk_no", [P, 1])
        blk_e = qT[0:1, 1, :].bitcast(I32)
        pend_i = qT[0:1, 2, 0:NE + 1].bitcast(I32)
        pos_last = R2[:, 0:NE]
        count = R2[:, NE:2 * NE]
        gt_f, g_fin = mods[:, 0, :], mods[:, 1, :]
        y_of = y_rows.rearrange("(t p k) d -> t p k d", p=P, k=8)

        BANK = {GB: 0, GA: 1, GV: 0, GQ: 1, GG: 0, GK: 1}

        def floor(n):
            return max(n, 0) if isinstance(n, int) else n

        def bc(ap, shape):
            return ap.unsqueeze(2).to_broadcast(shape)

        def everywhere(row, n=P):
            return row.to_broadcast([n, row.shape[1]])

        block = ctx.enter_context(nc.Block())

        @block.sync
        def _(sp):
            def ada(ch):
                sp.dma_start(ada_w[ch % 3],
                             t["w_ada"][0][:, 512 * ch:512 * ch + 512].rearrange("(k p) n -> p k n", p=P)).then_inc(ada_in[ch % 3], 16)

            sp.dma_start(xr[0:1, :], t["c_prompt"]).then_inc(c_in, 16)
            sp.dma_start(xr[1:9, :], t["c_sample"]).then_inc(c_in, 16)
            sp.dma_start(ident[:, :], t["ident"]).then_inc(ident_in, 16)
            for ch in range(3):
                ada(ch)
            sp.dma_start(mod_sb, everywhere(t["b_ada"][0:1, :], 9)).then_inc(bada_in, 16)
            sp.dma_start(gains[:, 0:D], everywhere(t["g_mix"][0:1, :], 9)).then_inc(bada_in, 16)
            sp.dma_start(gains[:, D:2 * D], everywhere(t["g_ffn"][0:1, :], 9)).then_inc(bada_in, 16)
            sp.dma_start(x_t[:, :], t["x_prompt"][0, 0:P, :]).then_inc(x_in, 16)
            sp.dma_start(rope[:, :, :], t["rope"][0:P]).then_inc(rope_in, 16)
            for ch in range(3, 12):
                sp.wait_ge(ada_done, ch - 2)
                ada(ch)
            for k in range(KT // 2):
                sp.dma_start(w_in[:, k, :], t["w_in"][0][P * k:P * k + P, :]).then_inc(win_in, 16)
            for n, name in enumerate(("conv_b", "conv_norm_g", "conv_norm_b")):
                sp.dma_start(cvrow[4 * n:4 * n + 4, :], t[name][0].rearrange("(c p) -> c p", p=P)).then_inc(cvec_in, 16)
            sp.dma_start(cv[0:CW, :, :], t["conv_w"][0].rearrange("w (c p) -> w c p", p=P)).then_inc(cvec_in, 16)
            for o, n in ((mean_w, "mean_w"), (maskT, "maskT"), (rows_c, "rows_c"), (lt, "lt"), (kconst, "kconst"),
                         (blk_no, "blk_no")):
                sp.dma_start(o[:], t[n]).then_inc(consts_in, 16)
            sp.dma_start(w_rt[:, :, :], t["w_router"][0].rearrange("(k p) n -> p k n", p=P)).then_inc(consts_in, 16)
            sp.dma_start(bias_r[:, :], everywhere(t["router_bias"][0:1, :])).then_inc(consts_in, 16)
            sp.dma_start(gret[:, 0, :], everywhere(t["ret_norm_g"][0:1, :])).then_inc(consts_in, 16)
            sp.dma_start(gret[:, 1, :], everywhere(t["ret_norm_b"][0:1, :])).then_inc(consts_in, 16)
            sp.wait_ge(mod_ready, 12)
            sp.dma_start(mod_rows, mod_sb).then_inc(mod_stored, 16)
            for k in range(KT // 2, KT):
                sp.dma_start(w_in[:, k, :], t["w_in"][0][P * k:P * k + P, :]).then_inc(win_in, 16)
            sp.wait_ge(mod_stored, 16)
            for v, m in enumerate((1, 0, 2, 4, 3)):
                sp.dma_start(mods[:, v, :], everywhere(mod_rows[0:1, D * m:D * m + D])).then_inc(modv_in, 16)
            sp.dma_start(w_out[:, :, :], t["w_out"][0].rearrange("(k p) n -> p k n", p=P)).then_inc(wout_in, 16)

            def load_next(i):
                sp.wait_ge(x_posed, i + 1)
                if isinstance(i, int) and i + 1 == TP:
                    sp.dma_start(x_t[0:NS, :], t["x_sample"][:, 0, :]).then_inc(x_in, 16)
                else:
                    sp.dma_start(x_t[:, :], t["x_prompt"][0][bass.ds((i + 1) * P, P), :]).then_inc(x_in, 16)

            def load_rope(i):
                sp.wait_ge(k_rot, i + 1)
                sp.dma_start(rope[:, :, :], t["rope"][bass.ds((i + 1) * P, P)]).then_inc(rope_in, 16)

            def store_route(m):
                sp.wait_ge(x2_ready, m + 1)
                sp.dma_start(x2_rows[bass.ds(m * P, P), :], xr[:, :]).then_inc(x2_stored, 16)
                sp.wait_ge(h2_ready, m + 1)
                sp.dma_start(h2_rows[bass.ds(m * P, P), :], xr[:, :]).then_inc(h2_stored, 16)

            def load_residual(j):
                if isinstance(j, int) and j == 0:
                    sp.wait_ge(cT_ready, 1)
                else:
                    sp.wait_ge(h2_stored, 16 * j)
                    sp.wait_ge(h2_posed, j)
                if isinstance(j, int) and j == TP:
                    sp.dma_start(xr[0:NS, :], t["x_sample"][:, 0, :]).then_inc(xr_in, 16)
                else:
                    sp.dma_start(xr[:, :], t["x_prompt"][0][bass.ds(j * P, P), :]).then_inc(xr_in, 16)

            load_next(0)
            load_rope(0)
            load_next(1)
            load_residual(0)
            load_rope(1)
            with sp.Fori(2, TP - 1) as i:
                load_next(i)
                store_route(i - 2)
                load_residual(i - 1)
                load_rope(i)
            sp.wait_ge(h_ready, TP)
            sp.dma_start(mods[0:NS, 0, :], mod_rows[1:9, D:2 * D]).then_inc(smod1_in, 16)
            sp.dma_start(mods[0:NS, 1, :], mod_rows[1:9, 0:D]).then_inc(smod1_in, 16)
            load_next(TP - 1)
            store_route(TP - 3)
            load_residual(TP - 2)
            sp.wait_ge(glu_ready, TP)
            sp.dma_start(out["new_conv_prompt"][0, 0], glu[P - CW + 1:P, :]).then_inc(glu_last_out, 16)
            load_rope(TP - 1)
            sp.dma_start(out["new_conv_sample"][0][:, 0:CW - 2, :],
                         t["state_conv"][0][:, 1:CW - 1, :]).then_inc(newconv_out, 16)
            store_route(TP - 2)
            load_residual(TP - 1)
            sp.wait_ge(uk_done, NT)
            for r in range(2):
                sp.dma_start(sconv[0:120, r, :],
                             t["state_conv"][0][4 * r:4 * r + 4].rearrange("b w n -> (b w) n")).then_inc(sconv_in, 16)
            for b in range(NS):
                sp.dma_start(S0[:, b, :, :], t["state_ret"][0][b].rearrange("h d e -> d h e")).then_inc(s0_in, 16)

            def load_expert(e, r):
                o = ring[:, r, 0:KT * 2 * DE].rearrange("p (k x n) -> p k x n", k=KT, x=2)
                one = bass.ds(e, 1)
                sp.dma_start(o[:, :, 0, :],
                             t["w1"][0][one].rearrange("a (k p) n -> p (a k) n", p=P)).then_inc(ring_in[r], 16)
                sp.dma_start(o[:, :, 1, :],
                             t["w3"][0][one].rearrange("a (k p) n -> p (a k) n", p=P)).then_inc(ring_in[r], 16)
                sp.dma_start(ring[:, r, KT * 2 * DE:].rearrange("p (f n) -> p f n", f=FT),
                             t["w2"][0][one].rearrange("a (f p) n -> p (a f) n", p=P)).then_inc(ring_in[r], 16)

            load_expert(0, 0)
            load_expert(1, 1)
            sp.wait_ge(glu_ready, NT)
            sp.dma_start(out["new_conv_sample"][0][:, CW - 2, :], glu[0:NS, :]).then_inc(newconv_out, 16)
            sp.wait_ge(S_ready, TP)
            sp.dma_start(out["new_ret_prompt"][0, 0].rearrange("h d e -> d h e"), S[:, :, :]).then_inc(newret_out, 16)
            sp.wait_ge(y_gated, TP)
            sp.dma_start(mods[0:NS, 2, :], mod_rows[1:9, 2 * D:3 * D]).then_inc(smod2_in, 16)
            store_route(TP - 1)
            sp.dma_start(mods[0:NS, 3, :],
                         mod_rows[1:9, 4 * D:5 * D]).then_inc(smod3_in, 16)
            sp.dma_start(mods[0:NS, 4, :], mod_rows[1:9, 3 * D:4 * D]).then_inc(smod3_in, 16)
            load_residual(TP)
            sp.wait_ge(state_upd, 2 * H)
            for b in range(NS):
                sp.dma_start(out["new_ret_sample"][0, b].rearrange("h d e -> d h e"),
                             S0[:, b, :, :]).then_inc(newret_out, 16)
            sp.wait_ge(newret_out, 16 * (NS + 1))
            sp.wait_ge(wout_done, NT)
            o = shw[:, 0:KT * 2 * DE].rearrange("p (k x n) -> p k x n", k=KT, x=2)
            sp.dma_start(o[:, :, 0, :], t["ws1"][0].rearrange("(k p) n -> p k n", p=P)).then_inc(shw_in, 16)
            sp.dma_start(o[:, :, 1, :], t["ws3"][0].rearrange("(k p) n -> p k n", p=P)).then_inc(shw_in, 16)
            sp.dma_start(shw[:, KT * 2 * DE:].rearrange("p (f n) -> p f n", f=FT),
                         t["ws2"][0].rearrange("(f p) n -> p f n", p=P)).then_inc(shw_in, 16)
            store_route(TP)
            sp.wait_ge(h2_stored, 16 * NT)
            sp.dma_start(tri_f, t["tri"]).then_inc(tri_in, 16)
            sp.dma_start(slot_val, t["slot_val"]).then_inc(tri_in, 16)
            sp.wait_ge(pad_ready, 1)
            sp.dma_start(slot_tab.rearrange("(b r) a -> b (r a)", r=P), pad_row).then_inc(table_filled, 16)
            sp.dma_start(xg[:, :], h2_rows[0:P, :]).then_inc(xg_in, 16)
            load_expert(2, 2)
            load_expert(3, 3)

            def load_rows(n):
                sp.wait_ge(xg_posed, n)
                sp.dma_start(xg[:, :], h2_rows[bass.ds(n * P, P), :]).then_inc(xg_in, 16)

            def store_shared(n):
                sp.wait_ge(y_evac, n + 1)
                sp.dma_start(y_of[bass.ds(n, 1), :, 6, :].rearrange("a p d -> (a p) d"), y_sb[:, :]).then_inc(ysh_stored, 16)

            load_rows(1)
            with sp.Fori(1, NT - 1) as n:
                load_rows(n + 1)
                store_shared(n - 1)
            store_shared(NT - 2)
            store_shared(NT - 1)
            sp.wait_ge(slots_out, 16 * NT * TOPK)
            sp.dma_start(slot_row, slot_tab.rearrange("(b r) a -> b (r a)", r=P)).then_inc(slot_in, 16)
            for r in range(RING - 1):
                sp.wait_ge(ring_in[r], 48)
                sp.sem_inc(w_ready, 1)
            sp.wait_ge(blkrow_ready, 1)
            with sp.Fori(1, NE // RING) as g:
                for r in range(RING):
                    before = sp.value_load(pend_i[0:1, bass.ds((g - 1) * RING + r, 1)], min_val=0, max_val=MAXBLK)
                    sp.wait_ge(y_done, before + NT)
                    load_expert(g * RING + r, r)
                    sp.wait_ge(ring_in[(r - 1) % RING], 48 * g if r == 0 else 48 * g + 48)
                    sp.sem_inc(w_ready, 1)
            sp.wait_ge(ring_in[RING - 1], 48 * (NE // RING))
            sp.sem_inc(w_ready, 1)
            last = sp.value_load(pend_i[0:1, NE:], min_val=MINPAIR - 1, max_val=MAXPAIR - 1)
            sp.dma_start(gt_f, everywhere(mod_rows[0:1, 5 * D:6 * D])).then_inc(finv_in, 16)
            sp.dma_start(g_fin, everywhere(t["g_final"].rearrange("(a n) -> a n", a=1))).then_inc(finv_in, 16)
            sp.wait_ge(ysh_stored, 16 * NT)
            sp.wait_ge(x2_stored, 16 * NT)
            for r in range(2):
                sp.wait_ge(scattered[r], 16 * last + 16)
                sp.sem_inc(sp_free, 1)
                sp.wait_ge(gathered[r], 16 * last + 32)
                sp.sem_inc(sp_free, 1)

            def load_tile(i, r, rows=P):
                sp.dma_start(yk[r][0:rows],
                             y_of[bass.ds(i, 1), 0:rows, 0:7, :].rearrange("a p k d -> (a p) k d")).then_inc(rows_in[r], 16)
                sp.dma_start(x2f[r][0:rows], x2_rows[bass.ds(i * P, rows), :]).then_inc(rows_in[r], 16)

            load_tile(0, 0)
            load_tile(1, 1)

            def store_result(g, r):
                sp.wait_ge(fin_ready[r], g + 1)
                sp.dma_start(out["y_prompt"][0][bass.ds((2 * g + r) * P, P), :], fin[r]).then_inc(fin_stored[r], 16)

            with sp.Fori(0, TP // 2 - 1) as g:
                for r in range(2):
                    store_result(g, r)
                    load_tile(2 * g + r + 2, r)
            for r in range(2):
                store_result(TP // 2 - 1, r)
            sp.dma_start(gt_f[0:NS, :], mod_rows[1:9, 5 * D:6 * D]).then_inc(finv_in, 16)
            load_tile(TP, 0, NS)
            sp.wait_ge(fin_ready[0], TP // 2 + 1)
            sp.dma_start(out["y_sample"][:, 0, :], fin[0][0:NS, :]).then_inc(fin_stored[0], 16)
            sp.wait_ge(fin_stored[0], 16 * (TP // 2 + 1))
            sp.wait_ge(fin_stored[1], 16 * (TP // 2))
            sp.wait_ge(glu_last_out, 16)
            sp.wait_ge(newconv_out, 32)

        @block.tensor
        def _(pe):
            mm, tr = nc.tensor.matmul, nc.tensor.transpose

            pe.wait_ge(csilu, 1)
            pe.wait_ge(ident_in, 16)
            for k in range(KT):
                last = tr(X[:, 16 * k:16 * k + 9], xr[0:9, P * k:P * k + P], ident[0:9, 0:9])
            last.then_inc(c_posed, 1)
            pe.wait_ge(cT_ready, 1)
            for ch in range(12):
                pe.wait_ge(ada_in[ch % 3], 16 * (ch // 3 + 1))
                pe.wait_ge(mod_ready, floor(ch - 1))
                for k in range(KT):
                    last = mm(U[ch % 2][0:9, :], hT[:, k, 0:9], ada_w[ch % 3][:, k, :], start=k == 0, stop=k == KT - 1)
                last.then_inc(ada_done, 1)
            pe.wait_ge(cvec_in, 64)
            for c in range(CT):
                tr(T0[:, 32 * c:32 * c + CW], cv[0:CW, c, :], ident[0:CW, 0:CW])
            tr(T0[:, P:P + 12], cvrow[0:12, :], ident[0:12, 0:12]).then_inc(cvec_posed, 1)

            def x_trans(i):
                pe.wait_ge(h_ready, i + 1)
                pe.wait_ge(h2T_ready, floor(i - 2))
                for k in range(KT):
                    last = tr(Xk[:, k, :], x_t[:, P * k:P * k + P], ident[:, :])
                last.then_inc(x_posed, 1)

            def project(i, g, done, free, n):
                pe.wait_ge(free, n)
                for k in range(KT):
                    last = mm(U[BANK[g]][:, :], hT[:, k, :], w_in[:, k, 512 * g:512 * g + 512], start=k == 0, stop=k == KT - 1)
                last.then_inc(done, 1)

            def four(src, done, free, n, ready, m, bank=T4):
                pe.wait_ge(ready, m)
                pe.wait_ge(free, n)
                for c in range(4):
                    last = tr(bank[:, c, :], src[:, P * c:P * c + P], ident[:, :])
                last.then_inc(done, 1)

            def norm_sum(src, done, ready, n):
                pe.wait_ge(ready, n)
                for c in range(CT):
                    last = mm(T0[:, 0:P], mean_w[:, :], src[:, c, :], start=c == 0, stop=c == CT - 1)
                last.then_inc(done, 1)

            def body(i, front=True, tail=True, route=True, nxt=True):
                j, m = i - 1, i - 2
                prompt = not (isinstance(j, int) and j == TP)
                if tail:
                    four(q_r, q_posed, win_ready, j + 1, q_rot, j + 1)
                if front:
                    pe.wait_ge(hT_ready, i + 1)
                    project(i, GB, ub_done, sg_ready, i)
                if tail:
                    four(k_r, k_posed, qT_ready, j + 1, k_rot, j + 1)
                if front:
                    project(i, GA, ua_done, k_rot, i)
                if tail and prompt:
                    pe.wait_ge(kT_ready, j + 1)
                    for h in range(H):
                        last = mm(T4[:, h, :], kT[:, h, :], qT[:, h, :], start=True, stop=True)
                    last.then_inc(scores_done, 1)
                if front:
                    project(i, GV, uv_done, sig_ready, i + 1)
                if tail and prompt:
                    pe.wait_ge(sm_ready, j + 1)
                    pe.wait_ge(v_ready, j + 1)
                    pe.wait_ge(S_ready, j)
                    pe.wait_ge(y_gated, j)
                    pe.wait_ge(x2_ready, j)
                    pe.wait_ge(h2_ready, j)
                    for h in range(H):
                        mm(inner[:, h, :], sm[:, h, :], v_t[:, P * h:P * h + P], start=True, stop=True)
                        mm(cross[:, h, :], qT[:, h, :], S[:, h, :], start=True, stop=True)
                    pe.wait_ge(kd_ready, j + 1)
                    pe.wait_ge(catB_ready, j)
                    for h in range(H):
                        last = mm(R24[:, h, :], k_d[:, P * h:P * h + P], v_t[:, P * h:P * h + P], start=True, stop=True)
                    last.then_inc(ret_done, 1)
                if tail and not prompt:
                    pe.wait_ge(kT_ready, j + 1)
                    pe.wait_ge(s0_in, 16 * NS)
                    pe.wait_ge(h2_ready, j)
                    for h in range(H):
                        for b in range(NS):
                            last = mm(R[:, h * NS + b:h * NS + b + 1], S0[:, b, h, :], qT[:, h, b:b + 1], start=True, stop=True)
                    last.then_inc(s_cross_done, 1)
                    pe.wait_ge(crossT_ready, 1)
                    for h in range(H):
                        last = tr(cross[0:NS, h, :], crossT[:, h, :], ident[:, :])
                    last.then_inc(cross_posed, 1)
                    pe.wait_ge(vmask_ready, 1)
                    for n in range(2 * H):
                        h, half = n // 2, n % 2
                        pe.wait_ge(state_upd, floor(n - 1))
                        if n == 0:
                            pe.wait_ge(v_ready, NT)
                            pe.wait_ge(sg_ready, NT)
                        mm(U[n % 2][:, :], k_r[0:NS, P * h:P * h + P], vmask[:, 4 * half:4 * half + 4, P * h:P * h + P],
                           start=True, stop=True).then_inc(state_mm, 1)
                    pe.wait_ge(kT_ready, NT)
                    pe.wait_ge(sconv_in, 32)
                    for c in range(CT):
                        pe.wait_ge(cs_half, 2 * (c))
                        for r in range(2):
                            last = tr(T0[:, 128 * r:128 * r + 120], sconv[0:120, r, P * c:P * c + P], ident[0:120, 0:120])
                        last.then_inc(cs_posed, 1)
                    pe.wait_ge(cs_half, 2 * (CT))
                if front:
                    project(i, GQ, uq_done, glu_ready, i + 1)
                if route:
                    pe.wait_ge(h2_ready, m + 1)
                    pe.wait_ge(hT_ready, min(i + 1, NT) if isinstance(i, int) else i + 1)
                    for k in range(KT):
                        last = tr(Xk[:, k, :], xr[:, P * k:P * k + P], ident[:, :])
                    last.then_inc(h2_posed, 1)
                if tail:
                    pe.wait_ge(conv3_ready, j + 1)
                    pe.wait_ge(sm_ready, min(j + 1, TP) if isinstance(j, int) else j + 1)
                    norm_sum(cv, sum1_done, conv_ready, j + 1)
                if front:
                    project(i, GG, ug_done, v_ready, i + 1)
                if route:
                    pe.wait_ge(h2T_ready, m + 1)
                    pe.wait_ge(S_ready, min(i, TP) if isinstance(i, int) else i)
                    for k in range(KT):
                        last = mm(R2[:, 0:NE], h2T[:, k, :], w_rt[:, k, :], start=k == 0, stop=k == KT - 1)
                    last.then_inc(router_done, 1)
                if tail:
                    pe.wait_ge(cen_ready, j + 1)
                    norm_sum(sq, sum2_done, sq_ready, j + 1)
                if front:
                    project(i, GK, uk_done, q_rot, i + 1)
                if nxt:
                    x_trans(i + 1)
                if front:
                    four(glu, glu_posed, cnorm_ready, i, glu_ready, i + 1)
                if tail:
                    four(o_t[:, :, :].rearrange("p h e -> p (h e)"), ret_posed, score_ready, j, ret_ready, j + 1, R24)
                    pe.wait_ge(catA_part, 4 * (j + 1))
                    pe.wait_ge(catB_ready, j + 1)
                    for n in range(2):
                        for k in range(KT):
                            last = mm(R[:, 512 * n:512 * n + 512], cat[:, k, :], w_out[:, k, 512 * n:512 * n + 512],
                                      start=k == 0, stop=k == KT - 1)
                    last.then_inc(wout_done, 1)

            x_trans(0)
            pe.wait_ge(win_in, 16 * KT)
            pe.wait_ge(cvec_ready, 1)
            body(0, tail=False, route=False)
            pe.wait_ge(consts_in, 16 * 10)
            pe.wait_ge(wout_in, 16)
            pe.wait_ge(state_zero, 1)
            body(1, route=False)
            with pe.Fori(2, TP) as i:
                body(i)
            body(TP, nxt=False)
            body(TP + 1, front=False, nxt=False)
            body(TP + 2, front=False, tail=False, nxt=False)

            pe.wait_ge(pairs_ready, 1)
            pe.wait_ge(score_ready, NT)
            for i in range(NT):
                o = U[0][:, NE * i:NE * i + NE] if i < TP else pos_last
                for j in range(i):
                    mm(o, ones_bf, pairs[:, j, :], start=j == 0, stop=False)
                mm(o, tri_bf, pairs[:, i, :], start=i == 0, stop=True)
            for j in range(NT):
                last = mm(count, ones_bf, pairs[:, j, :], start=j == 0, stop=j == NT - 1)
            last.then_inc(pos_done, 1)

            def rows_trans(n, arrived, k, r=0):
                pe.wait_ge(arrived, k)
                pe.wait_ge(xgT_ready, n)
                for c in range(KT):
                    last = tr(Xk[:, c, :], xgs[r][:, P * c:P * c + P], ident[:, :])
                last.then_inc(xg_posed, 1)

            def up(n, weights):
                pe.wait_ge(xgT_ready, n + 1)
                for k in range(KT):
                    last = mm(U[1][:, :], xgT[:, k, :], weights[:, 512 * k:512 * k + 512], start=k == 0, stop=k == KT - 1)
                last.then_inc(h_done, 1)

            def hidden_trans(n):
                pe.wait_ge(hid_ready, n + 1)
                for f in range(FT):
                    last = tr(T0[:, P * f:P * f + P], hid[:, P * f:P * f + P], ident[:, :])
                last.then_inc(hid_posed, 1)

            def down(n, weights):
                pe.wait_ge(hidT_ready, n + 1)
                pe.wait_ge(y_evac, n)
                for half in range(2):
                    for f in range(FT):
                        at = KT * 2 * DE + D * f + 512 * half
                        last = mm(R[:, 512 * half:512 * half + 512], hidT[:, f, :], weights[:, at:at + 512],
                                  start=f == 0, stop=f == FT - 1)
                last.then_inc(y_done, 1)

            pe.wait_ge(shw_in, 48)
            rows_trans(0, xg_in, 16)
            up(0, shw)
            rows_trans(1, xg_in, 32)
            hidden_trans(0)
            def shared(n):
                up(n, shw)
                rows_trans(n + 1, xg_in, 16 * n + 32)
                down(n - 1, shw)
                hidden_trans(n)

            shared(1)
            with pe.Fori(2, NT - 1) as n:
                shared(n)
            up(NT - 1, shw)
            down(NT - 2, shw)
            hidden_trans(NT - 1)
            down(NT - 1, shw)
            pe.wait_ge(dest_ready, NT)
            pe.wait_ge(slot_in, 16)
            tr(U[0][:, 0:P], slot_row, ident[:, :]).then_inc(slot_posed, 1)
            pe.wait_ge(blk_ready, 1)
            mm(U[0][0:1, P:2 * P], blk_f, ident[:, :], start=True, stop=True).then_inc(blkrow_posed, 1)

            def weights_of(b, first=True):
                e = pe.value_load(blk_e[0:1, bass.ds(b, 1)], min_val=0, max_val=NE - 1)
                if first:
                    pe.wait_ge(w_ready, e + 1)
                return ring[:, bass.ds(e % RING, 1), :].rearrange("p a w -> p (a w)")

            pe.wait_ge(blkrow_ready, 1)
            last = pe.value_load(pend_i[0:1, NE:], min_val=MINPAIR - 1, max_val=MAXPAIR - 1)

            def routed(g, r, first=False):
                b = 2 * g + r
                up(b + NT, weights_of(b))
                if r == 0:
                    rows_trans(b + NT + 1, gathered[1], 16 * g + 16, 1)
                else:
                    rows_trans(b + NT + 1, gathered[0], 16 * g + 32, 0)
                if not first:
                    down(b + NT - 1, weights_of(b - 1, False))
                hidden_trans(b + NT)

            rows_trans(NT, gathered[0], 16, 0)
            routed(0, 0, True)
            routed(0, 1)
            with pe.Fori(1, MAXPAIR) as g:
                with pe.If(g <= last):
                    routed(g, 0)
                    routed(g, 1)
            down(2 * last + NT + 1, weights_of(2 * last + 1, False))

        @block.scalar
        def _(act):
            act.wait_ge(c_in, 32)
            nc.scalar.activation(xr[0:9, :], xr[0:9, :], ACT.Silu).then_inc(csilu, 1)
            act.wait_ge(csilu, 1)
            act.wait_ge(c_posed, 1)
            nc.scalar.activation(hT[:, :, 0:9], X[:, 0:16 * KT].rearrange("p (k n) -> p k n", k=KT)[:, :, 0:9],
                                 ACT.Copy).then_inc(cT_ready, 1)
            act.wait_ge(cT_ready, 1)

            def norm1(i):
                act.wait_ge(x_in, 16 * (i + 1))
                act.wait_ge(glu_ready, i)
                nc.scalar.activation(junk, x_t[:, :], ACT.Square, accum_out=ssq1).then_inc(norm1_ssq, 1)
                act.wait_ge(norm1_ssq, i + 1)
                act.wait_ge(norm1_ssq, i + 1)
                act.wait_ge(h_scaled, i)
                nc.scalar.activation(std1, ssq1, ACT.Sqrt, scale=1.0 / D, bias=eps_c[:, 0:1]).then_inc(norm1_std, 1)
                act.wait_ge(norm1_std, i + 1)

            def hT_copy(i):
                act.wait_ge(x_posed, i + 1)
                nc.scalar.activation(hT[:, :, :], Xk, ACT.Copy).then_inc(hT_ready, 1)
                act.wait_ge(hT_ready, i + 1)

            def body(i, front=True, tail=True, route=True, nxt=True):
                j, m = i - 1, i - 2
                if tail:
                    act.wait_ge(q_posed, j + 1)
                    nc.scalar.activation(qT[:, :, :], T4, ACT.Copy).then_inc(qT_ready, 1)
                    act.wait_ge(qT_ready, j + 1)
                if route:
                    act.wait_ge(x2_ready, m + 1)
                    act.wait_ge(glu_ready, min(i, NT) if isinstance(i, int) else i)
                    nc.scalar.activation(junk, xr[:, :], ACT.Square, accum_out=ssq2).then_inc(norm2_ssq, 1)
                    act.wait_ge(norm2_ssq, m + 1)
                    act.wait_ge(norm2_ssq, m + 1)
                    nc.scalar.activation(std2, ssq2, ACT.Sqrt, scale=1.0 / D, bias=eps_c[:, 0:1]).then_inc(norm2_std, 1)
                    act.wait_ge(norm2_std, m + 1)
                if front:
                    act.wait_ge(ub_done, i + 1)
                    nc.scalar.activation(sig[:, :], U[0][:, :], ACT.Sigmoid).then_inc(sig_ready, 1)
                    act.wait_ge(sig_ready, i + 1)
                if tail:
                    act.wait_ge(k_posed, j + 1)
                    nc.scalar.activation(kT[:, :, :], T4, ACT.Copy).then_inc(kT_ready, 1)
                    act.wait_ge(kT_ready, j + 1)
                if front:
                    act.wait_ge(uv_done, i + 1)
                    act.wait_ge(ret_done, i)
                    nc.scalar.activation(v_t[:, :], U[0][:, :], ACT.Copy).then_inc(v_ready, 1)
                    act.wait_ge(v_ready, i + 1)
                if nxt:
                    norm1(i + 1)
                prompt = not (isinstance(j, int) and j == TP)
                if tail and not prompt:
                    act.wait_ge(s_cross_done, 1)
                    nc.scalar.activation(crossT, R[:, 0:H * NS].rearrange("p (h b) -> p h b", h=H),
                                         ACT.Copy).then_inc(crossT_ready, 1)
                    act.wait_ge(crossT_ready, 1)
                    for c in range(CT):
                        act.wait_ge(cs_posed, c + 1)
                        for r in range(2):
                            nc.scalar.activation(cbuf[:, c, 4 * r:4 * r + 4, 0:CW - 1],
                              T0[:, 128 * r:128 * r + 120].rearrange("p (b w) -> p b w", b=4), ACT.Copy).then_inc(
                                  cs_half, 1)
                            act.wait_ge(cs_half, 2 * c + r + 1)
                if tail:
                    act.wait_ge(gn_var, j + 1)
                    nc.scalar.activation(gstd[:, :], mv[:, :, 1], ACT.Sqrt, bias=eps_c[:, 0:1]).then_inc(gn_std, 1)
                    act.wait_ge(gn_std, j + 1)
                if route:
                    act.wait_ge(h2_posed, m + 1)
                    nc.scalar.activation(h2T[:, :, :], Xk, ACT.Copy).then_inc(h2T_ready, 1)
                    act.wait_ge(h2T_ready, m + 1)
                if tail:
                    act.wait_ge(cen_ready, j + 1)
                    nc.scalar.activation(sq, cv[:, :, :], ACT.Square).then_inc(sq_ready, 1)
                    act.wait_ge(sq_ready, j + 1)
                if route:
                    act.wait_ge(router_done, m + 1)
                    nc.scalar.activation(sc_t, R2[:, 0:NE], ACT.Sigmoid).then_inc(score_ready, 1)
                    act.wait_ge(score_ready, m + 1)
                if tail:
                    act.wait_ge(sum2_done, j + 1)
                    nc.scalar.activation(T0[:, P:2 * P], T0[:, 0:P], ACT.Sqrt, bias=eps_c[:, 0:1]).then_inc(std_c, 1)
                    act.wait_ge(std_c, j + 1)
                if front:
                    act.wait_ge(ug_done, i + 1)
                    act.wait_ge(ret_ready, i)
                    nc.scalar.activation(sg[:, :], U[0][:, :], ACT.Silu).then_inc(sg_ready, 1)
                    act.wait_ge(sg_ready, i + 1)
                if tail:
                    act.wait_ge(cnorm_ready, j + 1)
                    act.wait_ge(router_done, m + 1)
                    for c in range(CT):
                        nc.scalar.activation(cat[:, c, :], cv[:, c, :], ACT.Silu, scale=cvec[:, CT + c:CT + c + 1],
                                             bias=cvec[:, 2 * CT + c:2 * CT + c + 1]).then_inc(catA_part, 1)
                        act.wait_ge(catA_part, 4 * j + c + 1)
                if nxt:
                    hT_copy(i + 1)
                if front:
                    act.wait_ge(glu_posed, i + 1)
                    act.wait_ge(win_shifted, i)
                    nc.scalar.activation(win[:, :, CW - 1:], T4, ACT.Copy).then_inc(win_ready, 1)
                    act.wait_ge(win_ready, i + 1)
                if tail:
                    act.wait_ge(ret_posed, j + 1)
                    nc.scalar.activation(cat[:, CT:, :], R24, ACT.Copy).then_inc(catB_ready, 1)
                    act.wait_ge(catB_ready, j + 1)

            act.wait_ge(state_zero, 1)
            norm1(0)
            hT_copy(0)
            body(0, tail=False, route=False)
            body(1, route=False)
            with act.Fori(2, TP) as i:
                body(i)
            body(TP, nxt=False)
            body(TP + 1, front=False, nxt=False)
            body(TP + 2, front=False, tail=False, nxt=False)

            def blk_T(n):
                act.wait_ge(xg_posed, n + 1)
                nc.scalar.activation(xgT[:, :, :], Xk, ACT.Copy).then_inc(xgT_ready, 1)

            def blk_silu(n):
                act.wait_ge(h_done, n + 1)
                act.wait_ge(hid_ready, n)
                nc.scalar.activation(hsil, U[1][:, 0:DE], ACT.Silu).then_inc(silu_ready, 1)

            act.wait_ge(h2_posed, NT)
            blk_T(0)
            blk_silu(0)
            blk_T(1)
            with act.Fori(1, NT - 1) as n:
                blk_silu(n)
                blk_T(n + 1)
            blk_silu(NT - 1)
            blk_T(NT)
            act.wait_ge(blkrow_ready, 1)
            last = act.value_load(pend_i[0:1, NE:], min_val=MINPAIR - 1, max_val=MAXPAIR - 1)
            with act.Fori(0, MAXPAIR) as g:
                with act.If(g <= last):
                    for r in range(2):
                        blk_silu(2 * g + r + NT)
                        blk_T(2 * g + r + NT + 1)

            def last_norm(i, rows=P):
                act.wait_ge(x3_ready, i + 1)
                nc.scalar.activation(junk[0:rows, :], xg[0:rows, :],
                                     ACT.Square, accum_out=ssq1[0:rows, :]).then_inc(fin_ssq, 1)
                act.wait_ge(fin_ssq, i + 1)
                act.wait_ge(fin_ssq, i + 1)
                nc.scalar.activation(std1[0:rows, :], ssq1[0:rows, :],
                                     ACT.Sqrt, scale=1.0 / D, bias=eps_c[0:rows, 0:1]).then_inc(fin_std, 1)
                act.wait_ge(fin_std, i + 1)

            with act.Fori(0, TP) as i:
                last_norm(i)
            last_norm(TP, NS)

        @block.vector
        def _(dve):
            v = nc.vector
            own = Steps(dve, dve_step)
            link = own.link

            link(v.memset(win[:, :, 0:CW - 1], 0.0))
            link(v.memset(ones64[:, :], 1.0))
            link(v.memset(mk_all[:, TP, :], 0.0))
            link(v.memset(eps_c[:, :], EPS))
            v.memset(S[:, :, :], 0.0).then_inc(state_zero, 1)
            dve.wait_ge(state_zero, 1)

            def norm1(i):
                dve.wait_ge(norm1_std, i + 1)
                link(v.reciprocal(rstd1, std1))
                if isinstance(i, int) and i == TP:
                    dve.wait_ge(smod1_in, 32)
                v.scalar_tensor_tensor(x_t[:, :], x_t[:, :], rstd1, A_m, ALU.mult, ALU.mult).then_inc(h_scaled, 1)
                dve.wait_ge(h_scaled, i + 1)

            dve.wait_ge(bada_in, 48)
            for ch in range(12):
                dve.wait_ge(ada_done, ch + 1)
                o = mod_sb[:, 512 * ch:512 * ch + 512]
                ins = v.tensor_tensor(o, U[ch % 2][0:9, :], o, ALU.add)
                if ch // 2 in (1, 4):
                    link(ins)
                    at = D * (ch // 8) + 512 * (ch % 2)
                    ins = v.scalar_tensor_tensor(o, o, 1.0, gains[:, at:at + 512], ALU.add, ALU.mult)
                ins.then_inc(mod_ready, 1)
                dve.wait_ge(mod_ready, ch + 1)
            dve.wait_ge(modv_in, 80)
            norm1(0)
            dve.wait_ge(cvec_posed, 1)
            link(v.tensor_copy(cw[:, :, :], T0[:, 0:P].rearrange("p (c w) -> p c w", c=CT)[:, :, 0:CW]))
            v.tensor_copy(cvec[:, :], T0[:, P:P + 12]).then_inc(cvec_ready, 1)
            dve.wait_ge(cvec_ready, 1)
            dve.wait_ge(consts_in, 16 * 10)

            def rotate(o, bank, done, i):
                u = U[bank][:, :].rearrange("p (g d) -> p g d", d=HD // 2)
                uh = U[bank][:, :].rearrange("p (h z d) -> p h z d", h=H, z=2)
                th = rt2[:, :].rearrange("p (h z d) -> p h z d", h=H, z=2)
                half = [P, H, HD // 2]
                v.tensor_tensor(o[:, :].rearrange("p (g d) -> p g d", d=HD // 2), u,
                                rope[:, 0, :].unsqueeze(1).to_broadcast([P, 2 * H, HD // 2]), ALU.mult)
                v.tensor_tensor(th[:, :, 0, :], uh[:, :, 1, :], rope[:, 1, :].unsqueeze(1).to_broadcast(half), ALU.mult)
                link(v.tensor_tensor(th[:, :, 1, :], uh[:, :, 0, :], rope[:, 2, :].unsqueeze(1).to_broadcast(half), ALU.mult))
                v.tensor_tensor(o[:, :], o[:, :], rt2[:, :], ALU.add).then_inc(done, 1)
                dve.wait_ge(done, i + 1)

            def conv(first, last):
                for w in range(first, last):
                    for c in range(CT - 1):
                        if w == 0:
                            ins = v.tensor_scalar(cv[:, c, :], win[:, c, 0:P], cw[:, c, 0:1], cvec[:, c:c + 1], ALU.mult, ALU.add)
                        else:
                            dve.wait_ge(dve_step, own.base + conv_step[c])
                            ins = v.scalar_tensor_tensor(cv[:, c, :], win[:, c, w:w + P], cw[:, c, w:w + 1], cv[:, c, :],
                                                         ALU.mult, ALU.add)
                        if w < CW - 1:
                            own.add(ins)
                            conv_step[c] = own.k
                return ins

            conv_step = [0] * (CT - 1)

            def residual(m):
                dve.wait_ge(wout_done, m + 1)
                if isinstance(m, int) and m == TP:
                    dve.wait_ge(smod2_in, 16)
                v.tensor_tensor(R[:, :], R[:, :], gt_m, ALU.mult).then_inc(y_gated, 1)
                dve.wait_ge(y_gated, m + 1)
                dve.wait_ge(xr_in, 16 * (m + 1))
                v.tensor_tensor(xr[:, :], R[:, :], xr[:, :], ALU.add).then_inc(x2_ready, 1)
                dve.wait_ge(x2_ready, m + 1)

            def norm2(m):
                dve.wait_ge(norm2_std, m + 1)
                link(v.reciprocal(rstd2, std2))
                if isinstance(m, int) and m == TP:
                    dve.wait_ge(smod3_in, 32)
                link(v.scalar_tensor_tensor(R[:, :], xr[:, :], rstd2, A_f, ALU.mult, ALU.mult))
                dve.wait_ge(x2_stored, 16 * (m + 1))
                v.tensor_tensor(xr[:, :], R[:, :], B_f, ALU.add).then_inc(h2_ready, 1)
                dve.wait_ge(h2_ready, m + 1)

            def top_k(m):
                dve.wait_ge(score_ready, m + 1)
                g3 = [P, NG, PER]
                link(v.tensor_tensor(sel, sc_t, bias_r[:, :], ALU.add))
                v.memset(scrap[:, :], 0.0)
                for g in range(NG):
                    ins = v.max(top8s[:, PER * g:PER * g + PER], sel[:, PER * g:PER * g + PER])
                link(ins)
                tops = top8s.rearrange("p (g e) -> p g e", g=NG)
                link(v.tensor_tensor(gsum, tops[:, :, 0], tops[:, :, 1], ALU.add))
                this, other = bc(gsum, g3), gsum.unsqueeze(1).to_broadcast(g3)
                pa, pb = (x.rearrange("p (g e) -> p g e", g=NG) for x in (pair_a, pair_b))
                v.tensor_tensor(pa, other, this, ALU.is_gt)
                link(v.tensor_tensor(pb, other, this, ALU.is_equal))
                link(v.tensor_tensor(pb, pb, lt[:, :, :], ALU.mult))
                link(v.tensor_tensor(pa, pa, pb, ALU.add))
                link(v.tensor_reduce(rank, pa, AX.X, ALU.add))
                link(v.tensor_scalar(keep, rank, float(TOPG), None, ALU.is_lt))
                link(v.tensor_scalar(pen, keep, BIG, -BIG, ALU.mult, ALU.add))
                s3 = sel.rearrange("p (g e) -> p g e", g=NG)
                link(v.tensor_tensor(s3, s3, bc(keep, g3), ALU.mult))
                link(v.tensor_tensor(s3, s3, bc(pen, g3), ALU.add))
                v.memset(scrap[:, :], 0.0)
                link(v.max(t8, sel))
                th = t8[:, TOPK - 1:TOPK]
                link(v.tensor_scalar(pair_a, sel, th, None, ALU.is_gt))
                link(v.tensor_reduce(ngt, pair_a, AX.X, ALU.add))
                v.tensor_scalar(need, ngt, -1.0, float(TOPK), ALU.mult, ALU.add)
                link(v.tensor_scalar(pair_b, sel, th, None, ALU.is_equal))
                link(v.tensor_tensor_scan(top8s, ones64[:, :], pair_b, 0.0, ALU.mult, ALU.add))
                link(v.scalar_tensor_tensor(pair_b, top8s, need, pair_b, ALU.is_le, ALU.mult))
                link(v.tensor_tensor(pick, pair_a, pair_b, ALU.add))
                v.tensor_tensor(wfull, pick, sc_t, ALU.mult)
                link(v.tensor_tensor_scan(top8s, ones64[:, :], pick, 0.0, ALU.mult, ALU.add))
                link(v.tensor_reduce(wsum, wfull, AX.X, ALU.add))
                link(v.reciprocal(wrec, wsum))
                own.add(v.tensor_scalar(wfull, wfull, wrec, 2.5, ALU.mult, ALU.mult))
                link(v.tensor_tensor(top8s, top8s, pick, ALU.mult))
                if isinstance(m, int) and m == TP:
                    v.tensor_copy(mk_all[0:NS, TP, :], top8s[0:NS, :])
                else:
                    v.tensor_copy(mk_all[:, bass.ds(m, 1), :].rearrange("p a e -> p (a e)"), top8s)

            def weights_by_k(m):
                o6 = w6[:, TP, :] if isinstance(m, int) and m == TP else w6[:, bass.ds(m, 1), :].rearrange("p a k -> p (a k)")
                dve.wait_ge(sum2_done, min(m + 2, NT) if isinstance(m, int) else m + 2)
                six = [P, TOPK, NE]
                link(v.tensor_tensor(eq_k, top8s.unsqueeze(1).to_broadcast(six), bc(kconst[:, 0:TOPK], six), ALU.is_equal))
                link(v.tensor_tensor(eq_k, eq_k, wfull.unsqueeze(1).to_broadcast(six), ALU.mult))
                v.tensor_reduce(o6, eq_k, AX.X, ALU.add).then_inc(topk_done, 1)
                dve.wait_ge(topk_done, m + 1)

            def body(i, front=True, tail=True, route=True, nxt=True):
                j, m = i - 1, i - 2
                prompt = not (isinstance(j, int) and j == TP)
                h3, c3 = [P, H, HD], [P, CT, P]
                if tail and prompt:
                    dve.wait_ge(win_ready, j + 1)
                    dve.wait_ge(catA_part, 4 * j)
                    conv(0, TAPS[0])
                if route:
                    residual(m)
                if tail and prompt:
                    conv(TAPS[0], TAPS[1])
                if route:
                    norm2(m)
                if tail and prompt:
                    conv(TAPS[1], TAPS[2])
                if front:
                    dve.wait_ge(ua_done, i + 1)
                    dve.wait_ge(sig_ready, i + 1)
                    if isinstance(i, int) and i == TP:
                        dve.wait_ge(glu_last_out, 16)
                    v.tensor_tensor(glu[:, :], U[1][:, :], sig[:, :], ALU.mult).then_inc(glu_ready, 1)
                    dve.wait_ge(glu_ready, i + 1)
                if tail and prompt:
                    v.tensor_tensor(k_d[:, :].rearrange("p (h d) -> p h d", h=H), k_r[:, :].rearrange("p (h d) -> p h d", h=H),
                                    bc(k_dec, h3), ALU.mult).then_inc(kd_ready, 1)
                    dve.wait_ge(kd_ready, j + 1)
                    dve.wait_ge(scores_done, j + 1)
                    v.tensor_tensor(sm[:, :, :], T4, maskT[:, :, :], ALU.mult).then_inc(sm_ready, 1)
                    dve.wait_ge(sm_ready, j + 1)
                    conv(TAPS[2], TAPS[3])
                    dve.wait_ge(ret_done, j + 1)
                    v.tensor_tensor(o_t[:, :, :], cross, bc(q_dec, h3), ALU.mult)
                    for h in range(H):
                        ins = v.scalar_tensor_tensor(S[:, h, :], S[:, h, :], float(GAMMA[h] ** P), R24[:, h, :], ALU.mult, ALU.add)
                    link(ins)
                    ins = v.tensor_tensor(o_t[:, :, :], o_t[:, :, :], inner, ALU.add)
                    ins.then_inc(S_ready, 1)
                    dve.wait_ge(S_ready, j + 1)
                if tail and not prompt:
                    link(v.tensor_tensor(qk_prod, q_r[:, :].rearrange("p (h d) -> p h d", h=H),
                                         k_r[:, :].rearrange("p (h d) -> p h d", h=H), ALU.mult))
                    link(v.tensor_reduce(qk, qk_prod, AX.X, ALU.add))
                    link(v.tensor_scalar(qk, qk, HD ** -0.5, None, ALU.mult))
                    dve.wait_ge(v_ready, NT)
                    vh = v_t[0:NS, :].rearrange("p (h d) -> p h d", h=H)
                    for b in range(NS):
                        ins = v.tensor_scalar(vmask[:, b, :], v_t[0:NS, :], ident[0:NS, b:b + 1], None, ALU.mult)
                    ins.then_inc(vmask_ready, 1)
                    dve.wait_ge(vmask_ready, 1)
                    n3 = [NS, H, HD]
                    link(v.tensor_tensor(qk_prod[0:NS], vh, bc(qk[0:NS, :], n3), ALU.mult))
                    dve.wait_ge(cross_posed, 1)
                    link(v.tensor_tensor(o_t[0:NS], cross[0:NS], bc(s_dec[0:NS, :], n3), ALU.mult))
                    v.tensor_tensor(o_t[0:NS], o_t[0:NS], qk_prod[0:NS], ALU.add).then_inc(sret_ready, 1)
                    dve.wait_ge(sret_ready, 1)
                    for n in range(2 * H):
                        h, half = n // 2, n % 2
                        dve.wait_ge(state_mm, n + 1)
                        sl = S0[:, 4 * half:4 * half + 4, h, :]
                        v.scalar_tensor_tensor(sl, sl, float(GAMMA[h]), U[n % 2][:, :].rearrange("p (b e) -> p b e", b=4),
                                               ALU.mult, ALU.add).then_inc(state_upd, 1)
                        dve.wait_ge(state_upd, n + 1)
                    dve.wait_ge(cs_half, 2 * (CT))
                    dve.wait_ge(win_ready, NT)
                    dve.wait_ge(catA_part, 4 * (j))
                    link(v.tensor_copy(cbuf[:, :, :, CW - 1], win[:, :, CW - 1:CW - 1 + NS]))
                    for c in range(CT):
                        link(v.tensor_tensor(cprod, cbuf[:, c], cw[:, c, :].unsqueeze(1).to_broadcast([P, NS, CW]), ALU.mult))
                        link(v.tensor_reduce(cv[:, c, 0:NS], cprod, AX.X, ALU.add))
                        ins = v.tensor_scalar(cv[:, c, 0:NS], cv[:, c, 0:NS], cvec[:, c:c + 1], None, ALU.add)
                        if c < CT - 1:
                            link(ins)
                    ins.then_inc(conv_ready, 1)
                    dve.wait_ge(conv_ready, j + 1)
                    dve.wait_ge(sret_ready, 1)
                if tail:
                    for h in range(H):
                        ins = v.bn_stats(bn[:, h, :], o_t[:, h, :])
                    link(ins)
                    v.memset(scrap[:, :], 0.0)
                    for h in range(H):
                        ins = v.bn_aggr(mv[:, h, :], bn[:, h, :])
                    ins.then_inc(gn_var, 1)
                    dve.wait_ge(gn_var, j + 1)
                if nxt:
                    norm1(i + 1)
                if tail and prompt:
                    conv(TAPS[3], CW).then_inc(conv_ready, 1)
                    dve.wait_ge(conv_ready, j + 1)
                    dve.wait_ge(conv3_ready, j + 1)
                    v.tensor_copy(win[:, :, 0:CW - 1], win[:, :, P:P + CW - 1]).then_inc(win_shifted, 1)
                    dve.wait_ge(win_shifted, j + 1)
                if tail:
                    dve.wait_ge(gn_std, j + 1)
                    link(v.reciprocal(gstd[:, :], gstd[:, :]))
                    for h in range(H):
                        ins = v.tensor_scalar(o_t[:, h, :], o_t[:, h, :], mv[:, h, 0:1], gstd[:, h:h + 1], ALU.subtract, ALU.mult)
                    ins.then_inc(gn_ready, 1)
                    dve.wait_ge(gn_ready, j + 1)
                if front:
                    dve.wait_ge(uq_done, i + 1)
                    dve.wait_ge(rope_in, 16 * (i + 1))
                    rotate(q_r, 1, q_rot, i)
                if tail:
                    dve.wait_ge(sum1_done, j + 1)
                    v.tensor_tensor(cv[:, :, :], cv[:, :, :], T0[:, 0:P].unsqueeze(1).to_broadcast(c3),
                                    ALU.subtract).then_inc(cen_ready, 1)
                    dve.wait_ge(cen_ready, j + 1)
                if tail:
                    dve.wait_ge(std_c, j + 1)
                    link(v.reciprocal(T0[:, P:2 * P], T0[:, P:2 * P]))
                    dve.wait_ge(sq_ready, j + 1)
                    v.tensor_tensor(cv[:, :, :], cv[:, :, :], T0[:, P:2 * P].unsqueeze(1).to_broadcast(c3),
                                    ALU.mult).then_inc(cnorm_ready, 1)
                    dve.wait_ge(cnorm_ready, j + 1)
                if route:
                    top_k(m)
                    weights_by_k(m)
                if front:
                    dve.wait_ge(uk_done, i + 1)
                    rotate(k_r, 1, k_rot, i)

            body(0, tail=False, route=False)
            body(1, route=False)
            before = own.base + own.k
            with dve.Fori(2, TP - 1) as i:
                own.at((i - 2) * DVE_LOOP + before)
                body(i)
                assert own.k == DVE_LOOP, own.k
            own.at(before + DVE_LOOP * (TP - 3))
            body(TP - 1)
            body(TP, nxt=False)
            body(TP + 1, front=False, nxt=False)
            body(TP + 2, front=False, tail=False, nxt=False)

            dve.wait_ge(topk_done, NT)
            dve.wait_ge(tri_in, 32)
            dve.wait_ge(q_posed, NT)
            dve.wait_ge(catA_part, 4 * NT)
            v.memset(ones_bf, 1.0)
            link(v.tensor_copy(tri_bf, tri_f))
            v.tensor_scalar(pairs, mk_all[:, :, :], 0.0, None, ALU.is_gt).then_inc(pairs_ready, 1)
            dve.wait_ge(pairs_ready, 1)
            dve.wait_ge(pos_done, 1)
            link(v.tensor_scalar(cnt_f, count, float(P - 1), None, ALU.add))
            link(v.tensor_copy(cnt_i, cnt_f))
            link(v.tensor_scalar(cnt_i, cnt_i, 7, None, ALU.arith_shift_right))
            link(v.tensor_copy(nblk, cnt_i))
            link(v.tensor_tensor_scan(pend, ones64[:, :], nblk, 0.0, ALU.mult, ALU.add))
            link(v.tensor_tensor(pbase, pend, nblk, ALU.subtract))
            link(v.tensor_scalar(pbase, pbase, float(P), None, ALU.mult))
            link(v.tensor_copy(pend_i[:, 0:NE], pend[0:1, :]))
            link(v.tensor_scalar(pend_i[:, NE:], pend[0:1, NE - 1:NE], -1.0, None, ALU.add))
            link(v.tensor_scalar(pend_i[:, NE:], pend_i[:, NE:], 1, None, ALU.arith_shift_right))
            link(v.tensor_scalar(blk_cmp, pend, blk_no[:, 0:1], None, ALU.is_le))
            link(v.tensor_reduce(blk_f, blk_cmp, AX.X, ALU.add))
            v.tensor_scalar(blk_f, blk_f, float(NE - 1), None, ALU.min).then_inc(blk_ready, 1)
            dve.wait_ge(blk_ready, 1)

            def slots(i):
                it = bass.ds(i, 1)
                pos = pos_last if isinstance(i, int) and i == TP else U[0][:, bass.ds(i * NE, NE)]
                six = [P, TOPK, NE]
                v.tensor_tensor(eq_k, mk_all[:, it, :].to_broadcast(six), bc(kconst[:, 0:TOPK], six), ALU.is_equal)
                link(v.tensor_tensor(dest, pos, pbase, ALU.add))
                link(v.tensor_tensor(eq_k, eq_k, dest.unsqueeze(1).to_broadcast(six), ALU.mult))
                link(v.tensor_reduce(dst_f[:, 0:TOPK], eq_k, AX.X, ALU.add))
                v.tensor_copy(dst_i[:, it, 0:TOPK].rearrange("p a k -> p (a k)"), dst_f[:, 0:TOPK]).then_inc(dest_ready, 1)
                dve.wait_ge(dest_ready, i + 1)

            def blk_hid(n):
                dve.wait_ge(silu_ready, n + 1)
                v.tensor_tensor(hid, U[1][:, DE:2 * DE], hsil, ALU.mult).then_inc(hid_ready, 1)

            def blk_hidT(n):
                dve.wait_ge(hid_posed, n + 1)
                v.tensor_copy(hidT, T0[:, 0:DE].rearrange("p (f n) -> p f n", f=FT)).then_inc(hidT_ready, 1)

            def blk_y(n, stored, k, r=0):
                dve.wait_ge(y_done, n + 1)
                dve.wait_ge(stored, k)
                v.tensor_copy(y_sbs[r], R[:, :]).then_inc(y_evac, 1)

            dve.wait_ge(h2_stored, 16 * NT)
            slots(0)
            blk_hid(0)
            blk_hidT(0)
            def shared(n):
                slots(n)
                blk_hid(n)
                blk_y(n - 1, ysh_stored, 16 * n - 16)
                blk_hidT(n)

            shared(1)
            before = own.base + own.k
            with dve.Fori(2, NT - 1) as n:
                own.at((n - 2) * 3 + before)
                shared(n)
                assert own.k == 3
            own.at(before + 3 * (NT - 3))
            slots(TP)
            blk_hid(NT - 1)
            blk_y(NT - 2, ysh_stored, 16 * (NT - 2))
            blk_hidT(NT - 1)
            blk_y(NT - 1, ysh_stored, 16 * (NT - 1))
            dve.wait_ge(slot_posed, 1)
            dve.wait_ge(blkrow_posed, 1)
            link(v.tensor_copy(slot_i, U[0][:, 0:P]))
            v.tensor_scalar(tok_i, slot_i, 3, None, ALU.arith_shift_right).then_inc(slot_ready, 1)
            dve.wait_ge(slot_ready, 1)
            v.tensor_copy(blk_e, U[0][0:1, P:2 * P]).then_inc(blkrow_ready, 1)
            dve.wait_ge(blkrow_ready, 1)

            dve.wait_ge(blkrow_ready, 1)
            last = dve.value_load(pend_i[0:1, NE:], min_val=MINPAIR - 1, max_val=MAXPAIR - 1)
            dve.wait_ge(ysh_stored, 16 * NT)

            def routed(g, r, first=False):
                b = 2 * g + r
                blk_hid(b + NT)
                if not first:
                    if r == 0:
                        blk_y(b + NT - 1, scattered[1], 16 * g - 16, 1)
                    else:
                        blk_y(b + NT - 1, scattered[0], 16 * g, 0)
                blk_hidT(b + NT)

            routed(0, 0, True)
            routed(0, 1)
            routed(1, 0)
            routed(1, 1)
            with dve.Fori(2, MAXPAIR) as g:
                with dve.If(g <= last):
                    routed(g, 0)
                    routed(g, 1)
            blk_y(2 * last + 1 + NT, scattered[1], 16 * last, 1)

            def combine(i, r, g, rows=P):
                it = bass.ds(i, 1)
                dve.wait_ge(rows_in[r], 32 * (g + 1))
                acc = yk[r][0:rows, 6, :]
                for k in range(TOPK):
                    link(v.scalar_tensor_tensor(acc, yk[r][0:rows, k, :], w6[0:rows, it, k:k + 1].rearrange("p a k -> p (a k)"),
                                                acc, ALU.mult, ALU.add))
                link(v.tensor_tensor(acc, acc, gt_f[0:rows, :], ALU.mult))
                v.tensor_tensor(xg[0:rows, :], acc, x2f[r][0:rows], ALU.add).then_inc(x3_ready, 1)
                dve.wait_ge(x3_ready, i + 1)
                dve.wait_ge(fin_std, i + 1)
                link(v.reciprocal(rstd1[0:rows, :], std1[0:rows, :]))
                dve.wait_ge(fin_stored[r], 16 * g)
                v.scalar_tensor_tensor(fin[r][0:rows], xg[0:rows, :], rstd1[0:rows, :], g_fin[0:rows, :],
                                       ALU.mult, ALU.mult).then_inc(fin_ready[r], 1)
                dve.wait_ge(fin_ready[r], g + 1)

            dve.wait_ge(finv_in, 32)
            for r in range(2):
                combine(r, r, 0)
            before = own.base + own.k
            with dve.Fori(1, TP // 2) as g:
                own.at((g - 1) * 16 + before)
                for r in range(2):
                    combine(2 * g + r, r, g)
                assert own.k == 16
            own.at(before + 16 * (TP // 2 - 1))
            dve.wait_ge(finv_in, 48)
            combine(TP, 0, TP // 2, NS)

        @block.gpsimd
        def _(pool):
            g_ = nc.gpsimd
            own = Steps(pool, pool_step)

            def shift(i):
                pool.wait_ge(h_scaled, i + 1)
                g_.tensor_tensor(x_t[:, :], x_t[:, :], B_m, ALU.add).then_inc(h_ready, 1)

            def ret_out(j):
                o = o_t[:, :, :].rearrange("p h e -> p (h e)")
                pool.wait_ge(gn_ready, j + 1)
                own.link(g_.tensor_tensor(o, o, gret[:, 0, :], ALU.mult))
                own.link(g_.tensor_tensor(o, o, gret[:, 1, :], ALU.add))
                pool.wait_ge(sg_ready, j + 1)
                g_.tensor_tensor(o, o, sg[:, :], ALU.mult).then_inc(ret_ready, 1)

            def conv3(j):
                c = CT - 1
                pool.wait_ge(win_ready, j + 1)
                pool.wait_ge(catA_part, 4 * j)
                def tap(w):
                    return cw[:, c, w:w + 1].to_broadcast([P, P])

                g_.tensor_tensor(cv[:, c, :], win[:, c, 0:P], tap(0), ALU.mult)
                for w in range(1, CW):
                    own.link(g_.tensor_tensor(prod[:, :], win[:, c, w:w + P], tap(w), ALU.mult))
                    own.link(g_.tensor_tensor(cv[:, c, :], cv[:, c, :], prod[:, :], ALU.add))
                ins = g_.tensor_tensor(cv[:, c, :], cv[:, c, :], cvec[:, c:c + 1].to_broadcast([P, P]), ALU.add)
                ins.then_inc(conv3_ready, 1)

            shift(0)
            shift(1)
            pool.wait_ge(cvec_ready, 1)
            conv3(0)
            shift(2)
            ret_out(0)
            before = own.k
            with pool.Fori(2, TP) as i:
                own.at((i - 2) * POOL_LOOP + before)
                conv3(i - 1)
                shift(i + 1)
                ret_out(i - 1)
                assert own.k == POOL_LOOP, own.k
            own.at(before + (TP - 2) * POOL_LOOP)
            conv3(TP - 1)
            ret_out(TP - 1)
            pool.sem_inc(conv3_ready, 1)
            ret_out(TP)

            pool.wait_ge(cen_ready, NT)
            pool.wait_ge(catA_part, 4 * (NT))
            g_.memset(pad_row, float(8 * (ROWS - 1))).then_inc(pad_ready, 1)
            pool.wait_ge(table_filled, 16)
            for i in range(NT):
                pool.wait_ge(dest_ready, i + 1)
                rows = P if i < TP else NS
                for k in range(TOPK):
                    pool.indirect_dma_start(slot_tab, bass.IndirectOffsetOnAxis(ap=dst_i[0:rows, i, k:k + 1], axis=0),
                                            slot_val[0:rows, i, k:k + 1], None, bounds_check=NSLOT - 1,
                                            oob_is_err=False).then_inc(slots_out, 16)

            def gather(g, r):
                pool.wait_ge(xg_posed, 2 * g + r + NT - 1)
                g_.tensor_copy(tok_cur[:, r:r + 1], tok_i[:, bass.ds(2 * g + r, 1)]).then_inc(tok_ready, 1)
                pool.wait_ge(tok_ready, 2 * g + r + 1)
                pool.sem_inc(pool_free, 1)
                pool.indirect_dma_start(xgs[r], None, h2_rows, bass.IndirectOffsetOnAxis(ap=tok_cur[:, r:r + 1], axis=0),
                                        bounds_check=ROWS - 1, oob_is_err=False).then_inc(gathered[r], 16)

            def scatter(g, r):
                pool.wait_ge(y_evac, 2 * g + r + NT + 1)
                g_.tensor_copy(slot_cur[:, r:r + 1], slot_i[:, bass.ds(2 * g + r, 1)]).then_inc(slot_picked, 1)
                pool.wait_ge(slot_picked, 2 * g + r + 1)
                pool.sem_inc(pool_free, 1)
                pool.indirect_dma_start(y_rows, bass.IndirectOffsetOnAxis(ap=slot_cur[:, r:r + 1], axis=0), y_sbs[r], None,
                                        bounds_check=8 * TOKENS - 1, oob_is_err=False).then_inc(scattered[r], 16)

            pool.wait_ge(slot_ready, 1)
            pool.wait_ge(blkrow_ready, 1)
            last = pool.value_load(pend_i[0:1, NE:], min_val=MINPAIR - 1, max_val=MAXPAIR - 1)
            gather(0, 0)
            gather(0, 1)
            gather(1, 0)
            gather(1, 1)
            scatter(0, 0)
            with pool.Fori(1, MAXPAIR) as g:
                with pool.If(g <= last):
                    gather(g + 1, 0)
                    scatter(g - 1, 1)
                    gather(g + 1, 1)
                    scatter(g, 0)
            scatter(last, 1)


GAMMA = [1.0 - 2.0 ** (-5.0 - h) for h in range(H)]
TAPS = (17, 21, 26, 29)
POOL_LOOP = 2 * CW - 2 + 2
DVE_LOOP = 124


def constants():
    f = np.float32
    pos = np.concatenate([np.arange(SEQ), np.full(NS, PAST), np.zeros(ROWS - TOKENS)]).astype(f)
    inv = (10000.0 ** (-np.arange(HD // 2) / (HD // 2))).astype(f)
    ang = pos[:, None] * inv[None, :]
    cos, sin = np.cos(ang.astype(np.float64)), np.sin(ang.astype(np.float64))
    i = np.arange(P, dtype=np.float64)
    gam = np.array(GAMMA)
    rel = i[None, :] - i[:, None]
    mask = np.where(rel[:, None, :] >= 0, gam[None, :, None] ** np.maximum(rel, 0)[:, None, :], 0.0) * HD ** -0.5
    rows = np.concatenate([gam[None, :] ** (i[:, None] + 1) * HD ** -0.5, gam[None, :] ** (P - 1 - i[:, None]),
                           np.tile(gam[None, :] * HD ** -0.5, (P, 1))], 1)
    g = np.arange(NG)
    token = np.arange(ROWS).reshape(NT, P).T
    return {
        "ident": np.eye(P), "mean_w": np.full((P, P), 1.0 / DC), "tri": np.triu(np.ones((P, P)), 1), "maskT": mask,
        "rows_c": rows, "lt": np.tile((g[None, :] < g[:, None])[None], (P, 1, 1)), "kconst": np.tile(1.0 + g[None, :], (P, 1)),
        "rope": np.stack([cos, -sin, sin], 1), "slot_val": 8 * token[:, :, None] + g[None, None, :], "blk_no": i[:, None],
    }


OUTS = {
    "y_prompt": (1, SEQ, D), "y_sample": (NS, 1, D), "new_conv_prompt": (1, 1, CW - 1, DC), "new_ret_prompt": (1, 1, H, HD, HD),
    "new_conv_sample": (1, NS, CW - 1, DC), "new_ret_sample": (1, NS, H, HD, HD),
}


def kernel(**inputs):
    import concourse.bacc as bacc
    from concourse.bass_utils import run_bass_kernel_spmd

    nc = bacc.Bacc("TRN2", target_bir_lowering=False, num_devices=1)
    arrays = {name: np.ascontiguousarray(a) for name, a in inputs.items()}
    arrays |= {name: np.ascontiguousarray(a.astype(np.float32)) for name, a in constants().items()}
    t = {name: nc.dram_tensor("in_" + name, a.shape, F32, kind="ExternalInput").ap() for name, a in arrays.items()}
    out = {name: nc.dram_tensor("out_" + name, shape, F32, kind="ExternalOutput").ap() for name, shape in OUTS.items()}
    build(nc, t, out)
    r = run_bass_kernel_spmd(nc, [{"in_" + name: a for name, a in arrays.items()}], core_ids=[0])
    return tuple(r.results[0]["out_" + name] for name in OUTS)
```

```python
import numpy as np
import concourse.bass as bass
import concourse.mybir as mybir
from concourse.alu_op_type import AluOpType as ALU
from contextlib import ExitStack

P = 128
D = 1024
KT = D // P
SEQ, NS = 1024, 8
TP = SEQ // P
NT = TP + 1
ROWS = NT * P
DC, DR, H, HD = 512, 512, 4, 128
CT = DC // P
CW = 31
PAST = 8192
NE, NG, PER, TOPG, TOPK = 64, 8, 8, 4, 6
DE = 256
FT = DE // P
EPS = 1e-6
BIG = 1e30
TOKENS = SEQ + NS
MAXBLK = (TOKENS * TOPK + NE * P) // P
MINBLK = max(NE, -(-TOKENS * TOPK // P))
MAXPAIR = -(-MAXBLK // 2)
MINPAIR = -(-MINBLK // 2)
NSLOT = P * P
RING = 4
WE = KT * 2 * DE + FT * D
F32, BF16, I32 = mybir.dt.float32, mybir.dt.bfloat16, mybir.dt.int32
ACT = mybir.ActivationFunctionType
AX = mybir.AxisListType
GA, GB, GQ, GK, GV, GG = range(6)




class Steps:

    def __init__(self, eng, sem):
        self.eng, self.sem, self.base, self.k = eng, sem, 0, 0

    def add(self, ins):
        ins.then_inc(self.sem, 1)
        self.k += 1

    def link(self, ins):
        self.add(ins)
        self.eng.wait_ge(self.sem, self.base + self.k)

    def at(self, base):
        self.base, self.k = base, 0


def build(nc, t, out):
    with ExitStack() as ctx:
        def sb(name, shape, dt=F32):
            return ctx.enter_context(nc.sbuf_tensor(name, shape, dt))

        def sem(name):
            return ctx.enter_context(nc.semaphore(name))

        c_in, bada_in, ident_in, csilu, c_posed, cT_ready, ada_done, mod_ready, mod_stored, consts_in, win_in = (
            sem(n) for n in "c_in bada_in ident_in csilu c_posed cT_ready ada_done mod_ready mod_stored consts_in win_in".split())
        wout_in, modv_in, smod1_in, smod2_in, smod3_in, state_zero, x_in, rope_in, xr_in, norm1_ssq, norm1_std = (
            sem(n) for n in "wout_in modv_in smod1_in smod2_in smod3_in state_zero x_in rope_in xr_in norm1_ssq norm1_std".split())
        h_scaled, h_ready, x_posed, hT_ready, ub_done, ua_done, uq_done, uk_done, uv_done, ug_done, sig_ready = (
            sem(n) for n in "h_scaled h_ready x_posed hT_ready ub_done ua_done uq_done uk_done uv_done ug_done sig_ready".split())
        glu_ready, q_rot, k_rot, v_ready, sg_ready, glu_posed, win_ready, q_posed, qT_ready, k_posed, kT_ready = (
            sem(n) for n in "glu_ready q_rot k_rot v_ready sg_ready glu_posed win_ready q_posed qT_ready k_posed kT_ready".split())
        scores_done, sm_ready, kd_ready, ret_done, S_ready, conv_ready, win_shifted, sum1_done, cen_ready = (
            sem(n) for n in "scores_done sm_ready kd_ready ret_done S_ready conv_ready win_shifted sum1_done cen_ready".split())
        sq_ready, sum2_done, std_c, cnorm_ready, catA_part, gn_var, gn_std, gn_ready, ret_ready, ret_posed = (
            sem(n) for n in "sq_ready sum2_done std_c cnorm_ready catA_part gn_var gn_std gn_ready ret_ready ret_posed".split())
        catB_ready, wout_done, y_gated, x2_ready, norm2_ssq, norm2_std, x2_stored, h2_ready, h2_stored, h2_posed = (
            sem(n) for n in "catB_ready wout_done y_gated x2_ready norm2_ssq norm2_std x2_stored h2_ready h2_stored h2_posed".split())
        h2T_ready, router_done, score_ready, topk_done, cvec_in, cvec_posed, cvec_ready, glu_last_out = (
            sem(n) for n in "h2T_ready router_done score_ready topk_done cvec_in cvec_posed cvec_ready glu_last_out".split())
        newconv_out, newret_out, s0_in, sconv_in, cs_posed, cs_half, s_cross_done, crossT_ready, cross_posed = (
            sem(n) for n in "newconv_out newret_out s0_in sconv_in cs_posed cs_half s_cross_done crossT_ready cross_posed".split())
        sret_ready, vmask_ready, state_mm, state_upd, tri_in, pairs_ready, pos_done, pad_ready, table_filled = (
            sem(n) for n in "sret_ready vmask_ready state_mm state_upd tri_in pairs_ready pos_done pad_ready table_filled".split())
        dest_ready, slots_out, slot_in, slot_posed, slot_ready, blk_ready, blkrow_posed, blkrow_ready, shw_in = (
            sem(n) for n in "dest_ready slots_out slot_in slot_posed slot_ready blk_ready blkrow_posed blkrow_ready shw_in".split())
        xg_posed, xgT_ready, h_done, silu_ready, hid_ready, hid_posed, hidT_ready, y_done, y_evac = (
            sem(n) for n in "xg_posed xgT_ready h_done silu_ready hid_ready hid_posed hidT_ready y_done y_evac".split())
        ysh_stored, w_ready, finv_in, x3_ready, fin_ssq, fin_std, dve_step, conv3_ready, pool_step = (
            sem(n) for n in "ysh_stored w_ready finv_in x3_ready fin_ssq fin_std dve_step conv3_ready pool_step".split())
        tok_ready, slot_picked, pool_free, sp_free, modab_in, shift_stored, win_late, gtf_in, x2_in, sample_in, x3s_ready, sample_ready = (
            sem(n) for n in "tok_ready slot_picked pool_free sp_free modab_in shift_stored win_late gtf_in x2_in sample_in x3s_ready sample_ready".split())
        ada_in = [sem(f"ada_in{r}") for r in range(3)]
        ring_in = [sem(f"ring_in{r}") for r in range(RING)]
        rows_in, fin_ready, fin_stored = ([sem(f"{n}{r}") for r in range(2)] for n in ("rows_in", "fin_ready", "fin_stored"))
        xg_in, gathered, scattered = ([sem(f"{n}{r}") for r in range(2)] for n in ("xg_in", "gathered", "scattered"))

        def scratch(name, shape, dt=F32):
            return nc.dram_tensor(name, shape, dt, kind="Internal").ap()

        mod_rows = scratch("mod_rows", (1 + NS, 6 * D))
        x2_rows = scratch("x2_rows", (ROWS, D))
        h2_rows = scratch("h2_rows", (ROWS, D))
        y_rows = scratch("y_rows", (ROWS * 8, D))
        slot_tab = scratch("slot_tab", (NSLOT, 1))

        W = sb("W", [P, KT * 3072 + KT * D])
        ada_w = [W[:, 16384 + 4096 * r:20480 + 4096 * r].rearrange("p (k n) -> p k n", k=KT) for r in range(2)]
        mod_sb = W[0:9, 24576:24576 + 6 * D]
        gains = W[0:9, 24576 + 6 * D:24576 + 8 * D]
        w_in = W[:, 0:KT * 3072].rearrange("p (k n) -> p k n", k=KT)
        w_out = W[:, KT * 3072:KT * 4096].rearrange("p (k n) -> p k n", k=KT)
        late = W[:, 12288:24576].rearrange("p (k n) -> p k n", k=KT // 2)
        S0 = late[:, :, 0:1024].rearrange("p k (c h e) -> p k c h e", c=2, h=H)
        sconv = late[:, 0:2, 1024:1024 + DC]
        vmask = late[0:NS, :, 2048:3072].rearrange("p k (c n) -> p k c n", c=2)
        cbuf = late[:, 2, 1024:1024 + CT * NS * CW].rearrange("p (c b w) -> p c b w", c=CT, b=NS)
        cprod = late[:, 3, 1024:1024 + NS * CW].rearrange("p (b w) -> p b w", b=NS)
        crossT = late[:, 3, 1280:1280 + H * NS].rearrange("p (h b) -> p h b", h=H)
        qk = late[:, 3, 1320:1320 + H]
        qk_prod = late[:, 3, 1400:1912].rearrange("p (h d) -> p h d", h=H)
        shw = W[:, 0:WE]
        ring = W[:, WE:(RING + 1) * WE].rearrange("p (r w) -> p r w", r=RING)
        xg_b, y_sb_b = (W[:, (RING + 1) * WE + D * i:(RING + 1) * WE + D * i + D] for i in range(2))
        yk = [W[:, 7168 * r:7168 * (r + 1)].rearrange("p (k n) -> p k n", k=7) for r in range(2)]
        fin = [W[:, 16384 + D * r:17408 + D * r] for r in range(2)]
        x3 = [W[:, 18432 + D * r:19456 + D * r] for r in range(2)]
        yk_s = W[0:NS, 20480:27648].rearrange("p (k n) -> p k n", k=7)
        gt_s, x3_s, fin_s = (W[0:NS, 27648 + D * i:28672 + D * i] for i in range(3))

        ident = sb("ident", [P, P])
        mean_w = sb("mean_w", [P, P])
        maskT = sb("maskT", [P, H, P])
        rows_c = sb("rows_c", [P, 12])
        q_dec, k_dec, s_dec = rows_c[:, 0:4], rows_c[:, 4:8], rows_c[:, 8:12]
        lt = sb("lt", [P, NG, NG])
        kconst = sb("kconst", [P, 8])
        ones64 = sb("ones64", [P, NE])
        w_rt = sb("w_rt", [P, KT, NE])
        bias_r = sb("bias_r", [P, NE])
        mods = sb("mods", [P, 5, D])
        A_m, B_m, gt_m, A_f, B_f = (mods[:, v, :] for v in range(5))
        gret = sb("gret", [P, 2, DR])
        ada_mods = mods[:, 2:5, :].rearrange("p v n -> p (v n)").rearrange("p (k n) -> p k n", k=6)
        ada_rows = [[w[:, k, :] for k in range(KT)] for w in ada_w]
        ada_rows.append([ada_mods[:, k, :] for k in range(6)] + [gret[:, k, :] for k in range(2)])
        cvec = sb("cvec", [P, 12])
        cw = sb("cw", [P, CT, CW])
        mk_all = sb("mk_all", [P, NT, NE], BF16)
        w6 = sb("w6", [P, NT, TOPK])

        x_t = sb("x_t", [P, D])
        hT = sb("hT", [P, KT, P])
        sig = sb("sig", [P, DC])
        junk = sig[:, :].bitcast(BF16)
        glu = sb("glu", [P, DC])
        rt2 = sb("rt2", [P, DC])
        q_r = sb("q_r", [P, DR])
        k_r = sb("k_r", [P, DR])
        k_d = sb("k_d", [P, DR])
        v_t = sb("v_t", [P, DR])
        sg = sb("sg", [P, DR])
        win = sb("win", [P, CT, CW - 1 + P])
        qT = sb("qT", [P, H, P])
        kT = sb("kT", [P, H, P])
        sm = sb("sm", [P, H, P])
        S = sb("S", [P, H, HD])
        o_t = sb("o_t", [P, H, HD])
        cv = sb("cv", [P, CT, P])
        cat = sb("cat", [P, KT, P])
        h2T = cat
        xr = sb("xr", [P, D])
        rope = sb("rope", [P, 3, HD // 2])
        bn = sb("bn", [P, H, 6])
        mv = sb("mv", [P, H, 2])
        gstd = sb("gstd", [P, H])
        st = sb("st", [P, 6])
        eps_c = sb("eps_c", [P, 1])
        scrap = sb("scrap", [P, 1])
        prod = sb("prod", [P, P])
        tok_cur = sb("tok_cur", [P, 2], I32)
        slot_cur = sb("slot_cur", [P, 2], I32)
        ssq1, std1, rstd1, ssq2, std2, rstd2 = (st[:, i:i + 1] for i in range(6))
        sq = rt2[:, :].rearrange("p (c n) -> p c n", c=CT)
        cvrow = sm[:, 0, :]
        tk = sm[:, :, :].rearrange("p c n -> p (c n)")
        sc_t, sel, top8s = tk[:, 0:64], tk[:, 64:128], tk[:, 128:192]
        pair_a, pair_b = tk[:, 192:256], tk[:, 256:320]
        gsum, rank, keep, pen, t8 = (tk[:, 320 + 8 * i:328 + 8 * i] for i in range(5))
        ngt, need, wsum, wrec = (tk[:, 360 + i:361 + i] for i in range(4))
        pick, wfull = tk[:, 384:448], tk[:, 448:512]
        eq_k = rt2[:, 0:TOPK * NE].rearrange("p (k e) -> p k e", k=TOPK)
        U = [ctx.enter_context(nc.psum_tensor(f"U{i}", [P, 512], F32)) for i in range(2)]
        X = ctx.enter_context(nc.psum_tensor("X", [P, D], F32))
        T0 = ctx.enter_context(nc.psum_tensor("T0", [P, 512], F32))
        R = ctx.enter_context(nc.psum_tensor("R", [P, D], F32))
        R2 = ctx.enter_context(nc.psum_tensor("R2", [P, 512], F32))
        Xk = X[:, :].rearrange("p (k n) -> p k n", k=KT)
        T4 = T0[:, :].rearrange("p (h n) -> p h n", h=4)
        inner, cross = (R[:, 512 * i:512 * i + 512].rearrange("p (h n) -> p h n", h=H) for i in range(2))
        R24 = R2[:, :].rearrange("p (h n) -> p h n", h=4)
        xg, xgT, y_sb = x_t, hT, xr
        xgs, y_sbs = (xg[:, :], xg_b), (y_sb[:, :], y_sb_b)
        hsil, hid = sg[:, 0:DE], sg[:, DE:2 * DE]
        hidT = glu[:, 0:DE].rearrange("p (f n) -> p f n", f=FT)
        pairs = q_r[:, 0:NT * NE // 2].bitcast(BF16).rearrange("p (t e) -> p t e", t=NT)
        cnt_f, nblk, pend, pbase = (k_r[:, 64 * i:64 * i + 64] for i in range(4))
        cnt_i = k_r[:, 256:320].bitcast(I32)
        dest = k_d[:, 0:NE]
        dst_f = v_t[:, 0:8]
        dst_i = qT[:, 0, 0:NT * 8].bitcast(I32).rearrange("p (t k) -> p t k", t=NT)
        slot_val = qT[:, 3, 0:NT * 8].rearrange("p (t k) -> p t k", t=NT)
        slot_row, pad_row, tri_f = cv[:, 0, :], cv[:, 1, :], cv[:, 2, :]
        tri_bf, ones_bf = (cv[:, 3, 64 * i:64 * i + 64].bitcast(BF16) for i in range(2))
        slot_i = kT[:, 0, :].bitcast(I32)
        tok_i = kT[:, 1, :].bitcast(I32)
        blk_f = st[:, 0:1]
        blk_cmp = o_t[:, 0, 0:NE]
        blk_no = sb("blk_no", [P, 1])
        blk_e = qT[0:1, 1, :].bitcast(I32)
        pend_i = qT[0:1, 2, 0:NE + 1].bitcast(I32)
        pos_last = R2[:, 0:NE]
        count = R2[:, NE:2 * NE]
        gt_f, g_fin = mods[:, 0, :], mods[:, 1, :]
        x2c = cat[:, :, :].rearrange("p k n -> p (k n)")
        y_of = y_rows.rearrange("(t p k) d -> t p k d", p=P, k=8)

        BANK = {GB: 0, GA: 1, GV: 0, GQ: 1, GG: 0, GK: 1}

        def floor(n):
            return max(n, 0) if isinstance(n, int) else n

        def bc(ap, shape):
            return ap.unsqueeze(2).to_broadcast(shape)

        def everywhere(row, n=P):
            return row.to_broadcast([n, row.shape[1]])

        block = ctx.enter_context(nc.Block())

        @block.sync
        def _(sp):
            def ada(ch):
                rows = t["w_ada"][0][:, 512 * ch:512 * ch + 512].rearrange("(k p) n -> p k n", p=P)
                if ch % 3 < 2:
                    sp.dma_start(ada_w[ch % 3], rows).then_inc(ada_in[ch % 3], 16)
                else:
                    sp.dma_start(ada_mods, rows[:, 0:6, :]).then_inc(ada_in[2], 16)
                    sp.dma_start(gret[:, :, :], rows[:, 6:8, :]).then_inc(ada_in[2], 16)

            sp.dma_start(xr[0:1, :], t["c_prompt"]).then_inc(c_in, 16)
            sp.dma_start(xr[1:9, :], t["c_sample"]).then_inc(c_in, 16)
            sp.dma_start(ident[:, :], t["ident"]).then_inc(ident_in, 16)
            for ch in range(3):
                ada(ch)
            sp.dma_start(mod_sb, everywhere(t["b_ada"][0:1, :], 9)).then_inc(bada_in, 16)
            sp.dma_start(gains[:, 0:D], everywhere(t["g_mix"][0:1, :], 9)).then_inc(bada_in, 16)
            sp.dma_start(gains[:, D:2 * D], everywhere(t["g_ffn"][0:1, :], 9)).then_inc(bada_in, 16)
            sp.dma_start(x_t[:, :], t["x_prompt"][0, 0:P, :]).then_inc(x_in, 16)
            sp.dma_start(rope[:, :, :], t["rope"][0:P]).then_inc(rope_in, 16)
            for ch in range(3, 12):
                sp.wait_ge(ada_done, ch - 2)
                ada(ch)
                if ch == 6:
                    sp.wait_ge(mod_ready, 4)
                    sp.dma_start(mod_rows[:, 0:2 * D], mod_sb[:, 0:2 * D]).then_inc(shift_stored, 16)
                if ch == 7:
                    sp.wait_ge(shift_stored, 16)
                    for v, m in enumerate((1, 0)):
                        sp.dma_start(mods[:, v, :], everywhere(mod_rows[0:1, D * m:D * m + D])).then_inc(modab_in, 16)
            for k in range(5):
                sp.dma_start(w_in[:, k, :], t["w_in"][0][P * k:P * k + P, :]).then_inc(win_in, 16)
            for n, name in enumerate(("conv_b", "conv_norm_g", "conv_norm_b")):
                sp.dma_start(cvrow[4 * n:4 * n + 4, :], t[name][0].rearrange("(c p) -> c p", p=P)).then_inc(cvec_in, 16)
            sp.dma_start(cv[0:CW, :, :], t["conv_w"][0].rearrange("w (c p) -> w c p", p=P)).then_inc(cvec_in, 16)
            for k in range(5, KT):
                sp.wait_ge(ada_done, min(k + 5, 11))
                sp.dma_start(w_in[:, k, :], t["w_in"][0][P * k:P * k + P, :]).then_inc(win_in if k < 6 else win_late, 16)
            sp.wait_ge(mod_ready, 12)
            sp.dma_start(mod_rows[:, 2 * D:], mod_sb[:, 2 * D:]).then_inc(mod_stored, 16)
            for o, n in ((mean_w, "mean_w"), (maskT, "maskT"), (rows_c, "rows_c"), (lt, "lt"), (kconst, "kconst"),
                         (blk_no, "blk_no")):
                sp.dma_start(o[:], t[n]).then_inc(consts_in, 16)
            sp.dma_start(w_rt[:, :, :], t["w_router"][0].rearrange("(k p) n -> p k n", p=P)).then_inc(consts_in, 16)
            sp.dma_start(bias_r[:, :], everywhere(t["router_bias"][0:1, :])).then_inc(consts_in, 16)
            sp.dma_start(gret[:, 0, :], everywhere(t["ret_norm_g"][0:1, :])).then_inc(consts_in, 16)
            sp.dma_start(gret[:, 1, :], everywhere(t["ret_norm_b"][0:1, :])).then_inc(consts_in, 16)
            sp.wait_ge(mod_stored, 16)
            for v, m in ((2, 2), (3, 4), (4, 3)):
                sp.dma_start(mods[:, v, :], everywhere(mod_rows[0:1, D * m:D * m + D])).then_inc(modv_in, 16)
            sp.dma_start(w_out[:, :, :], t["w_out"][0].rearrange("(k p) n -> p k n", p=P)).then_inc(wout_in, 16)

            def load_next(i):
                sp.wait_ge(x_posed, i + 1)
                if isinstance(i, int) and i + 1 == TP:
                    sp.dma_start(x_t[0:NS, :], t["x_sample"][:, 0, :]).then_inc(x_in, 16)
                else:
                    sp.dma_start(x_t[:, :], t["x_prompt"][0][bass.ds((i + 1) * P, P), :]).then_inc(x_in, 16)

            def load_rope(i):
                sp.wait_ge(k_rot, i + 1)
                sp.dma_start(rope[:, :, :], t["rope"][bass.ds((i + 1) * P, P)]).then_inc(rope_in, 16)

            def store_route(m):
                sp.wait_ge(x2_ready, m + 1)
                sp.dma_start(x2_rows[bass.ds(m * P, P), :], xr[:, :]).then_inc(x2_stored, 16)
                sp.wait_ge(h2_ready, m + 1)
                sp.dma_start(h2_rows[bass.ds(m * P, P), :], xr[:, :]).then_inc(h2_stored, 16)

            def load_residual(j):
                if isinstance(j, int) and j == 0:
                    sp.wait_ge(cT_ready, 1)
                else:
                    sp.wait_ge(h2_stored, 16 * j)
                    sp.wait_ge(h2_posed, j)
                if isinstance(j, int) and j == TP:
                    sp.dma_start(xr[0:NS, :], t["x_sample"][:, 0, :]).then_inc(xr_in, 16)
                else:
                    sp.dma_start(xr[:, :], t["x_prompt"][0][bass.ds(j * P, P), :]).then_inc(xr_in, 16)

            load_next(0)
            load_rope(0)
            load_next(1)
            load_residual(0)
            load_rope(1)
            with sp.Fori(2, TP - 1) as i:
                load_next(i)
                store_route(i - 2)
                load_residual(i - 1)
                load_rope(i)
            sp.wait_ge(h_ready, TP)
            sp.dma_start(mods[0:NS, 0, :], mod_rows[1:9, D:2 * D]).then_inc(smod1_in, 16)
            sp.dma_start(mods[0:NS, 1, :], mod_rows[1:9, 0:D]).then_inc(smod1_in, 16)
            load_next(TP - 1)
            store_route(TP - 3)
            load_residual(TP - 2)
            sp.wait_ge(glu_ready, TP)
            sp.dma_start(out["new_conv_prompt"][0, 0], glu[P - CW + 1:P, :]).then_inc(glu_last_out, 16)
            load_rope(TP - 1)
            sp.dma_start(out["new_conv_sample"][0][:, 0:CW - 2, :],
                         t["state_conv"][0][:, 1:CW - 1, :]).then_inc(newconv_out, 16)
            store_route(TP - 2)
            load_residual(TP - 1)
            sp.wait_ge(ub_done, NT)
            sp.wait_ge(ua_done, NT)
            for b in range(NS):
                sp.dma_start(S0[:, b // 2, b % 2, :, :], t["state_ret"][0][b].rearrange("h d e -> d h e")).then_inc(s0_in, 16)
            sp.wait_ge(uq_done, NT)
            for r in range(2):
                sp.dma_start(sconv[0:120, r, :],
                             t["state_conv"][0][4 * r:4 * r + 4].rearrange("b w n -> (b w) n")).then_inc(sconv_in, 16)
            def load_up(e, r, x):
                sp.dma_start(ring[:, r, KT * DE * x:KT * DE * (x + 1)], t[("w1", "w3")[x]][0][bass.ds(e, 1)].rearrange(
                    "a (p k) n -> p (a k n)", p=P)).then_inc(ring_in[r], 16)

            def load_down(e, r):
                sp.dma_start(ring[:, r, KT * 2 * DE:],
                             t["w2"][0][bass.ds(e, 1)].rearrange("a (p f) n -> p (a f n)", p=P)).then_inc(ring_in[r], 16)

            def load_expert(e, r):
                load_up(e, r, 0)
                load_up(e, r, 1)
                load_down(e, r)

            sp.wait_ge(uk_done, NT)
            for x, w in enumerate(("ws1", "ws3", "ws2")):
                sp.dma_start(shw[:, KT * DE * x:KT * DE * (x + 1)],
                             t[w][0].rearrange("(p k) n -> p (k n)", p=P)).then_inc(shw_in, 16)
            load_expert(0, 0)
            sp.wait_ge(x_posed, NT)
            sp.wait_ge(h2_stored, 16)
            sp.dma_start(xg[:, :], h2_rows[0:P, :]).then_inc(xg_in[0], 16)
            sp.dma_start(gt_f, everywhere(mod_rows[0:1, 5 * D:6 * D])).then_inc(gtf_in, 16)
            sp.wait_ge(glu_ready, NT)
            sp.dma_start(out["new_conv_sample"][0][:, CW - 2, :], glu[0:NS, :]).then_inc(newconv_out, 16)
            sp.wait_ge(S_ready, TP)
            sp.dma_start(out["new_ret_prompt"][0, 0].rearrange("h d e -> d h e"), S[:, :, :]).then_inc(newret_out, 16)
            sp.wait_ge(y_gated, TP)
            sp.dma_start(mods[0:NS, 2, :], mod_rows[1:9, 2 * D:3 * D]).then_inc(smod2_in, 16)
            store_route(TP - 1)
            sp.dma_start(mods[0:NS, 3, :],
                         mod_rows[1:9, 4 * D:5 * D]).then_inc(smod3_in, 16)
            sp.dma_start(mods[0:NS, 4, :], mod_rows[1:9, 3 * D:4 * D]).then_inc(smod3_in, 16)
            load_residual(TP)
            sp.wait_ge(state_upd, 2 * H)
            for b in range(NS):
                sp.dma_start(out["new_ret_sample"][0, b].rearrange("h d e -> d h e"),
                             S0[:, b // 2, b % 2, :, :]).then_inc(newret_out, 16)
            sp.wait_ge(newret_out, 16 * (NS + 1))
            sp.wait_ge(wout_done, NT)
            sp.dma_start(tri_f, t["tri"]).then_inc(tri_in, 16)
            sp.dma_start(slot_val, t["slot_val"]).then_inc(tri_in, 16)
            sp.wait_ge(pad_ready, 1)
            sp.dma_start(slot_tab.rearrange("(b r) a -> b (r a)", r=P), pad_row).then_inc(table_filled, 16)

            def load_rows(g, r):
                sp.wait_ge(xg_posed, floor(2 * g + r - 1))
                sp.dma_start(xgs[r], h2_rows[bass.ds((2 * g + r) * P, P), :]).then_inc(xg_in[r], 16)

            def load_x2(n):
                sp.dma_start(x2c, x2_rows[bass.ds(n * P, P), :]).then_inc(x2_in, 16)

            def store_shared(n):
                sp.wait_ge(y_evac, n + 1)
                sp.dma_start(y_of[bass.ds(n, 1), :, 6, :].rearrange("a p d -> (a p) d"), y_sb_b).then_inc(ysh_stored, 16)
                if n < NT - 1:
                    load_x2(n + 1)

            load_rows(0, 1)
            load_rows(1, 0)
            store_route(TP)
            sp.wait_ge(h2_stored, 16 * NT)
            sp.wait_ge(x2_stored, 16 * NT)
            sp.wait_ge(router_done, NT)
            load_x2(0)
            parts = [(load_up, e, e, 0) for e in range(1, RING)]
            parts += [(load_up, e, e, 1) for e in range(1, RING)] + [(load_down, e, e) for e in range(1, RING)]
            parts.sort(key=lambda part: part[1])
            for n in range(1, 6):
                load_rows((n + 2) // 2, n % 2)
                store_shared(n - 1)
                for load, *which in parts[2 * n - 2:2 * n]:
                    load(*which)
            load_rows(NT // 2, 0)
            store_shared(NT - 4)
            sp.wait_ge(slots_out, 16 * NT * TOPK)
            sp.dma_start(slot_row, slot_tab.rearrange("(b r) a -> b (r a)", r=P)).then_inc(slot_in, 16)
            store_shared(NT - 3)
            store_shared(NT - 2)
            sp.dma_start(gt_f[0:NS, :], mod_rows[1:9, 5 * D:6 * D]).then_inc(gtf_in, 16)
            store_shared(NT - 1)
            sp.dma_start(gt_f[0:NS, :], everywhere(mod_rows[0:1, 5 * D:6 * D], NS)).then_inc(finv_in, 16)
            for r in range(RING - 1):
                sp.wait_ge(ring_in[r], 48)
                sp.sem_inc(w_ready, 1)
            sp.wait_ge(blkrow_ready, 1)
            with sp.Fori(1, NE // RING) as g:
                for r in range(RING):
                    before = sp.value_load(pend_i[0:1, bass.ds((g - 1) * RING + r, 1)], min_val=0, max_val=MAXBLK)
                    sp.wait_ge(y_done, before + NT)
                    load_expert(g * RING + r, r)
                    sp.wait_ge(ring_in[(r - 1) % RING], 48 * g if r == 0 else 48 * g + 48)
                    sp.sem_inc(w_ready, 1)
            sp.wait_ge(ring_in[RING - 1], 48 * (NE // RING))
            sp.sem_inc(w_ready, 1)
            last = sp.value_load(pend_i[0:1, NE:], min_val=MINPAIR - 1, max_val=MAXPAIR - 1)
            sp.dma_start(g_fin, everywhere(t["g_final"].rearrange("(a n) -> a n", a=1))).then_inc(finv_in, 16)
            sp.wait_ge(ysh_stored, 16 * NT)
            for r in range(2):
                sp.wait_ge(scattered[r], 16 * last + 16)
                sp.sem_inc(sp_free, 1)
                sp.wait_ge(gathered[r], 16 * last + 32)
                sp.sem_inc(sp_free, 1)

            def load_tile(i, r):
                sp.dma_start(yk[r], y_of[bass.ds(i, 1), :, 0:7, :].rearrange("a p k d -> (a p) k d")).then_inc(rows_in[r], 16)

            def load_next_tile(i, r):
                sp.wait_ge(x3_ready, i - 1)
                load_tile(i, r)

            def store_result(g, r):
                sp.wait_ge(fin_ready[r], g + 1)
                sp.dma_start(out["y_prompt"][0][bass.ds((2 * g + r) * P, P), :], fin[r]).then_inc(fin_stored[r], 16)

            sp.dma_start(yk_s, y_of[TP, 0:NS, 0:7, :]).then_inc(sample_in, 16)
            sp.dma_start(gt_s, mod_rows[1:9, 5 * D:6 * D]).then_inc(sample_in, 16)
            load_tile(0, 0)
            load_tile(1, 1)
            load_next_tile(2, 0)
            with sp.Fori(0, TP // 2 - 2) as g:
                store_result(g, 0)
                load_next_tile(2 * g + 3, 1)
                store_result(g, 1)
                load_next_tile(2 * g + 4, 0)
            store_result(TP // 2 - 2, 0)
            load_next_tile(TP - 1, 1)
            store_result(TP // 2 - 2, 1)
            store_result(TP // 2 - 1, 0)
            store_result(TP // 2 - 1, 1)
            sp.wait_ge(sample_ready, 1)
            sp.dma_start(out["y_sample"][:, 0, :], fin_s).then_inc(fin_stored[0], 16)
            sp.wait_ge(fin_stored[0], 16 * (TP // 2 + 1))
            sp.wait_ge(fin_stored[1], 16 * (TP // 2))
            sp.wait_ge(glu_last_out, 16)
            sp.wait_ge(newconv_out, 32)

        @block.tensor
        def _(pe):
            mm, tr = nc.tensor.matmul, nc.tensor.transpose

            pe.wait_ge(csilu, 1)
            pe.wait_ge(ident_in, 16)
            for k in range(KT):
                last = tr(X[:, 16 * k:16 * k + 9], xr[0:9, P * k:P * k + P], ident[0:9, 0:9])
            last.then_inc(c_posed, 1)
            pe.wait_ge(cT_ready, 1)
            for ch in range(12):
                pe.wait_ge(ada_in[ch % 3], (32 if ch % 3 == 2 else 16) * (ch // 3 + 1))
                pe.wait_ge(mod_ready, floor(ch - 1))
                for k in range(KT):
                    last = mm(U[ch % 2][0:9, :], hT[:, k, 0:9], ada_rows[ch % 3][k], start=k == 0, stop=k == KT - 1)
                last.then_inc(ada_done, 1)
            pe.wait_ge(cvec_in, 64)
            for c in range(CT):
                tr(T0[:, 32 * c:32 * c + CW], cv[0:CW, c, :], ident[0:CW, 0:CW])
            tr(T0[:, P:P + 12], cvrow[0:12, :], ident[0:12, 0:12]).then_inc(cvec_posed, 1)

            def x_trans(i):
                pe.wait_ge(h_ready, i + 1)
                pe.wait_ge(h2T_ready, floor(i - 2))
                for k in range(KT):
                    last = tr(Xk[:, k, :], x_t[:, P * k:P * k + P], ident[:, :])
                last.then_inc(x_posed, 1)

            def project(i, g, done, free, n):
                pe.wait_ge(free, n)
                for k in range(KT):
                    if isinstance(i, int) and (i, g, k) == (0, GB, 6):
                        pe.wait_ge(win_late, 32)
                    last = mm(U[BANK[g]][:, :], hT[:, k, :], w_in[:, k, 512 * g:512 * g + 512], start=k == 0, stop=k == KT - 1)
                last.then_inc(done, 1)

            def four(src, done, free, n, ready, m, bank=T4):
                pe.wait_ge(ready, m)
                pe.wait_ge(free, n)
                for c in range(4):
                    last = tr(bank[:, c, :], src[:, P * c:P * c + P], ident[:, :])
                last.then_inc(done, 1)

            def norm_sum(src, done, ready, n):
                pe.wait_ge(ready, n)
                for c in range(CT):
                    last = mm(T0[:, 0:P], mean_w[:, :], src[:, c, :], start=c == 0, stop=c == CT - 1)
                last.then_inc(done, 1)

            def state_product(n):
                h, half = n // 2, n % 2
                pe.wait_ge(state_upd, floor(n - 1))
                mm(U[n % 2][:, :], k_r[0:NS, P * h:P * h + P], vmask[:, 2 * half:2 * half + 2, :, P * h:P * h + P],
                   start=True, stop=True).then_inc(state_mm, 1)

            def rows2_trans(m, free, n):
                pe.wait_ge(h2_ready, m + 1)
                pe.wait_ge(free, n)
                for k in range(KT):
                    last = tr(Xk[:, k, :], xr[:, P * k:P * k + P], ident[:, :])
                last.then_inc(h2_posed, 1)

            def router(m, n):
                pe.wait_ge(h2T_ready, m + 1)
                pe.wait_ge(S_ready, n)
                for k in range(KT):
                    last = mm(R2[:, 0:NE], h2T[:, k, :], w_rt[:, k, :], start=k == 0, stop=k == KT - 1)
                last.then_inc(router_done, 1)

            def body(i, front=True, tail=True, route=True, nxt=True):
                j, m = i - 1, i - 2
                prompt = not (isinstance(j, int) and j == TP)
                if tail:
                    four(q_r, q_posed, win_ready, j + 1, q_rot, j + 1)
                if front:
                    pe.wait_ge(hT_ready, i + 1)
                    project(i, GB, ub_done, sg_ready, i)
                if tail:
                    four(k_r, k_posed, qT_ready, j + 1, k_rot, j + 1)
                if front:
                    project(i, GA, ua_done, k_rot, i)
                if tail and prompt:
                    pe.wait_ge(kT_ready, j + 1)
                    for h in range(H):
                        last = mm(T4[:, h, :], kT[:, h, :], qT[:, h, :], start=True, stop=True)
                    last.then_inc(scores_done, 1)
                if front:
                    project(i, GV, uv_done, sig_ready, i + 1)
                if tail and prompt:
                    pe.wait_ge(sm_ready, j + 1)
                    pe.wait_ge(v_ready, j + 1)
                    pe.wait_ge(S_ready, j)
                    pe.wait_ge(y_gated, j)
                    pe.wait_ge(x2_ready, j)
                    pe.wait_ge(h2_ready, j)
                    for h in range(H):
                        mm(inner[:, h, :], sm[:, h, :], v_t[:, P * h:P * h + P], start=True, stop=True)
                        mm(cross[:, h, :], qT[:, h, :], S[:, h, :], start=True, stop=True)
                    pe.wait_ge(kd_ready, j + 1)
                    pe.wait_ge(catB_ready, j)
                    for h in range(H):
                        last = mm(R24[:, h, :], k_d[:, P * h:P * h + P], v_t[:, P * h:P * h + P], start=True, stop=True)
                    last.then_inc(ret_done, 1)
                if tail and not prompt:
                    pe.wait_ge(kT_ready, j + 1)
                    pe.wait_ge(s0_in, 16 * NS)
                    pe.wait_ge(k_rot, NT)
                    pe.wait_ge(sg_ready, NT)
                    for h in range(H):
                        for b in range(NS):
                            last = mm(U[0][:, h * NS + b:h * NS + b + 1], S0[:, b // 2, b % 2, h, :], qT[:, h, b:b + 1], start=True, stop=True)
                    last.then_inc(s_cross_done, 1)
                    pe.wait_ge(crossT_ready, 1)
                    pe.wait_ge(h2_ready, j)
                    for h in range(H):
                        last = tr(cross[0:NS, h, :], crossT[:, h, :], ident[:, :])
                    last.then_inc(cross_posed, 1)
                    pe.wait_ge(kT_ready, NT)
                    pe.wait_ge(sconv_in, 32)
                    pe.wait_ge(vmask_ready, 1)
                    for c in range(CT):
                        pe.wait_ge(cs_half, 2 * (c))
                        for r in range(2):
                            last = tr(T0[:, 128 * r:128 * r + 120], sconv[0:120, r, P * c:P * c + P], ident[0:120, 0:120])
                        last.then_inc(cs_posed, 1)
                        state_product(c)
                    pe.wait_ge(cs_half, 2 * (CT))
                if front:
                    project(i, GQ, uq_done, glu_ready, i + 1)
                if route:
                    rows2_trans(m, hT_ready, min(i + 1, NT) if isinstance(i, int) else i + 1)
                if tail:
                    pe.wait_ge(conv3_ready, j + 1)
                    pe.wait_ge(sm_ready, min(j + 1, TP) if isinstance(j, int) else j + 1)
                    norm_sum(cv, sum1_done, conv_ready, j + 1)
                if front:
                    project(i, GG, ug_done, v_ready, i + 1)
                if route:
                    router(m, min(i, TP) if isinstance(i, int) else i)
                if tail:
                    pe.wait_ge(cen_ready, j + 1)
                    norm_sum(sq, sum2_done, sq_ready, j + 1)
                if front:
                    project(i, GK, uk_done, q_rot, i + 1)
                if tail and not prompt:
                    for n in range(H, 2 * H):
                        state_product(n)
                if tail:
                    four(o_t[:, :, :].rearrange("p h e -> p (h e)"), ret_posed, score_ready, j, ret_ready, j + 1, R24)
                if nxt:
                    x_trans(i + 1)
                if front:
                    four(glu, glu_posed, cnorm_ready, i, glu_ready, i + 1)
                if tail:
                    pe.wait_ge(catA_part, 4 * (j + 1))
                    pe.wait_ge(catB_ready, j + 1)
                    for n in range(2):
                        for k in range(KT):
                            last = mm(R[:, 512 * n:512 * n + 512], cat[:, k, :], w_out[:, k, 512 * n:512 * n + 512],
                                      start=k == 0, stop=k == KT - 1)
                    last.then_inc(wout_done, 1)

            x_trans(0)
            pe.wait_ge(win_in, 16 * 6)
            pe.wait_ge(cvec_ready, 1)
            body(0, tail=False, route=False)
            pe.wait_ge(consts_in, 16 * 10)
            pe.wait_ge(wout_in, 16)
            pe.wait_ge(state_zero, 1)
            body(1, route=False)
            with pe.Fori(2, TP) as i:
                body(i)
            body(TP, nxt=False)
            body(TP + 1, front=False, nxt=False)
            def rows_trans(n, arrived, k, r=0):
                pe.wait_ge(arrived, k)
                pe.wait_ge(xgT_ready, n)
                for c in range(KT):
                    last = tr(Xk[:, c, :], xgs[r].rearrange("p (d k) -> p k d", k=KT)[:, c, :], ident[:, :])
                last.then_inc(xg_posed, 1)

            def up(n, weights):
                pe.wait_ge(xgT_ready, n + 1)
                w13 = weights[:, 0:KT * 2 * DE].rearrange("p (x k n) -> p x k n", x=2, k=KT)
                for k in range(KT):
                    last = mm(U[1][:, :], xgT[:, k, :], w13[:, :, k, :], start=k == 0, stop=k == KT - 1)
                last.then_inc(h_done, 1)

            def hidden_trans(n):
                pe.wait_ge(hid_ready, n + 1)
                for f in range(FT):
                    last = tr(T0[:, P * f:P * f + P], hid.rearrange("p (d f) -> p f d", f=FT)[:, f, :], ident[:, :])
                last.then_inc(hid_posed, 1)

            def down(n, weights):
                pe.wait_ge(hidT_ready, n + 1)
                pe.wait_ge(y_evac, n)
                for half in range(2):
                    for f in range(FT):
                        at = KT * 2 * DE + D * f + 512 * half
                        last = mm(R[:, 512 * half:512 * half + 512], hidT[:, f, :], weights[:, at:at + 512],
                                  start=f == 0, stop=f == FT - 1)
                last.then_inc(y_done, 1)

            def positions():
                pe.wait_ge(pairs_ready, 1)
                pe.wait_ge(score_ready, NT)
                for i in range(NT):
                    o = U[0][:, NE * i:NE * i + NE] if i < TP else pos_last
                    for j in range(i):
                        mm(o, ones_bf, pairs[:, j, :], start=j == 0, stop=False)
                    mm(o, tri_bf, pairs[:, i, :], start=i == 0, stop=True)
                for j in range(NT):
                    last = mm(count, ones_bf, pairs[:, j, :], start=j == 0, stop=j == NT - 1)
                last.then_inc(pos_done, 1)

            pe.wait_ge(shw_in, 48)
            pe.wait_ge(state_upd, 2 * H)
            pe.wait_ge(h2T_ready, TP)
            rows_trans(0, xg_in[0], 16)
            up(0, shw)
            rows2_trans(TP, xgT_ready, 1)
            hidden_trans(0)
            router(TP, TP)
            rows_trans(1, xg_in[1], 16, 1)

            def shared(g, r):
                n = 2 * g + r
                up(n, shw)
                if r == 0:
                    rows_trans(n + 1, xg_in[1], 16 * g + 16, 1)
                else:
                    rows_trans(n + 1, xg_in[0], 16 * g + 32, 0)
                down(n - 1, shw)
                hidden_trans(n)

            shared(0, 1)
            positions()
            with pe.Fori(1, NT // 2) as g:
                shared(g, 0)
                shared(g, 1)
            pe.wait_ge(dest_ready, NT)
            pe.wait_ge(slot_in, 16)
            tr(U[0][:, 0:P], slot_row, ident[:, :]).then_inc(slot_posed, 1)
            pe.wait_ge(blk_ready, 1)
            mm(U[0][0:1, P:2 * P], blk_f, ident[:, :], start=True, stop=True).then_inc(blkrow_posed, 1)
            up(NT - 1, shw)
            down(NT - 2, shw)
            hidden_trans(NT - 1)
            down(NT - 1, shw)
            def weights_of(b, first=True):
                e = pe.value_load(blk_e[0:1, bass.ds(b, 1)], min_val=0, max_val=NE - 1)
                if first:
                    pe.wait_ge(w_ready, e + 1)
                return ring[:, bass.ds(e % RING, 1), :].rearrange("p a w -> p (a w)")

            pe.wait_ge(blkrow_ready, 1)
            last = pe.value_load(pend_i[0:1, NE:], min_val=MINPAIR - 1, max_val=MAXPAIR - 1)

            def routed(g, r, first=False):
                b = 2 * g + r
                up(b + NT, weights_of(b))
                if r == 0:
                    rows_trans(b + NT + 1, gathered[1], 16 * g + 16, 1)
                else:
                    rows_trans(b + NT + 1, gathered[0], 16 * g + 32, 0)
                if not first:
                    down(b + NT - 1, weights_of(b - 1, False))
                hidden_trans(b + NT)

            rows_trans(NT, gathered[0], 16, 0)
            routed(0, 0, True)
            routed(0, 1)
            with pe.Fori(1, MAXPAIR) as g:
                with pe.If(g <= last):
                    routed(g, 0)
                    routed(g, 1)
            down(2 * last + NT + 1, weights_of(2 * last + 1, False))

        @block.scalar
        def _(act):
            act.wait_ge(c_in, 32)
            nc.scalar.activation(xr[0:9, :], xr[0:9, :], ACT.Silu).then_inc(csilu, 1)
            act.wait_ge(csilu, 1)
            act.wait_ge(c_posed, 1)
            nc.scalar.activation(hT[:, :, 0:9], X[:, 0:16 * KT].rearrange("p (k n) -> p k n", k=KT)[:, :, 0:9],
                                 ACT.Copy).then_inc(cT_ready, 1)
            act.wait_ge(cT_ready, 1)

            def norm1(i):
                act.wait_ge(x_in, 16 * (i + 1))
                act.wait_ge(glu_ready, i)
                nc.scalar.activation(junk, x_t[:, :], ACT.Square, accum_out=ssq1).then_inc(norm1_ssq, 1)
                act.wait_ge(norm1_ssq, i + 1)
                act.wait_ge(h_scaled, i)
                nc.scalar.activation(std1, ssq1, ACT.Sqrt, scale=1.0 / D, bias=eps_c[:, 0:1]).then_inc(norm1_std, 1)
                act.wait_ge(norm1_std, i + 1)

            def hT_copy(i):
                act.wait_ge(x_posed, i + 1)
                nc.scalar.activation(hT[:, :, :], Xk, ACT.Copy).then_inc(hT_ready, 1)
                act.wait_ge(hT_ready, i + 1)

            def norm2(m, n):
                act.wait_ge(x2_ready, m + 1)
                act.wait_ge(glu_ready, n)
                nc.scalar.activation(junk, xr[:, :], ACT.Square, accum_out=ssq2).then_inc(norm2_ssq, 1)
                act.wait_ge(norm2_ssq, m + 1)
                nc.scalar.activation(std2, ssq2, ACT.Sqrt, scale=1.0 / D, bias=eps_c[:, 0:1]).then_inc(norm2_std, 1)
                act.wait_ge(norm2_std, m + 1)

            def h2T_copy(m):
                act.wait_ge(h2_posed, m + 1)
                nc.scalar.activation(h2T[:, :, :], Xk, ACT.Copy).then_inc(h2T_ready, 1)
                act.wait_ge(h2T_ready, m + 1)

            def score(m):
                act.wait_ge(router_done, m + 1)
                nc.scalar.activation(sc_t, R2[:, 0:NE], ACT.Sigmoid).then_inc(score_ready, 1)
                act.wait_ge(score_ready, m + 1)

            def body(i, front=True, tail=True, route=True, nxt=True):
                j, m = i - 1, i - 2
                if tail:
                    act.wait_ge(q_posed, j + 1)
                    nc.scalar.activation(qT[:, :, :], T4, ACT.Copy).then_inc(qT_ready, 1)
                    act.wait_ge(qT_ready, j + 1)
                if route:
                    norm2(m, min(i, NT) if isinstance(i, int) else i)
                if front:
                    act.wait_ge(ub_done, i + 1)
                    nc.scalar.activation(sig[:, :], U[0][:, :], ACT.Sigmoid).then_inc(sig_ready, 1)
                    act.wait_ge(sig_ready, i + 1)
                if tail:
                    act.wait_ge(k_posed, j + 1)
                    nc.scalar.activation(kT[:, :, :], T4, ACT.Copy).then_inc(kT_ready, 1)
                    act.wait_ge(kT_ready, j + 1)
                if front:
                    act.wait_ge(uv_done, i + 1)
                    act.wait_ge(ret_done, i)
                    nc.scalar.activation(v_t[:, :], U[0][:, :], ACT.Copy).then_inc(v_ready, 1)
                    act.wait_ge(v_ready, i + 1)
                if nxt:
                    norm1(i + 1)
                prompt = not (isinstance(j, int) and j == TP)
                if tail and not prompt:
                    act.wait_ge(s_cross_done, 1)
                    nc.scalar.activation(crossT, U[0][:, 0:H * NS].rearrange("p (h b) -> p h b", h=H),
                                         ACT.Copy).then_inc(crossT_ready, 1)
                    act.wait_ge(crossT_ready, 1)
                    for c in range(CT):
                        act.wait_ge(cs_posed, c + 1)
                        for r in range(2):
                            nc.scalar.activation(cbuf[:, c, 4 * r:4 * r + 4, 0:CW - 1],
                              T0[:, 128 * r:128 * r + 120].rearrange("p (b w) -> p b w", b=4), ACT.Copy).then_inc(
                                  cs_half, 1)
                            act.wait_ge(cs_half, 2 * c + r + 1)
                if tail:
                    act.wait_ge(gn_var, j + 1)
                    nc.scalar.activation(gstd[:, :], mv[:, :, 1], ACT.Sqrt, bias=eps_c[:, 0:1]).then_inc(gn_std, 1)
                    act.wait_ge(gn_std, j + 1)
                if route:
                    h2T_copy(m)
                if tail:
                    act.wait_ge(cen_ready, j + 1)
                    nc.scalar.activation(sq, cv[:, :, :], ACT.Square).then_inc(sq_ready, 1)
                    act.wait_ge(sq_ready, j + 1)
                if route:
                    score(m)
                if tail:
                    act.wait_ge(sum2_done, j + 1)
                    nc.scalar.activation(T0[:, P:2 * P], T0[:, 0:P], ACT.Sqrt, bias=eps_c[:, 0:1]).then_inc(std_c, 1)
                    act.wait_ge(std_c, j + 1)
                if front:
                    act.wait_ge(ug_done, i + 1)
                    act.wait_ge(ret_ready, i)
                    nc.scalar.activation(sg[:, :], U[0][:, :], ACT.Silu).then_inc(sg_ready, 1)
                    act.wait_ge(sg_ready, i + 1)
                if tail:
                    act.wait_ge(cnorm_ready, j + 1)
                    act.wait_ge(router_done, m + 1)
                    for c in range(CT):
                        nc.scalar.activation(cat[:, c, :], cv[:, c, :], ACT.Silu, scale=cvec[:, CT + c:CT + c + 1],
                                             bias=cvec[:, 2 * CT + c:2 * CT + c + 1]).then_inc(catA_part, 1)
                        act.wait_ge(catA_part, 4 * j + c + 1)
                if tail:
                    act.wait_ge(ret_posed, j + 1)
                    nc.scalar.activation(cat[:, CT:, :], R24, ACT.Copy).then_inc(catB_ready, 1)
                    act.wait_ge(catB_ready, j + 1)
                if nxt:
                    hT_copy(i + 1)
                if front:
                    act.wait_ge(glu_posed, i + 1)
                    act.wait_ge(win_shifted, i)
                    nc.scalar.activation(win[:, :, CW - 1:], T4, ACT.Copy).then_inc(win_ready, 1)
                    act.wait_ge(win_ready, i + 1)

            act.wait_ge(state_zero, 1)
            norm1(0)
            hT_copy(0)
            body(0, tail=False, route=False)
            body(1, route=False)
            with act.Fori(2, TP) as i:
                body(i)
            body(TP, nxt=False)
            body(TP + 1, front=False, nxt=False)

            def blk_T(n):
                act.wait_ge(xg_posed, n + 1)
                nc.scalar.activation(xgT[:, :, :], Xk, ACT.Copy).then_inc(xgT_ready, 1)

            def blk_silu(n):
                act.wait_ge(h_done, n + 1)
                act.wait_ge(hid_ready, n)
                nc.scalar.activation(hsil, U[1][:, 0:DE], ACT.Silu).then_inc(silu_ready, 1)

            blk_T(0)
            norm2(TP, NT)
            h2T_copy(TP)
            act.wait_ge(ret_ready, NT)
            blk_silu(0)
            score(TP)
            blk_T(1)
            with act.Fori(1, NT - 1) as n:
                blk_silu(n)
                blk_T(n + 1)
            blk_silu(NT - 1)
            blk_T(NT)
            act.wait_ge(blkrow_ready, 1)
            last = act.value_load(pend_i[0:1, NE:], min_val=MINPAIR - 1, max_val=MAXPAIR - 1)
            with act.Fori(0, MAXPAIR) as g:
                with act.If(g <= last):
                    for r in range(2):
                        blk_silu(2 * g + r + NT)
                        blk_T(2 * g + r + NT + 1)

            def last_norm(i, x, ready, n, ssq, std, rows=P):
                act.wait_ge(ready, n)
                nc.scalar.activation(junk[0:rows, :], x[0:rows], ACT.Square, accum_out=ssq[0:rows, :]).then_inc(fin_ssq, 1)
                act.wait_ge(fin_ssq, i + 1)
                nc.scalar.activation(std[0:rows, :], ssq[0:rows, :],
                                     ACT.Sqrt, scale=1.0 / D, bias=eps_c[0:rows, 0:1]).then_inc(fin_std, 1)
                act.wait_ge(fin_std, i + 1)

            with act.Fori(0, TP // 2) as g:
                for r in range(2):
                    last_norm(2 * g + r, x3[r], x3_ready, 2 * g + r + 1, ssq1, std1)
            last_norm(TP, x3_s, x3s_ready, 1, ssq2, std2, NS)

        @block.vector
        def _(dve):
            v = nc.vector
            own = Steps(dve, dve_step)
            link = own.link

            link(v.memset(win[:, :, 0:CW - 1], 0.0))
            link(v.memset(ones64[:, :], 1.0))
            link(v.memset(mk_all[:, TP, :], 0.0))
            link(v.memset(eps_c[:, :], EPS))
            v.memset(S[:, :, :], 0.0).then_inc(state_zero, 1)
            dve.wait_ge(state_zero, 1)

            def norm1(i):
                dve.wait_ge(norm1_std, i + 1)
                link(v.reciprocal(rstd1, std1))
                if isinstance(i, int) and i == TP:
                    dve.wait_ge(smod1_in, 32)
                v.scalar_tensor_tensor(x_t[:, :], x_t[:, :], rstd1, A_m, ALU.mult, ALU.mult).then_inc(h_scaled, 1)
                dve.wait_ge(h_scaled, i + 1)

            dve.wait_ge(bada_in, 48)
            for ch in range(12):
                dve.wait_ge(ada_done, ch + 1)
                o = mod_sb[:, 512 * ch:512 * ch + 512]
                ins = v.tensor_tensor(o, U[ch % 2][0:9, :], o, ALU.add)
                if ch // 2 in (1, 4):
                    link(ins)
                    at = D * (ch // 8) + 512 * (ch % 2)
                    ins = v.scalar_tensor_tensor(o, o, 1.0, gains[:, at:at + 512], ALU.add, ALU.mult)
                ins.then_inc(mod_ready, 1)
                dve.wait_ge(mod_ready, ch + 1)
            dve.wait_ge(modab_in, 32)
            norm1(0)
            dve.wait_ge(cvec_posed, 1)
            link(v.tensor_copy(cw[:, :, :], T0[:, 0:P].rearrange("p (c w) -> p c w", c=CT)[:, :, 0:CW]))
            v.tensor_copy(cvec[:, :], T0[:, P:P + 12]).then_inc(cvec_ready, 1)
            dve.wait_ge(cvec_ready, 1)
            dve.wait_ge(consts_in, 16 * 10)

            def rotate(o, bank, done, i):
                u = U[bank][:, :].rearrange("p (g d) -> p g d", d=HD // 2)
                uh = U[bank][:, :].rearrange("p (h z d) -> p h z d", h=H, z=2)
                th = rt2[:, :].rearrange("p (h z d) -> p h z d", h=H, z=2)
                half = [P, H, HD // 2]
                v.tensor_tensor(o[:, :].rearrange("p (g d) -> p g d", d=HD // 2), u,
                                rope[:, 0, :].unsqueeze(1).to_broadcast([P, 2 * H, HD // 2]), ALU.mult)
                v.tensor_tensor(th[:, :, 0, :], uh[:, :, 1, :], rope[:, 1, :].unsqueeze(1).to_broadcast(half), ALU.mult)
                link(v.tensor_tensor(th[:, :, 1, :], uh[:, :, 0, :], rope[:, 2, :].unsqueeze(1).to_broadcast(half), ALU.mult))
                v.tensor_tensor(o[:, :], o[:, :], rt2[:, :], ALU.add).then_inc(done, 1)
                dve.wait_ge(done, i + 1)

            def conv(first, last):
                for w in range(first, last):
                    for c in range(CT - 1):
                        if w == 0:
                            ins = v.tensor_scalar(cv[:, c, :], win[:, c, 0:P], cw[:, c, 0:1], cvec[:, c:c + 1], ALU.mult, ALU.add)
                        else:
                            dve.wait_ge(dve_step, own.base + conv_step[c])
                            ins = v.scalar_tensor_tensor(cv[:, c, :], win[:, c, w:w + P], cw[:, c, w:w + 1], cv[:, c, :],
                                                         ALU.mult, ALU.add)
                        if w < CW - 1:
                            own.add(ins)
                            conv_step[c] = own.k
                return ins

            conv_step = [0] * (CT - 1)

            def residual(m):
                dve.wait_ge(wout_done, m + 1)
                if isinstance(m, int) and m == TP:
                    dve.wait_ge(smod2_in, 16)
                v.tensor_tensor(R[:, :], R[:, :], gt_m, ALU.mult).then_inc(y_gated, 1)
                dve.wait_ge(y_gated, m + 1)
                dve.wait_ge(xr_in, 16 * (m + 1))
                v.tensor_tensor(xr[:, :], R[:, :], xr[:, :], ALU.add).then_inc(x2_ready, 1)
                dve.wait_ge(x2_ready, m + 1)

            def norm2(m):
                dve.wait_ge(norm2_std, m + 1)
                link(v.reciprocal(rstd2, std2))
                if isinstance(m, int) and m == TP:
                    dve.wait_ge(smod3_in, 32)
                link(v.scalar_tensor_tensor(R[:, :], xr[:, :], rstd2, A_f, ALU.mult, ALU.mult))
                dve.wait_ge(x2_stored, 16 * (m + 1))
                v.tensor_tensor(xr[:, :], R[:, :], B_f, ALU.add).then_inc(h2_ready, 1)
                dve.wait_ge(h2_ready, m + 1)

            def top_k(m):
                dve.wait_ge(score_ready, m + 1)
                g3 = [P, NG, PER]
                link(v.tensor_tensor(sel, sc_t, bias_r[:, :], ALU.add))
                v.memset(scrap[:, :], 0.0)
                for g in range(NG):
                    ins = v.max(top8s[:, PER * g:PER * g + PER], sel[:, PER * g:PER * g + PER])
                link(ins)
                tops = top8s.rearrange("p (g e) -> p g e", g=NG)
                link(v.tensor_tensor(gsum, tops[:, :, 0], tops[:, :, 1], ALU.add))
                this, other = bc(gsum, g3), gsum.unsqueeze(1).to_broadcast(g3)
                pa, pb = (x.rearrange("p (g e) -> p g e", g=NG) for x in (pair_a, pair_b))
                v.tensor_tensor(pa, other, this, ALU.is_gt)
                link(v.tensor_tensor(pb, other, this, ALU.is_equal))
                link(v.tensor_tensor(pb, pb, lt[:, :, :], ALU.mult))
                link(v.tensor_tensor(pa, pa, pb, ALU.add))
                link(v.tensor_reduce(rank, pa, AX.X, ALU.add))
                link(v.tensor_scalar(keep, rank, float(TOPG), None, ALU.is_lt))
                link(v.tensor_scalar(pen, keep, BIG, -BIG, ALU.mult, ALU.add))
                s3 = sel.rearrange("p (g e) -> p g e", g=NG)
                link(v.tensor_tensor(s3, s3, bc(keep, g3), ALU.mult))
                link(v.tensor_tensor(s3, s3, bc(pen, g3), ALU.add))
                v.memset(scrap[:, :], 0.0)
                link(v.max(t8, sel))
                th = t8[:, TOPK - 1:TOPK]
                link(v.tensor_scalar(pair_a, sel, th, None, ALU.is_gt))
                link(v.tensor_reduce(ngt, pair_a, AX.X, ALU.add))
                v.tensor_scalar(need, ngt, -1.0, float(TOPK), ALU.mult, ALU.add)
                link(v.tensor_scalar(pair_b, sel, th, None, ALU.is_equal))
                link(v.tensor_tensor_scan(top8s, ones64[:, :], pair_b, 0.0, ALU.mult, ALU.add))
                link(v.scalar_tensor_tensor(pair_b, top8s, need, pair_b, ALU.is_le, ALU.mult))
                link(v.tensor_tensor(pick, pair_a, pair_b, ALU.add))
                v.tensor_tensor(wfull, pick, sc_t, ALU.mult)
                link(v.tensor_tensor_scan(top8s, ones64[:, :], pick, 0.0, ALU.mult, ALU.add))
                link(v.tensor_reduce(wsum, wfull, AX.X, ALU.add))
                link(v.reciprocal(wrec, wsum))
                own.add(v.tensor_scalar(wfull, wfull, wrec, 2.5, ALU.mult, ALU.mult))
                link(v.tensor_tensor(top8s, top8s, pick, ALU.mult))
                if isinstance(m, int) and m == TP:
                    v.tensor_copy(mk_all[0:NS, TP, :], top8s[0:NS, :])
                else:
                    v.tensor_copy(mk_all[:, bass.ds(m, 1), :].rearrange("p a e -> p (a e)"), top8s)

            def weights_by_k(m):
                o6 = w6[:, TP, :] if isinstance(m, int) and m == TP else w6[:, bass.ds(m, 1), :].rearrange("p a k -> p (a k)")
                dve.wait_ge(sum2_done, min(m + 2, NT) if isinstance(m, int) else m + 2)
                six = [P, TOPK, NE]
                link(v.tensor_tensor(eq_k, top8s.unsqueeze(1).to_broadcast(six), bc(kconst[:, 0:TOPK], six), ALU.is_equal))
                link(v.tensor_tensor(eq_k, eq_k, wfull.unsqueeze(1).to_broadcast(six), ALU.mult))
                v.tensor_reduce(o6, eq_k, AX.X, ALU.add).then_inc(topk_done, 1)
                dve.wait_ge(topk_done, m + 1)

            def state_update(n):
                h, half = n // 2, n % 2
                dve.wait_ge(state_mm, n + 1)
                new = U[n % 2][:, :].rearrange("p (k c e) -> p k c e", k=2, c=2)
                for k in range(2):
                    sl = S0[:, 2 * half + k, :, h, :]
                    ins = v.scalar_tensor_tensor(sl, sl, float(GAMMA[h]), new[:, k], ALU.mult, ALU.add)
                ins.then_inc(state_upd, 1)
                dve.wait_ge(state_upd, n + 1)

            def body(i, front=True, tail=True, route=True, nxt=True):
                j, m = i - 1, i - 2
                prompt = not (isinstance(j, int) and j == TP)
                h3, c3 = [P, H, HD], [P, CT, P]
                if tail and prompt:
                    dve.wait_ge(win_ready, j + 1)
                    dve.wait_ge(catA_part, 4 * j)
                    conv(0, TAPS[0])
                if route:
                    residual(m)
                if tail and prompt:
                    conv(TAPS[0], TAPS[1])
                if route:
                    norm2(m)
                if tail and prompt:
                    conv(TAPS[1], TAPS[2])
                if front:
                    dve.wait_ge(ua_done, i + 1)
                    dve.wait_ge(sig_ready, i + 1)
                    if isinstance(i, int) and i == TP:
                        dve.wait_ge(glu_last_out, 16)
                    v.tensor_tensor(glu[:, :], U[1][:, :], sig[:, :], ALU.mult).then_inc(glu_ready, 1)
                    dve.wait_ge(glu_ready, i + 1)
                if tail and prompt:
                    v.tensor_tensor(k_d[:, :].rearrange("p (h d) -> p h d", h=H), k_r[:, :].rearrange("p (h d) -> p h d", h=H),
                                    bc(k_dec, h3), ALU.mult).then_inc(kd_ready, 1)
                    dve.wait_ge(kd_ready, j + 1)
                    dve.wait_ge(scores_done, j + 1)
                    v.tensor_tensor(sm[:, :, :], T4, maskT[:, :, :], ALU.mult).then_inc(sm_ready, 1)
                    dve.wait_ge(sm_ready, j + 1)
                    conv(TAPS[2], TAPS[3])
                    dve.wait_ge(ret_done, j + 1)
                    v.tensor_tensor(o_t[:, :, :], cross, bc(q_dec, h3), ALU.mult)
                    for h in range(H):
                        ins = v.scalar_tensor_tensor(S[:, h, :], S[:, h, :], float(GAMMA[h] ** P), R24[:, h, :], ALU.mult, ALU.add)
                    link(ins)
                    ins = v.tensor_tensor(o_t[:, :, :], o_t[:, :, :], inner, ALU.add)
                    ins.then_inc(S_ready, 1)
                    dve.wait_ge(S_ready, j + 1)
                if tail and not prompt:
                    link(v.tensor_tensor(qk_prod, q_r[:, :].rearrange("p (h d) -> p h d", h=H),
                                         k_r[:, :].rearrange("p (h d) -> p h d", h=H), ALU.mult))
                    link(v.tensor_reduce(qk, qk_prod, AX.X, ALU.add))
                    link(v.tensor_scalar(qk, qk, HD ** -0.5, None, ALU.mult))
                    dve.wait_ge(v_ready, NT)
                    vh = v_t[0:NS, :].rearrange("p (h d) -> p h d", h=H)
                    for b in range(NS):
                        ins = v.tensor_scalar(vmask[:, b // 2, b % 2, :], v_t[0:NS, :], ident[0:NS, b:b + 1], None, ALU.mult)
                    ins.then_inc(vmask_ready, 1)
                    dve.wait_ge(vmask_ready, 1)
                    n3 = [NS, H, HD]
                    link(v.tensor_tensor(qk_prod[0:NS], vh, bc(qk[0:NS, :], n3), ALU.mult))
                    dve.wait_ge(cross_posed, 1)
                    link(v.tensor_tensor(o_t[0:NS], cross[0:NS], bc(s_dec[0:NS, :], n3), ALU.mult))
                    v.tensor_tensor(o_t[0:NS], o_t[0:NS], qk_prod[0:NS], ALU.add).then_inc(sret_ready, 1)
                    dve.wait_ge(sret_ready, 1)
                    for n in range(H):
                        state_update(n)
                    dve.wait_ge(cs_half, 2 * (CT))
                    dve.wait_ge(win_ready, NT)
                    dve.wait_ge(catA_part, 4 * (j))
                    link(v.tensor_copy(cbuf[:, :, :, CW - 1], win[:, :, CW - 1:CW - 1 + NS]))
                    for c in range(CT):
                        link(v.tensor_tensor(cprod, cbuf[:, c], cw[:, c, :].unsqueeze(1).to_broadcast([P, NS, CW]), ALU.mult))
                        link(v.tensor_reduce(cv[:, c, 0:NS], cprod, AX.X, ALU.add))
                        ins = v.tensor_scalar(cv[:, c, 0:NS], cv[:, c, 0:NS], cvec[:, c:c + 1], None, ALU.add)
                        if c < CT - 1:
                            link(ins)
                    ins.then_inc(conv_ready, 1)
                    dve.wait_ge(conv_ready, j + 1)
                    dve.wait_ge(sret_ready, 1)
                if tail:
                    for h in range(H):
                        ins = v.bn_stats(bn[:, h, :], o_t[:, h, :])
                    link(ins)
                    v.memset(scrap[:, :], 0.0)
                    for h in range(H):
                        ins = v.bn_aggr(mv[:, h, :], bn[:, h, :])
                    ins.then_inc(gn_var, 1)
                    dve.wait_ge(gn_var, j + 1)
                if nxt:
                    norm1(i + 1)
                if tail and prompt:
                    conv(TAPS[3], CW).then_inc(conv_ready, 1)
                    dve.wait_ge(conv_ready, j + 1)
                    dve.wait_ge(conv3_ready, j + 1)
                    v.tensor_copy(win[:, :, 0:CW - 1], win[:, :, P:P + CW - 1]).then_inc(win_shifted, 1)
                    dve.wait_ge(win_shifted, j + 1)
                if tail:
                    dve.wait_ge(gn_std, j + 1)
                    link(v.reciprocal(gstd[:, :], gstd[:, :]))
                    for h in range(H):
                        ins = v.tensor_scalar(o_t[:, h, :], o_t[:, h, :], mv[:, h, 0:1], gstd[:, h:h + 1], ALU.subtract, ALU.mult)
                    ins.then_inc(gn_ready, 1)
                    dve.wait_ge(gn_ready, j + 1)
                if front:
                    dve.wait_ge(uq_done, i + 1)
                    dve.wait_ge(rope_in, 16 * (i + 1))
                    rotate(q_r, 1, q_rot, i)
                if tail:
                    dve.wait_ge(sum1_done, j + 1)
                    v.tensor_tensor(cv[:, :, :], cv[:, :, :], T0[:, 0:P].unsqueeze(1).to_broadcast(c3),
                                    ALU.subtract).then_inc(cen_ready, 1)
                    dve.wait_ge(cen_ready, j + 1)
                if tail:
                    dve.wait_ge(std_c, j + 1)
                    link(v.reciprocal(T0[:, P:2 * P], T0[:, P:2 * P]))
                    dve.wait_ge(sq_ready, j + 1)
                    v.tensor_tensor(cv[:, :, :], cv[:, :, :], T0[:, P:2 * P].unsqueeze(1).to_broadcast(c3),
                                    ALU.mult).then_inc(cnorm_ready, 1)
                    dve.wait_ge(cnorm_ready, j + 1)
                if tail and not prompt:
                    for n in range(H, 2 * H):
                        state_update(n)
                if route:
                    top_k(m)
                    weights_by_k(m)
                if front:
                    dve.wait_ge(uk_done, i + 1)
                    rotate(k_r, 1, k_rot, i)

            body(0, tail=False, route=False)
            dve.wait_ge(modv_in, 48)
            body(1, route=False)
            before = own.base + own.k
            with dve.Fori(2, TP - 1) as i:
                own.at((i - 2) * DVE_LOOP + before)
                body(i)
                assert own.k == DVE_LOOP, own.k
            own.at(before + DVE_LOOP * (TP - 3))
            body(TP - 1)
            body(TP, nxt=False)
            body(TP + 1, front=False, nxt=False)

            def blk_hid(n):
                dve.wait_ge(silu_ready, n + 1)
                v.tensor_tensor(hid, U[1][:, DE:2 * DE], hsil, ALU.mult).then_inc(hid_ready, 1)

            def blk_hidT(n):
                dve.wait_ge(hid_posed, n + 1)
                v.tensor_copy(hidT, T0[:, 0:DE].rearrange("p (f n) -> p f n", f=FT)).then_inc(hidT_ready, 1)

            def blk_y(n, stored, k, r=0):
                dve.wait_ge(y_done, n + 1)
                dve.wait_ge(stored, k)
                v.tensor_copy(y_sbs[r], R[:, :]).then_inc(y_evac, 1)

            def shared_y(n):
                dve.wait_ge(y_done, n + 1)
                dve.wait_ge(ysh_stored, 16 * n)
                link(v.tensor_tensor(y_sb_b, R[:, :], gt_f, ALU.mult))
                dve.wait_ge(x2_in, 16 * n + 16)
                v.tensor_tensor(y_sb_b, y_sb_b, x2c, ALU.add).then_inc(y_evac, 1)

            def shared(n):
                blk_hid(n)
                shared_y(n - 1)
                blk_hidT(n)

            residual(TP)
            norm2(TP)
            blk_hid(0)
            blk_hidT(0)
            top_k(TP)
            weights_by_k(TP)
            dve.wait_ge(tri_in, 32)
            dve.wait_ge(q_posed, NT)
            dve.wait_ge(catA_part, 4 * NT)
            v.memset(ones_bf, 1.0)
            link(v.tensor_copy(tri_bf, tri_f))
            v.tensor_scalar(pairs, mk_all[:, :, :], 0.0, None, ALU.is_gt).then_inc(pairs_ready, 1)
            dve.wait_ge(pairs_ready, 1)
            dve.wait_ge(gtf_in, 16)
            shared(1)
            dve.wait_ge(pos_done, 1)
            link(v.tensor_scalar(cnt_f, count, 1.0, float(P - 1), ALU.max, ALU.add))
            link(v.tensor_copy(cnt_i, cnt_f))
            link(v.tensor_scalar(cnt_i, cnt_i, 7, None, ALU.arith_shift_right))
            link(v.tensor_copy(nblk, cnt_i))
            link(v.tensor_tensor_scan(pend, ones64[:, :], nblk, 0.0, ALU.mult, ALU.add))
            link(v.tensor_tensor(pbase, pend, nblk, ALU.subtract))
            link(v.tensor_scalar(pbase, pbase, float(P), None, ALU.mult))
            link(v.tensor_copy(pend_i[:, 0:NE], pend[0:1, :]))
            link(v.tensor_scalar(pend_i[:, NE:], pend[0:1, NE - 1:NE], -1.0, None, ALU.add))
            link(v.tensor_scalar(pend_i[:, NE:], pend_i[:, NE:], 1, None, ALU.arith_shift_right))
            link(v.tensor_scalar(blk_cmp, pend, blk_no[:, 0:1], None, ALU.is_le))
            link(v.tensor_reduce(blk_f, blk_cmp, AX.X, ALU.add))
            v.tensor_scalar(blk_f, blk_f, float(NE - 1), None, ALU.min).then_inc(blk_ready, 1)
            dve.wait_ge(blk_ready, 1)

            def slots(i):
                it = bass.ds(i, 1)
                pos = pos_last if isinstance(i, int) and i == TP else U[0][:, bass.ds(i * NE, NE)]
                six = [P, TOPK, NE]
                v.tensor_tensor(eq_k, mk_all[:, it, :].to_broadcast(six), bc(kconst[:, 0:TOPK], six), ALU.is_equal)
                link(v.tensor_tensor(dest, pos, pbase, ALU.add))
                link(v.tensor_tensor(eq_k, eq_k, dest.unsqueeze(1).to_broadcast(six), ALU.mult))
                link(v.tensor_reduce(dst_f[:, 0:TOPK], eq_k, AX.X, ALU.add))
                v.tensor_copy(dst_i[:, it, 0:TOPK].rearrange("p a k -> p (a k)"), dst_f[:, 0:TOPK]).then_inc(dest_ready, 1)
                dve.wait_ge(dest_ready, i + 1)

            slots(0)
            slots(1)
            before = own.base + own.k
            with dve.Fori(2, NT // 2 + 1) as n:
                own.at((n - 2) * 7 + before)
                slots(2 * n - 2)
                slots(2 * n - 1)
                shared(n)
                assert own.k == 7, own.k
            own.at(before + 7 * (NT // 2 - 1))
            slots(TP)
            before = own.base + own.k
            with dve.Fori(NT // 2 + 1, NT - 1) as n:
                own.at(n - (NT // 2 + 1) + before)
                shared(n)
            own.at(before + NT - 1 - (NT // 2 + 1))
            dve.wait_ge(slot_posed, 1)
            dve.wait_ge(blkrow_posed, 1)
            link(v.tensor_copy(slot_i, U[0][:, 0:P]))
            v.tensor_scalar(tok_i, slot_i, 3, None, ALU.arith_shift_right).then_inc(slot_ready, 1)
            dve.wait_ge(slot_ready, 1)
            v.tensor_copy(blk_e, U[0][0:1, P:2 * P]).then_inc(blkrow_ready, 1)
            dve.wait_ge(blkrow_ready, 1)
            shared(NT - 1)
            dve.wait_ge(gtf_in, 32)
            shared_y(NT - 1)
            dve.wait_ge(blkrow_ready, 1)
            dve.wait_ge(h2_stored, 16 * NT)
            last = dve.value_load(pend_i[0:1, NE:], min_val=MINPAIR - 1, max_val=MAXPAIR - 1)
            dve.wait_ge(ysh_stored, 16 * NT)

            def routed(g, r, first=False):
                b = 2 * g + r
                blk_hid(b + NT)
                if not first:
                    if r == 0:
                        blk_y(b + NT - 1, scattered[1], 16 * g - 16, 1)
                    else:
                        blk_y(b + NT - 1, scattered[0], 16 * g, 0)
                blk_hidT(b + NT)

            routed(0, 0, True)
            routed(0, 1)
            routed(1, 0)
            routed(1, 1)
            with dve.Fori(2, MAXPAIR) as g:
                with dve.If(g <= last):
                    routed(g, 0)
                    routed(g, 1)
            blk_y(2 * last + 1 + NT, scattered[1], 16 * last, 1)

            def finish(i, r, g):
                dve.wait_ge(fin_std, i + 1)
                link(v.reciprocal(rstd1, std1))
                dve.wait_ge(fin_stored[r], 16 * g)
                v.scalar_tensor_tensor(fin[r], x3[r], rstd1, g_fin, ALU.mult, ALU.mult).then_inc(fin_ready[r], 1)
                dve.wait_ge(fin_ready[r], g + 1)

            def combine(i, r, g, before=True):
                dve.wait_ge(rows_in[r], 16 * (g + 1))
                acc = yk[r][:, 0, :]
                for k in range(TOPK):
                    w = w6[:, bass.ds(i, 1), k:k + 1].rearrange("p a k -> p (a k)")
                    if k == 0:
                        link(v.tensor_scalar(acc, acc, w, None, ALU.mult))
                    else:
                        link(v.scalar_tensor_tensor(acc, yk[r][:, k, :], w, acc, ALU.mult, ALU.add))
                    if k == TOPK // 2 and before:
                        finish(i - 1, 1 - r, g - 1 + r)
                link(v.tensor_tensor(acc, acc, gt_f, ALU.mult))
                v.tensor_tensor(x3[r], acc, yk[r][:, 6, :], ALU.add).then_inc(x3_ready, 1)
                dve.wait_ge(x3_ready, i + 1)

            dve.wait_ge(finv_in, 32)
            combine(0, 0, 0, before=False)
            combine(1, 1, 0)
            for r in range(2):
                combine(2 + r, r, 1)
            before = own.base + own.k
            with dve.Fori(2, TP // 2) as g:
                own.at((g - 2) * 16 + before)
                for r in range(2):
                    combine(2 * g + r, r, g)
                assert own.k == 16
            own.at(before + 16 * (TP // 2 - 2))
            finish(TP - 1, 1, TP // 2 - 1)
            dve.wait_ge(fin_std, NT)
            link(v.reciprocal(rstd2[0:NS, :], std2[0:NS, :]))
            v.scalar_tensor_tensor(fin_s, x3_s, rstd2[0:NS, :], g_fin[0:NS, :], ALU.mult, ALU.mult).then_inc(sample_ready, 1)

        @block.gpsimd
        def _(pool):
            g_ = nc.gpsimd
            own = Steps(pool, pool_step)

            def shift(i):
                pool.wait_ge(h_scaled, i + 1)
                g_.tensor_tensor(x_t[:, :], x_t[:, :], B_m, ALU.add).then_inc(h_ready, 1)

            def ret_out(j):
                o = o_t[:, :, :].rearrange("p h e -> p (h e)")
                pool.wait_ge(gn_ready, j + 1)
                own.link(g_.tensor_tensor(o, o, gret[:, 0, :], ALU.mult))
                own.link(g_.tensor_tensor(o, o, gret[:, 1, :], ALU.add))
                pool.wait_ge(sg_ready, j + 1)
                g_.tensor_tensor(o, o, sg[:, :], ALU.mult).then_inc(ret_ready, 1)

            def conv3(j):
                c = CT - 1
                pool.wait_ge(win_ready, j + 1)
                pool.wait_ge(catA_part, 4 * j)
                def tap(w):
                    return cw[:, c, w:w + 1].to_broadcast([P, P])

                g_.tensor_tensor(cv[:, c, :], win[:, c, 0:P], tap(0), ALU.mult)
                for w in range(1, CW):
                    own.link(g_.tensor_tensor(prod[:, :], win[:, c, w:w + P], tap(w), ALU.mult))
                    own.link(g_.tensor_tensor(cv[:, c, :], cv[:, c, :], prod[:, :], ALU.add))
                ins = g_.tensor_tensor(cv[:, c, :], cv[:, c, :], cvec[:, c:c + 1].to_broadcast([P, P]), ALU.add)
                ins.then_inc(conv3_ready, 1)

            shift(0)
            shift(1)
            pool.wait_ge(cvec_ready, 1)
            conv3(0)
            shift(2)
            ret_out(0)
            before = own.k
            with pool.Fori(2, TP) as i:
                own.at((i - 2) * POOL_LOOP + before)
                conv3(i - 1)
                shift(i + 1)
                ret_out(i - 1)
                assert own.k == POOL_LOOP, own.k
            own.at(before + (TP - 2) * POOL_LOOP)
            conv3(TP - 1)
            ret_out(TP - 1)
            pool.sem_inc(conv3_ready, 1)
            ret_out(TP)
            pool_steps = own.base + own.k

            pool.wait_ge(cen_ready, NT)
            pool.wait_ge(catA_part, 4 * (NT))
            g_.memset(pad_row, float(8 * (ROWS - 1))).then_inc(pad_ready, 1)
            pool.wait_ge(table_filled, 16)
            for i in range(NT):
                pool.wait_ge(dest_ready, i + 1)
                rows = P if i < TP else NS
                for k in range(TOPK):
                    pool.indirect_dma_start(slot_tab, bass.IndirectOffsetOnAxis(ap=dst_i[0:rows, i, k:k + 1], axis=0),
                                            slot_val[0:rows, i, k:k + 1], None, bounds_check=NSLOT - 1,
                                            oob_is_err=False).then_inc(slots_out, 16)

            def gather(g, r):
                first = isinstance(g, int) and 2 * g + r == 0
                pool.wait_ge(xg_posed, NT if first else 2 * g + r + NT - 1)
                g_.tensor_copy(tok_cur[:, r:r + 1], tok_i[:, bass.ds(2 * g + r, 1)]).then_inc(tok_ready, 1)
                pool.wait_ge(tok_ready, 2 * g + r + 1)
                pool.sem_inc(pool_free, 1)
                pool.indirect_dma_start(xgs[r], None, h2_rows, bass.IndirectOffsetOnAxis(ap=tok_cur[:, r:r + 1], axis=0),
                                        bounds_check=TOKENS - 1, oob_is_err=False).then_inc(gathered[r], 16)

            def scatter(g, r):
                pool.wait_ge(y_evac, 2 * g + r + NT + 1)
                g_.tensor_copy(slot_cur[:, r:r + 1], slot_i[:, bass.ds(2 * g + r, 1)]).then_inc(slot_picked, 1)
                pool.wait_ge(slot_picked, 2 * g + r + 1)
                pool.sem_inc(pool_free, 1)
                pool.indirect_dma_start(y_rows, bass.IndirectOffsetOnAxis(ap=slot_cur[:, r:r + 1], axis=0), y_sbs[r], None,
                                        bounds_check=8 * TOKENS - 1, oob_is_err=False).then_inc(scattered[r], 16)

            pool.wait_ge(slot_ready, 1)
            pool.wait_ge(blkrow_ready, 1)
            last = pool.value_load(pend_i[0:1, NE:], min_val=MINPAIR - 1, max_val=MAXPAIR - 1)
            gather(0, 0)
            gather(0, 1)
            gather(1, 0)
            gather(1, 1)
            scatter(0, 0)
            with pool.Fori(1, MAXPAIR) as g:
                with pool.If(g <= last):
                    gather(g + 1, 0)
                    scatter(g - 1, 1)
                    gather(g + 1, 1)
                    scatter(g, 0)
            scatter(last, 1)

            own.at(pool_steps)
            pool.wait_ge(sample_in, 32)
            for k in range(TOPK):
                ins = g_.tensor_tensor(yk_s[:, k, :], yk_s[:, k, :], w6[0:NS, TP, k:k + 1].to_broadcast([NS, D]), ALU.mult)
            own.link(ins)
            for k in range(1, TOPK):
                own.link(g_.tensor_tensor(yk_s[:, 0, :], yk_s[:, 0, :], yk_s[:, k, :], ALU.add))
            own.link(g_.tensor_tensor(yk_s[:, 0, :], yk_s[:, 0, :], gt_s, ALU.mult))
            g_.tensor_tensor(x3_s, yk_s[:, 0, :], yk_s[:, 6, :], ALU.add).then_inc(x3s_ready, 1)


GAMMA = [1.0 - 2.0 ** (-5.0 - h) for h in range(H)]
TAPS = (17, 21, 26, 29)
DVE_LOOP = 124
POOL_LOOP = 2 * (CW - 1) + 2


def constants():
    f = np.float32
    pos = np.concatenate([np.arange(SEQ), np.full(NS, PAST), np.zeros(ROWS - TOKENS)]).astype(f)
    inv = (10000.0 ** (-np.arange(HD // 2) / (HD // 2))).astype(f)
    ang = pos[:, None] * inv[None, :]
    cos, sin = np.cos(ang.astype(np.float64)), np.sin(ang.astype(np.float64))
    i = np.arange(P, dtype=np.float64)
    gam = np.array(GAMMA)
    rel = i[None, :] - i[:, None]
    mask = np.where(rel[:, None, :] >= 0, gam[None, :, None] ** np.maximum(rel, 0)[:, None, :], 0.0) * HD ** -0.5
    rows = np.concatenate([gam[None, :] ** (i[:, None] + 1) * HD ** -0.5, gam[None, :] ** (P - 1 - i[:, None]),
                           np.tile(gam[None, :] * HD ** -0.5, (P, 1))], 1)
    g = np.arange(NG)
    token = np.arange(ROWS).reshape(NT, P).T
    return {
        "ident": np.eye(P), "mean_w": np.full((P, P), 1.0 / DC), "tri": np.triu(np.ones((P, P)), 1), "maskT": mask,
        "rows_c": rows, "lt": np.tile((g[None, :] < g[:, None])[None], (P, 1, 1)), "kconst": np.tile(1.0 + g[None, :], (P, 1)),
        "rope": np.stack([cos, -sin, sin], 1), "slot_val": 8 * token[:, :, None] + g[None, None, :], "blk_no": i[:, None],
    }


OUTS = {
    "y_prompt": (1, SEQ, D), "y_sample": (NS, 1, D), "new_conv_prompt": (1, 1, CW - 1, DC), "new_ret_prompt": (1, 1, H, HD, HD),
    "new_conv_sample": (1, NS, CW - 1, DC), "new_ret_sample": (1, NS, H, HD, HD),
}


def kernel(**inputs):
    import concourse.bacc as bacc
    from concourse.bass_utils import run_bass_kernel_spmd

    nc = bacc.Bacc("TRN2", target_bir_lowering=False, num_devices=1)
    arrays = {name: np.ascontiguousarray(a) for name, a in inputs.items()}
    arrays |= {name: np.ascontiguousarray(a.astype(np.float32)) for name, a in constants().items()}
    t = {name: nc.dram_tensor("in_" + name, a.shape, F32, kind="ExternalInput").ap() for name, a in arrays.items()}
    out = {name: nc.dram_tensor("out_" + name, shape, F32, kind="ExternalOutput").ap() for name, shape in OUTS.items()}
    build(nc, t, out)
    r = run_bass_kernel_spmd(nc, [{"in_" + name: a for name, a in arrays.items()}], core_ids=[0])
    return tuple(r.results[0]["out_" + name] for name in OUTS)
```
